# Optimizing a Trainium2 kernel written in Bass

```python
import jax, jax.numpy as jnp
from jax import lax
import numpy as np
import math

D_MODEL = 1024
BATCH = 1
SEQ = 256
DEPTH = 2

CTX_LEN = 256
GRID_W = 64
N_MIXERS = 2
N_HEADS = 16
N_KV_HEADS = 4
HEAD_DIM = D_MODEL // N_HEADS
KV_GROUP = N_HEADS // N_KV_HEADS
ROPE_PAIRS_PER_AXIS = HEAD_DIM // 4
ROPE_THETA = 10000.0
Q_BLOCK = 128
CONV_WIDTH = 31
CONV_PAD = CONV_WIDTH // 2
D_FF = (((8 * D_MODEL + 2) // 3 + 255) // 256) * 256
N_CONV_LAYERS = (DEPTH + N_MIXERS - 1) // N_MIXERS
N_ATTN_LAYERS = DEPTH // N_MIXERS
N_MOD = 6
EPS = 1e-6


def rmsnorm(x, g):
    xf = x.astype(jnp.float32)
    y = xf * lax.rsqrt(jnp.mean(xf * xf, axis=-1, keepdims=True) + EPS)
    return (y * g.astype(jnp.float32)).astype(x.dtype)

def layernorm(x, g, b):
    xf = x.astype(jnp.float32)
    mu = jnp.mean(xf, axis=-1, keepdims=True)
    var = jnp.mean(jnp.square(xf - mu), axis=-1, keepdims=True)
    y = (xf - mu) * lax.rsqrt(var + EPS)
    return (y * g.astype(jnp.float32) + b.astype(jnp.float32)).astype(x.dtype)

def axial_rope_tables(row, col):
    freqs = ROPE_THETA ** (-jnp.arange(ROPE_PAIRS_PER_AXIS, dtype=jnp.float32) / ROPE_PAIRS_PER_AXIS)
    ang = jnp.concatenate([row.astype(jnp.float32)[:, None] * freqs[None, :],
                           col.astype(jnp.float32)[:, None] * freqs[None, :]], axis=-1)
    return jnp.cos(ang), jnp.sin(ang)

def apply_rope(x, cos, sin):
    B, S, H, Dh = x.shape
    xr = x.astype(jnp.float32).reshape(B, S, H, Dh // 2, 2)
    x0, x1 = xr[..., 0], xr[..., 1]
    c = cos[None, :, None, :]
    s = sin[None, :, None, :]
    out = jnp.stack([x0 * c - x1 * s, x0 * s + x1 * c], axis=-1)
    return out.reshape(B, S, H, Dh).astype(x.dtype)

def conv_module(h, w_pw1, b_pw1, w_dw, b_dw, ln_g, ln_b, w_pw2, b_pw2):
    u = h @ w_pw1 + b_pw1
    a, gt = jnp.split(u, 2, axis=-1)
    u = a * jax.nn.sigmoid(gt)
    u = lax.conv_general_dilated(
        u, w_dw[:, None, :].astype(u.dtype), window_strides=(1,),
        padding=[(CONV_PAD, CONV_PAD)], dimension_numbers=("NWC", "WIO", "NWC"),
        feature_group_count=u.shape[-1]) + b_dw
    u = jax.nn.silu(layernorm(u, ln_g, ln_b))
    return u @ w_pw2 + b_pw2

def gqa_sdpa(q, k, v):
    B, Q, H, Dh = q.shape
    qg = q.reshape(B, Q, N_KV_HEADS, KV_GROUP, Dh)
    s = jnp.einsum("bqkgd,bskd->bkgqs", qg, k).astype(jnp.float32) * (Dh ** -0.5)
    p = jax.nn.softmax(s, axis=-1).astype(v.dtype)
    o = jnp.einsum("bkgqs,bskd->bqkgd", p, v)
    return o.reshape(B, Q, H * Dh)

def attention_module(hx, hc, wq, wk, wv, wo, q_g, k_g, cos, sin, need_ctx):
    B, S, _ = hx.shape
    L = hc.shape[1]
    qx = apply_rope(rmsnorm((hx @ wq).reshape(B, S, N_HEADS, HEAD_DIM), q_g), cos, sin)
    kx = apply_rope(rmsnorm((hx @ wk).reshape(B, S, N_KV_HEADS, HEAD_DIM), k_g), cos, sin)
    vx = (hx @ wv).reshape(B, S, N_KV_HEADS, HEAD_DIM)
    kc = rmsnorm((hc @ wk).reshape(B, L, N_KV_HEADS, HEAD_DIM), k_g)
    vc = (hc @ wv).reshape(B, L, N_KV_HEADS, HEAD_DIM)
    k_all = jnp.concatenate([kx, kc], axis=1)
    v_all = jnp.concatenate([vx, vc], axis=1)
    n_blk = S // Q_BLOCK
    qb = qx.reshape(B, n_blk, Q_BLOCK, N_HEADS, HEAD_DIM).transpose(1, 0, 2, 3, 4)
    ob = lax.map(lambda q: gqa_sdpa(q, k_all, v_all), qb)
    yx = ob.transpose(1, 0, 2, 3).reshape(B, S, N_HEADS * HEAD_DIM) @ wo
    yc = None
    if need_ctx:
        qc = rmsnorm((hc @ wq).reshape(B, L, N_HEADS, HEAD_DIM), q_g)
        yc = gqa_sdpa(qc, kc, vc) @ wo
    return yx, yc

def swiglu(h, w1, w3, w2):
    return (jax.nn.silu(h @ w1) * (h @ w3)) @ w2

def first_inputs(seed: int = 0) -> dict:
    key = jax.random.key(seed)
    ks = jax.random.split(key, 32)
    D = D_MODEL

    def nrm(k, shape, scale):
        return jax.random.normal(k, shape, jnp.float32) * scale

    NC, NA = N_CONV_LAYERS, N_ATTN_LAYERS
    return {
        "x": nrm(ks[0], (BATCH, SEQ, D), 1.0),
        "c": nrm(ks[1], (BATCH, D), 1.0),
        "ctx": nrm(ks[2], (BATCH, CTX_LEN, D), 1.0),
        "c_ctx": nrm(ks[3], (D,), 1.0),
        "w_mod": nrm(ks[4], (DEPTH, D, N_MOD * D), 0.5 * D ** -0.5),
        "b_mod": nrm(ks[5], (DEPTH, N_MOD * D), 0.01),
        "norm_g": 1.0 + nrm(ks[6], (DEPTH, 4, D), 0.05),
        "conv_w_pw1": nrm(ks[7], (NC, D, 2 * D), D ** -0.5),
        "conv_b_pw1": nrm(ks[8], (NC, 2 * D), 0.01),
        "conv_w_dw": nrm(ks[9], (NC, CONV_WIDTH, D), CONV_WIDTH ** -0.5),
        "conv_b_dw": nrm(ks[10], (NC, D), 0.01),
        "conv_ln_g": 1.0 + nrm(ks[11], (NC, D), 0.05),
        "conv_ln_b": nrm(ks[12], (NC, D), 0.01),
        "conv_w_pw2": nrm(ks[13], (NC, D, D), D ** -0.5),
        "conv_b_pw2": nrm(ks[14], (NC, D), 0.01),
        "attn_wq": nrm(ks[15], (NA, D, N_HEADS * HEAD_DIM), D ** -0.5),
        "attn_wk": nrm(ks[16], (NA, D, N_KV_HEADS * HEAD_DIM), D ** -0.5),
        "attn_wv": nrm(ks[17], (NA, D, N_KV_HEADS * HEAD_DIM), D ** -0.5),
        "attn_wo": nrm(ks[18], (NA, N_HEADS * HEAD_DIM, D), (N_HEADS * HEAD_DIM) ** -0.5),
        "attn_q_g": 1.0 + nrm(ks[19], (NA, HEAD_DIM), 0.05),
        "attn_k_g": 1.0 + nrm(ks[20], (NA, HEAD_DIM), 0.05),
        "ffn_w1": nrm(ks[21], (DEPTH, D, D_FF), D ** -0.5),
        "ffn_w3": nrm(ks[22], (DEPTH, D, D_FF), D ** -0.5),
        "ffn_w2": nrm(ks[23], (DEPTH, D_FF, D), D_FF ** -0.5),
    }

def first_block(x, c, ctx, c_ctx, w_mod, b_mod, norm_g,
              conv_w_pw1, conv_b_pw1, conv_w_dw, conv_b_dw, conv_ln_g, conv_ln_b, conv_w_pw2, conv_b_pw2,
              attn_wq, attn_wk, attn_wv, attn_wo, attn_q_g, attn_k_g,
              ffn_w1, ffn_w3, ffn_w2):
    B, S, D = x.shape
    rows = S // GRID_W
    row = jnp.repeat(jnp.arange(rows), GRID_W)
    col = jnp.tile(jnp.arange(GRID_W), rows)
    cos, sin = axial_rope_tables(row, col)
    silu_c = jax.nn.silu(c)
    silu_cc = jax.nn.silu(c_ctx)

    for i in range(DEPTH):
        need_ctx = i < DEPTH - 1
        mod_x = (silu_c @ w_mod[i] + b_mod[i])[:, None, :]
        mod_c = silu_cc @ w_mod[i] + b_mod[i]
        sh_x, sc_x, g_x, shf_x, scf_x, gf_x = jnp.split(mod_x, N_MOD, axis=-1)
        sh_c, sc_c, g_c, shf_c, scf_c, gf_c = jnp.split(mod_c, N_MOD, axis=-1)

        hx = rmsnorm(x, norm_g[i, 0]) * (1.0 + sc_x) + sh_x
        hc = rmsnorm(ctx, norm_g[i, 0]) * (1.0 + sc_c) + sh_c
        if i % N_MIXERS == 0:
            j = i // N_MIXERS
            cp = (conv_w_pw1[j], conv_b_pw1[j], conv_w_dw[j], conv_b_dw[j],
                  conv_ln_g[j], conv_ln_b[j], conv_w_pw2[j], conv_b_pw2[j])
            yx = conv_module(hx, *cp)
            yc = conv_module(hc, *cp) if need_ctx else None
        else:
            j = i // N_MIXERS
            yx, yc = attention_module(hx, hc, attn_wq[j], attn_wk[j], attn_wv[j], attn_wo[j],
                                      attn_q_g[j], attn_k_g[j], cos, sin, need_ctx)
        x = x + g_x * rmsnorm(yx, norm_g[i, 1])
        if need_ctx:
            ctx = ctx + g_c * rmsnorm(yc, norm_g[i, 1])

        fx = rmsnorm(x, norm_g[i, 2]) * (1.0 + scf_x) + shf_x
        x = x + gf_x * rmsnorm(swiglu(fx, ffn_w1[i], ffn_w3[i], ffn_w2[i]), norm_g[i, 3])
        if need_ctx:
            fc = rmsnorm(ctx, norm_g[i, 2]) * (1.0 + scf_c) + shf_c
            ctx = ctx + gf_c * rmsnorm(swiglu(fc, ffn_w1[i], ffn_w3[i], ffn_w2[i]), norm_g[i, 3])
    return x


HEAD_DIM_2 = 64
ROPE_DIMS = HEAD_DIM_2 // 4
ROPE_THETA_2 = 500000.0
CONV_W = 3
CONV_WIDTH_2 = 512
DIFF_HEADS = 4
DIFF_V_DIM = 2 * HEAD_DIM_2
NSA_HEADS = 8
NSA_GROUPS = 2
NSA_HPG = NSA_HEADS // NSA_GROUPS
CMP_BLOCK = 32
CMP_STRIDE = 16
SEL_BLOCK = 64
SEL_TOPK = 16
N_LOCAL_SEL = 2
WINDOW = 512
PHI_HIDDEN = 128
BRANCH_WIDTH = 512
N_BRANCHES = 3
D_FF_2 = 2816
ALPHA = (2 * DEPTH) ** 0.25
BETA = (8 * DEPTH) ** -0.25
LN_EPS = 1e-5
NEG = -1e30
BIG = 1e30

COL_SIZES = (CONV_WIDTH_2, CONV_WIDTH_2, CONV_WIDTH_2,
             DIFF_HEADS * 2 * HEAD_DIM_2, DIFF_HEADS * 2 * HEAD_DIM_2, DIFF_HEADS * DIFF_V_DIM,
             NSA_HEADS * HEAD_DIM_2, 6 * NSA_GROUPS * HEAD_DIM_2, N_BRANCHES * NSA_HEADS,
             N_BRANCHES * D_MODEL)
D_IN = sum(COL_SIZES)
SPLIT_POINTS = tuple(int(c) for c in np.cumsum(COL_SIZES)[:-1])


def rope_tables(seq):
    pos = jnp.arange(seq, dtype=jnp.float32)
    inv_freq = ROPE_THETA_2 ** (-jnp.arange(0, ROPE_DIMS, 2, dtype=jnp.float32) / ROPE_DIMS)
    ang = pos[:, None] * inv_freq[None, :]
    return jnp.cos(ang), jnp.sin(ang)

def partial_rope(t, cos, sin):
    half = ROPE_DIMS // 2
    c = cos[None, :, None, :].astype(t.dtype)
    s = sin[None, :, None, :].astype(t.dtype)
    t1, t2, rest = t[..., :half], t[..., half:ROPE_DIMS], t[..., ROPE_DIMS:]
    return jnp.concatenate([t1 * c - t2 * s, t1 * s + t2 * c, rest], axis=-1)

def causal_dwconv(x, w):
    c = x.shape[-1]
    return lax.conv_general_dilated(
        x, w[:, None, :].astype(x.dtype), window_strides=(1,),
        padding=[(w.shape[0] - 1, 0)], dimension_numbers=('NWC', 'WIO', 'NWC'),
        feature_group_count=c)

def layer_norm(x, g, b):
    xf = x.astype(jnp.float32)
    mu = jnp.mean(xf, axis=-1, keepdims=True)
    var = jnp.mean(jnp.square(xf - mu), axis=-1, keepdims=True)
    return ((xf - mu) * lax.rsqrt(var + LN_EPS) * g.astype(jnp.float32) + b.astype(jnp.float32)).astype(x.dtype)

def rms_norm(x, g):
    xf = x.astype(jnp.float32)
    ms = jnp.mean(jnp.square(xf), axis=-1, keepdims=True)
    return (xf * lax.rsqrt(ms + LN_EPS) * g.astype(jnp.float32)).astype(x.dtype)

def diff_attention(q, k, v, lam, lam_init, subln_g):
    b, s = q.shape[0], q.shape[1]
    nb = s // Q_BLOCK
    scale = HEAD_DIM_2 ** -0.5
    qb = q.reshape(b, nb, Q_BLOCK, DIFF_HEADS, 2, HEAD_DIM_2).transpose(1, 0, 2, 3, 4, 5)
    kpos = jnp.arange(s)

    def one_block(args):
        i, q_i = args
        qpos = i * Q_BLOCK + jnp.arange(Q_BLOCK)
        sc = jnp.einsum('bqhmd,bkhmd->bhmqk', q_i, k).astype(jnp.float32) * scale
        sc = jnp.where(kpos[None, :] <= qpos[:, None], sc, -jnp.inf)
        p = jax.nn.softmax(sc, axis=-1)
        a = p[:, :, 0] - lam * p[:, :, 1]
        return jnp.einsum('bhqk,bkhd->bqhd', a.astype(v.dtype), v)

    o = lax.map(one_block, (jnp.arange(nb), qb))
    o = o.transpose(1, 0, 2, 3, 4).reshape(b, s, DIFF_HEADS, DIFF_V_DIM)
    o = rms_norm(o, subln_g) * (1.0 - lam_init)
    return o.reshape(b, s, DIFF_HEADS * DIFF_V_DIM)

def compress_kv(kv, pos_emb, w1, w2):
    b, s = kv.shape[0], kv.shape[1]
    n_cmp = (s - CMP_BLOCK) // CMP_STRIDE + 1
    idx = jnp.arange(n_cmp)[:, None] * CMP_STRIDE + jnp.arange(CMP_BLOCK)[None, :]
    blocks = kv[:, idx] + pos_emb[None, None, :, None, :]
    flat = blocks.transpose(0, 1, 3, 2, 4).reshape(b, n_cmp, NSA_GROUPS, CMP_BLOCK * HEAD_DIM_2)
    return jax.nn.gelu(flat @ w1, approximate=False) @ w2

def nsa_attention(q, kc, vc, ks, vs, kw, vw, gate_logits, cmp_pos, phi_w1, phi_w2):
    b, s = q.shape[0], q.shape[1]
    scale = HEAD_DIM_2 ** -0.5
    qg = q.reshape(b, s, NSA_GROUPS, NSA_HPG, HEAD_DIM_2)
    tpos = jnp.arange(s)

    kc_c = compress_kv(kc, cmp_pos[0], phi_w1[0], phi_w2[0])
    vc_c = compress_kv(vc, cmp_pos[1], phi_w1[1], phi_w2[1])
    n_cmp = kc_c.shape[1]
    cstart = jnp.arange(n_cmp) * CMP_STRIDE
    cvalid = (cstart + CMP_BLOCK - 1)[None, :] <= tpos[:, None]
    sc = jnp.einsum('bsghd,bngd->bghsn', qg, kc_c).astype(jnp.float32) * scale
    p_cmp = jax.nn.softmax(jnp.where(cvalid, sc, NEG), axis=-1) * cvalid
    o_cmp = jnp.einsum('bghsn,bngd->bsghd', p_cmp.astype(vc_c.dtype), vc_c)

    n_sel = s // SEL_BLOCK
    sstart = jnp.arange(n_sel) * SEL_BLOCK
    overlap = jnp.maximum(
        jnp.minimum((cstart + CMP_BLOCK)[:, None], (sstart + SEL_BLOCK)[None, :])
        - jnp.maximum(cstart[:, None], sstart[None, :]), 0).astype(jnp.float32) / CMP_BLOCK
    imp = jnp.einsum('bghsn,nj->bgsj', p_cmp, overlap)
    cur = tpos // SEL_BLOCK
    j = jnp.arange(n_sel)
    forced = (j[None, :] == 0) | ((j[None, :] <= cur[:, None]) & (j[None, :] > cur[:, None] - N_LOCAL_SEL))
    future = j[None, :] > cur[:, None]
    imp = jnp.where(forced, BIG, jnp.where(future, NEG, imp))
    top_k = min(SEL_TOPK, n_sel)
    _, sel_idx = lax.top_k(imp, top_k)

    nb = s // Q_BLOCK
    qb = qg.reshape(b, nb, Q_BLOCK, NSA_GROUPS, NSA_HPG, HEAD_DIM_2).transpose(1, 0, 2, 3, 4, 5)
    idxb = sel_idx.reshape(b, NSA_GROUPS, nb, Q_BLOCK, top_k).transpose(2, 0, 1, 3, 4)
    ks_blk = ks.reshape(b, n_sel, SEL_BLOCK, NSA_GROUPS, HEAD_DIM_2).transpose(0, 3, 1, 2, 4)
    vs_blk = vs.reshape(b, n_sel, SEL_BLOCK, NSA_GROUPS, HEAD_DIM_2).transpose(0, 3, 1, 2, 4)
    gather = jax.vmap(jax.vmap(lambda blocks, ix: blocks[ix]))
    kw_p = jnp.pad(kw, ((0, 0), (WINDOW, 0), (0, 0), (0, 0)))
    vw_p = jnp.pad(vw, ((0, 0), (WINDOW, 0), (0, 0), (0, 0)))
    offs = jnp.arange(SEL_BLOCK)
    n_keys = top_k * SEL_BLOCK

    def one_block(args):
        i, q_i, ix = args
        qpos = i * Q_BLOCK + jnp.arange(Q_BLOCK)
        kg = gather(ks_blk, ix).reshape(b, NSA_GROUPS, Q_BLOCK, n_keys, HEAD_DIM_2)
        vg = gather(vs_blk, ix).reshape(b, NSA_GROUPS, Q_BLOCK, n_keys, HEAD_DIM_2)
        kpos = (ix[..., None] * SEL_BLOCK + offs).reshape(b, NSA_GROUPS, Q_BLOCK, n_keys)
        sc = jnp.einsum('bqghd,bgqnd->bghqn', q_i, kg).astype(jnp.float32) * scale
        sc = jnp.where((kpos <= qpos[None, None, :, None])[:, :, None], sc, -jnp.inf)
        o_sel = jnp.einsum('bghqn,bgqnd->bqghd', jax.nn.softmax(sc, axis=-1).astype(vg.dtype), vg)
        kwin = lax.dynamic_slice_in_dim(kw_p, i * Q_BLOCK, Q_BLOCK + WINDOW, axis=1)
        vwin = lax.dynamic_slice_in_dim(vw_p, i * Q_BLOCK, Q_BLOCK + WINDOW, axis=1)
        wpos = i * Q_BLOCK - WINDOW + jnp.arange(Q_BLOCK + WINDOW)
        wmask = ((wpos[None, :] <= qpos[:, None]) & (wpos[None, :] > qpos[:, None] - WINDOW)
                 & (wpos[None, :] >= 0))
        sc = jnp.einsum('bqghd,bkgd->bghqk', q_i, kwin).astype(jnp.float32) * scale
        sc = jnp.where(wmask, sc, -jnp.inf)
        o_win = jnp.einsum('bghqk,bkgd->bqghd', jax.nn.softmax(sc, axis=-1).astype(vwin.dtype), vwin)
        return o_sel, o_win

    o_sel, o_win = lax.map(one_block, (jnp.arange(nb), qb, idxb))
    o_sel = o_sel.transpose(1, 0, 2, 3, 4, 5).reshape(b, s, NSA_GROUPS, NSA_HPG, HEAD_DIM_2)
    o_win = o_win.transpose(1, 0, 2, 3, 4, 5).reshape(b, s, NSA_GROUPS, NSA_HPG, HEAD_DIM_2)
    g = jax.nn.sigmoid(gate_logits).reshape(b, s, NSA_GROUPS, NSA_HPG, N_BRANCHES)
    o = g[..., 0:1] * o_cmp + g[..., 1:2] * o_sel + g[..., 2:3] * o_win
    return o.reshape(b, s, NSA_HEADS * HEAD_DIM_2)

def token_mixing(x, w_in, conv_a_w, lam_vec, subln_g, cmp_pos, phi_w1, phi_w2, w_branch, w_o,
                 lam_init, cos, sin):
    b, s = x.shape[0], x.shape[1]
    z = x @ w_in
    a_b, a_c, a_v, d_q, d_k, d_v, n_q, n_kv, n_g, m_g = jnp.split(z, SPLIT_POINTS, axis=-1)
    y_a = a_b * causal_dwconv(a_c * a_v, conv_a_w)
    dq = partial_rope(d_q.reshape(b, s, DIFF_HEADS * 2, HEAD_DIM_2), cos, sin).reshape(b, s, DIFF_HEADS, 2, HEAD_DIM_2)
    dk = partial_rope(d_k.reshape(b, s, DIFF_HEADS * 2, HEAD_DIM_2), cos, sin).reshape(b, s, DIFF_HEADS, 2, HEAD_DIM_2)
    dv = d_v.reshape(b, s, DIFF_HEADS, DIFF_V_DIM)
    lf = lam_vec.astype(jnp.float32)
    lam = jnp.exp(jnp.dot(lf[0], lf[1])) - jnp.exp(jnp.dot(lf[2], lf[3])) + lam_init
    y_b = diff_attention(dq, dk, dv, lam, lam_init, subln_g)
    nq = partial_rope(n_q.reshape(b, s, NSA_HEADS, HEAD_DIM_2), cos, sin)
    kv6 = n_kv.reshape(b, s, 6, NSA_GROUPS, HEAD_DIM_2)
    kc = partial_rope(kv6[:, :, 0], cos, sin)
    ks = partial_rope(kv6[:, :, 2], cos, sin)
    kw = partial_rope(kv6[:, :, 4], cos, sin)
    y_c = nsa_attention(nq, kc, kv6[:, :, 1], ks, kv6[:, :, 3], kw, kv6[:, :, 5], n_g,
                        cmp_pos, phi_w1, phi_w2)
    gates = jax.nn.sigmoid(m_g).reshape(b, s, N_BRANCHES, D_MODEL)
    merged = (gates[:, :, 0] * (y_a @ w_branch[0])
              + gates[:, :, 1] * (y_b @ w_branch[1])
              + gates[:, :, 2] * (y_c @ w_branch[2]))
    return merged @ w_o

def conv_ffn(x, w_up, conv_w, conv_b, w_down):
    h = causal_dwconv(x @ w_up, conv_w) + conv_b
    a, u = jnp.split(h, 2, axis=-1)
    return (jax.nn.gelu(a, approximate=False) * u) @ w_down

def second_inputs(seed: int = 0) -> dict:
    key = jax.random.key(seed)
    k = jax.random.split(key, 20)

    def nrm(kk, shape, scale):
        return jax.random.normal(kk, shape, jnp.float32) * scale

    return {
        'x': nrm(k[0], (BATCH, SEQ, D_MODEL), 1.0),
        'w_in': nrm(k[1], (DEPTH, D_MODEL, D_IN), D_MODEL ** -0.5),
        'conv_a_w': nrm(k[2], (DEPTH, CONV_W, CONV_WIDTH_2), CONV_W ** -0.5),
        'diff_lambda': nrm(k[3], (DEPTH, 4, HEAD_DIM_2), 0.1),
        'diff_subln': 1.0 + nrm(k[4], (DEPTH, DIFF_V_DIM), 0.02),
        'nsa_cmp_pos': nrm(k[5], (DEPTH, 2, CMP_BLOCK, HEAD_DIM_2), 0.1),
        'nsa_phi_w1': nrm(k[6], (DEPTH, 2, CMP_BLOCK * HEAD_DIM_2, PHI_HIDDEN), (CMP_BLOCK * HEAD_DIM_2) ** -0.5),
        'nsa_phi_w2': nrm(k[7], (DEPTH, 2, PHI_HIDDEN, HEAD_DIM_2), PHI_HIDDEN ** -0.5),
        'w_branch': nrm(k[8], (DEPTH, N_BRANCHES, BRANCH_WIDTH, D_MODEL), BRANCH_WIDTH ** -0.5),
        'w_o': nrm(k[9], (DEPTH, D_MODEL, D_MODEL), BETA * D_MODEL ** -0.5),
        'ln1_g': 1.0 + nrm(k[10], (DEPTH, D_MODEL), 0.02),
        'ln1_b': nrm(k[11], (DEPTH, D_MODEL), 0.02),
        'ffn_w_up': nrm(k[12], (DEPTH, D_MODEL, 2 * D_FF_2), D_MODEL ** -0.5),
        'ffn_conv_w': nrm(k[13], (DEPTH, CONV_W, 2 * D_FF_2), CONV_W ** -0.5),
        'ffn_conv_b': nrm(k[14], (DEPTH, 2 * D_FF_2), 0.02),
        'ffn_w_down': nrm(k[15], (DEPTH, D_FF_2, D_MODEL), BETA * D_FF_2 ** -0.5),
        'ln2_g': 1.0 + nrm(k[16], (DEPTH, D_MODEL), 0.02),
        'ln2_b': nrm(k[17], (DEPTH, D_MODEL), 0.02),
    }

def second_block(x, w_in, conv_a_w, diff_lambda, diff_subln, nsa_cmp_pos, nsa_phi_w1, nsa_phi_w2,
              w_branch, w_o, ln1_g, ln1_b, ffn_w_up, ffn_conv_w, ffn_conv_b, ffn_w_down,
              ln2_g, ln2_b):
    cos, sin = rope_tables(x.shape[1])
    for l in range(DEPTH):
        lam_init = 0.8 - 0.6 * math.exp(-0.3 * l)
        mix = token_mixing(x, w_in[l], conv_a_w[l], diff_lambda[l], diff_subln[l], nsa_cmp_pos[l],
                           nsa_phi_w1[l], nsa_phi_w2[l], w_branch[l], w_o[l], lam_init, cos, sin)
        x = layer_norm(ALPHA * x + mix, ln1_g[l], ln1_b[l])
        ffn = conv_ffn(x, ffn_w_up[l], ffn_conv_w[l], ffn_conv_b[l], ffn_w_down[l])
        x = layer_norm(ALPHA * x + ffn, ln2_g[l], ln2_b[l])
    return x


def setup_inputs(seed=0):
    out = dict(first_inputs(seed))
    for name, value in second_inputs(seed + 1).items():
        if name != "x":
            out[name + "_2"] = value
    return out


def reference(
    x, c, ctx, c_ctx, w_mod, b_mod, norm_g, conv_w_pw1, conv_b_pw1, conv_w_dw, conv_b_dw,
    conv_ln_g, conv_ln_b, conv_w_pw2, conv_b_pw2, attn_wq, attn_wk, attn_wv, attn_wo, attn_q_g,
    attn_k_g, ffn_w1, ffn_w3, ffn_w2, w_in_2, conv_a_w_2, diff_lambda_2, diff_subln_2,
    nsa_cmp_pos_2, nsa_phi_w1_2, nsa_phi_w2_2, w_branch_2, w_o_2, ln1_g_2, ln1_b_2, ffn_w_up_2,
    ffn_conv_w_2, ffn_conv_b_2, ffn_w_down_2, ln2_g_2, ln2_b_2,
):
    x = first_block(
        x, c, ctx, c_ctx, w_mod, b_mod, norm_g, conv_w_pw1, conv_b_pw1, conv_w_dw, conv_b_dw,
        conv_ln_g, conv_ln_b, conv_w_pw2, conv_b_pw2, attn_wq, attn_wk, attn_wv, attn_wo,
        attn_q_g, attn_k_g, ffn_w1, ffn_w3, ffn_w2,
    )
    return second_block(
        x, w_in_2, conv_a_w_2, diff_lambda_2, diff_subln_2, nsa_cmp_pos_2, nsa_phi_w1_2,
        nsa_phi_w2_2, w_branch_2, w_o_2, ln1_g_2, ln1_b_2, ffn_w_up_2, ffn_conv_w_2,
        ffn_conv_b_2, ffn_w_down_2, ln2_g_2, ln2_b_2,
    )


_drawn_inputs = setup_inputs


def setup_inputs(seed=0):
    import zlib

    import numpy as np

    out = dict(_drawn_inputs(seed))
    spreads = {}
    factors = {'conv_b_pw1': 8.0,
     'conv_b_dw': 7.356,
     'conv_ln_b': 8.0,
     'conv_b_pw2': 6.771,
     'attn_q_g': 8.0,
     'attn_k_g': 8.0,
     'diff_subln_2': 8.0,
     'nsa_cmp_pos_2': 7.119,
     'ffn_conv_b_2': 6.073}
    for name, (base, spread) in spreads.items():
        noise = np.random.default_rng([zlib.crc32(name.encode()), seed]).standard_normal(out[name].shape)
        drawn = base * np.exp(spread * noise) if base else spread * noise
        out[name] = __import__('jax').numpy.asarray(drawn.astype(out[name].dtype))
    for name, factor in factors.items():
        out[name] = (out[name] * factor).astype(out[name].dtype)
    return out
```

```python
import numpy as np
from contextlib import ExitStack

import concourse.bass as bass
from concourse import mybir

F32 = mybir.dt.float32
F32R = mybir.dt.float32r
ACT = mybir.ActivationFunctionType
ALU = mybir.AluOpType
AX = mybir.AxisListType.X

D = 1024
T = 256
FT = 22
CHUNK = 2048
PIECE = 1024
NRAW = 4
NPIECE = 5
NTMP = 9
NCB = 3
ALPHA = 4 ** 0.25
HD = 64
LAM_INIT = [0.8 - 0.6 * float(np.exp(-0.3 * l)) for l in range(2)]
CONVW = 31
PAD = 15
FFN0 = [8, 7, 7]
FFN1 = [11, 11]


def _cols(name, idx, c0, n, width, k0=0, kt=8):
    return [("w", name, idx, (k0 + k) * 128, c0, n, width) for k in range(kt)]


def stream_blocks():
    b = []

    def tiles(name, idx, m, k0=0, kt=8):
        b.extend(_cols(name, idx, m * 128, 128, 128, k0, kt))

    def mod(l, g0, g1):
        for g in range(g0, g1):
            b.extend(_cols("w_mod", (l,), g * 512, 512, 512))

    def ffn(l, parts):
        j0 = 0
        for n in parts:
            for j in range(j0, j0 + n):
                tiles("ffn_w1", (l,), j)
                tiles("ffn_w3", (l,), j)
            for m in range(8):
                tiles("ffn_w2", (l,), m, j0, n)
            j0 += n

    mod(0, 0, 4)
    for j in range(8):
        tiles("conv_w_pw1", (0,), j + 8)
        tiles("conv_w_pw1", (0,), j)
    mod(0, 4, 12)
    mod(1, 0, 12)
    for m in range(8):
        tiles("conv_w_pw2", (0,), m)
    ffn(0, FFN0)
    for m in range(2):
        tiles("attn_wk", (0,), m)
    b.extend(_cols("attn_wv", (0,), 0, 256, 256))
    for m in range(8):
        tiles("attn_wq", (0,), m)
    for m in range(8):
        tiles("attn_wo", (0,), m)
    ffn(1, FFN1)
    for l in range(2):
        for m in range(4):
            tiles("w_in_2", (l,), 16 + m)
            tiles("w_in_2", (l,), 12 + m)
        b.extend(_cols("w_in_2", (l,), 2560, 512, 512))
        for m in (28, 30, 32, 29):
            tiles("w_in_2", (l,), m)
        for k in range(8):
            b.append(("vvg", "w_in_2", (l,), k * 128, 0, 280, 512))
        for m in range(4):
            tiles("w_in_2", (l,), 24 + m)
        b.append(("align",))
        for kv in range(2):
            for k in range(16):
                b.append(("raw", "nsa_phi_w1_2", (l, kv), k * 128, 0, 128, 128))
        for j in range(4):
            for o in (8, 4, 0):
                tiles("w_in_2", (l,), o + j)
        for m in range(16):
            b.extend(_cols("w_in_2", (l,), 4376 + m * 128, 128, 128))
        for m in range(8):
            b.extend(_cols("w_in_2", (l,), 4376 + (16 + m) * 128, 128, 128))
            for br in range(3):
                tiles("w_branch_2", (l, br), m, 0, 4)
        for m in range(8):
            tiles("w_o_2", (l,), m)
        j0 = 0
        for n in FFN1:
            for j in range(j0, j0 + n):
                tiles("ffn_w_up_2", (l,), j)
                tiles("ffn_w_up_2", (l,), 22 + j)
            for m in range(8):
                tiles("ffn_w_down_2", (l,), m, j0, n)
            j0 += n
    return b


def stream_plan():
    out, at = [], 0
    for blk in stream_blocks():
        if blk[0] == "align":
            at += -at % CHUNK
            continue
        width = blk[6]
        assert at % PIECE + width <= PIECE
        out.append((at, blk))
        at += width
    return out, at + (-at % CHUNK)


def vec_plan():
    off, at = {}, 0
    for name, n in (("c", 8), ("c_ctx", 8), ("b_mod", 96), ("norm_g", 64), ("conv_b_pw1", 16), ("conv_w_dw", 248),
                    ("conv_b_dw", 8), ("conv_ln_g", 8), ("conv_ln_b", 8), ("conv_b_pw2", 8), ("attn_q_g", 1),
                    ("attn_k_g", 1), ("conv_a_w_2", 24), ("diff_lambda_2", 8), ("diff_subln_2", 2),
                    ("nsa_cmp_pos_2", 64), ("ln1_g_2", 16), ("ln1_b_2", 16), ("ln2_g_2", 16), ("ln2_b_2", 16),
                    ("ffn_conv_w_2", 264), ("ffn_conv_b_2", 88), ("nsa_phi_w2_2", 512)):
        off[name] = at
        at += n
    return off, at


CONSTS = (("ident", 128), ("ones", 128), ("mean", 128), ("mean128", 128), ("mean64", 128), ("rot1", 128), ("rot2", 128),
          ("dup0", 128), ("dup1", 128), ("cos1", 256), ("sin1", 256), ("cos2", 256), ("sin2", 256), ("causal", 256),
          ("cmpadd", 30), ("cmpok", 30), ("eps6", 1), ("eps5", 1))


def const_plan():
    off, at = {}, 0
    for name, n in CONSTS:
        off[name] = at
        at += n
    return off, at


class Queue:
    def __init__(self, sem):
        self.sem, self.items, self.n = sem, [], 0

    def __call__(self, fn, *after, inc=True):
        self.items.append((flat(after), fn, inc))
        if inc:
            self.n += 1
        return (self.sem, self.n)

    def play(self, eng):
        seen = {}
        for waits, fn, inc in self.items:
            most = {}
            for s, v in waits:
                if v > seen.get(id(s), 0) and v > most.get(id(s), (s, 0))[1]:
                    most[id(s)] = (s, v)
            for key, (s, v) in most.items():
                eng.wait_ge(s, v)
                seen[key] = v
            ins = fn(eng)
            if inc:
                ins.then_inc(self.sem, 1)


def flat(x):
    if x is None:
        return []
    if isinstance(x, tuple) and len(x) == 2 and isinstance(x[1], int):
        return [x]
    return [t for y in x for t in flat(y)]


class Ring:

    def __init__(self, bufs):
        self.bufs, self.rel, self.at = bufs, [[] for _ in bufs], 0

    def get(self):
        i = next(j % len(self.bufs) for j in range(self.at, self.at + len(self.bufs)) if self.rel[j % len(self.bufs)] is not None)
        self.at = i + 1
        w = self.rel[i]
        self.rel[i] = None
        return i, self.bufs[i], w

    def free(self, i, *toks):
        assert self.rel[i] is None
        self.rel[i] = flat(toks)


def build(nc, wstream, vecs_d, const_d, xin, out):
    plan, total = stream_plan()
    voff, nvec = vec_plan()
    coff, ncon = const_plan()
    nchunk = total // CHUNK
    ctx = ExitStack()
    with ctx:
        def sb(name, shape, dt=F32):
            return ctx.enter_context(nc.sbuf_tensor(name, shape, dt))

        def sem(name):
            return ctx.enter_context(nc.semaphore(name))

        raw = sb("raw", [128, NRAW, CHUNK])
        whi = sb("whi", [128, NPIECE, PIECE], F32R)
        wlo = sb("wlo", [128, NPIECE, PIECE], F32R)
        X = sb("X", [128, 2, 8, T])
        Hh = sb("Hh", [128, 4096], F32R)
        Hl = sb("Hl", [128, 4096], F32R)
        Y = sb("Y", [128, 4096])
        VEC = sb("VEC", [128, nvec])
        CON = sb("CON", [128, ncon])
        MOD = sb("MOD", [128, 2, 48, 2])
        MA = sb("MA", [128, 2, 4, 2, 8])
        CS = sb("CS", [128, 8, 4], F32R)
        SM = sb("SM", [128, 256])
        tmpb = sb("tmpb", [128, NTMP, 512])
        cbb = sb("cbb", [128, NCB, 260])
        arena = []

        def arena_open(specs):
            for cm in reversed(arena):
                cm.__exit__(None, None, None)
            arena.clear()
            got = []
            for name, shape, dt in specs:
                cm = nc.sbuf_tensor(name, shape, dt)
                got.append(cm.__enter__())
                arena.append(cm)
            return got

        banks = [ctx.enter_context(nc.psum_tensor(f"pb{i}", [128, 512], F32)) for i in range(8)]

        S, A, V, G, P = (Queue(sem(n)) for n in ("s_sync", "s_act", "s_dve", "s_pool", "s_pe"))
        s_raw = [sem(f"s_raw{i}") for i in range(NRAW)]
        s_con = sem("s_con")
        s_x = sem("s_x")
        s_out = sem("s_out")

        tmp = Ring([tmpb[:, i, :] for i in range(NTMP)])
        cbr = Ring([cbb[:, i, :] for i in range(NCB)])
        pm = Ring([b[:, :] for b in banks[0:4]])
        pt = Ring([b[:, :] for b in banks[4:6]])
        pst = Ring([b[:, :] for b in banks[6:8]])

        def con(name, a=0, b=None, p0=0, p1=128):
            n = dict(CONSTS)[name]
            return CON[p0:p1, coff[name] + a:coff[name] + (n if b is None else b)]

        def vec(name, i=0, n=1):
            return VEC[:, voff[name] + i:voff[name] + i + n]

        def act(out_, in_, func, *after, bias=None, scale=None, accum=None):
            kw = {}
            if bias is not None:
                kw["bias"] = bias
            if scale is not None:
                kw["scale"] = scale
            if accum is not None:
                kw["accum_out"] = accum
            return A(lambda e: e.activation(out_, in_, func, **kw), *after)

        def tt(out_, a, b, op, *after, q=None):
            return (q or V)(lambda e: e.tensor_tensor(out_, a, b, op), *after)

        def stt(out_, a, s, b, op0, op1, *after):
            return V(lambda e: e.scalar_tensor_tensor(out=out_, in0=a, scalar=s, in1=b, op0=op0, op1=op1), *after)

        def ts(out_, a, s1, s2, op0, op1, *after):
            if op1 is None:
                return V(lambda e: e.tensor_scalar(out_, a, s1, None, op0), *after)
            return V(lambda e: e.tensor_scalar(out_, a, s1, s2, op0, op1), *after)

        def vcopy(out_, a, *after):
            return V(lambda e: e.tensor_copy(out_, a), *after)

        def recip(out_, a, *after):
            return V(lambda e: e.reciprocal(out_, a), *after)

        def mm(out_, lhsT, rhs, start, stop, *after, inc=False):
            return P(lambda e: e.matmul(out_, lhsT, rhs, start=start, stop=stop), *after, inc=inc)

        def tr(out_, in_, idn, *after, inc=False):
            return P(lambda e: e.transpose(out_, in_, idn), *after, inc=inc)

        def f32(ap):
            return ap.bitcast(F32)

        def load(dst, src, s):
            S.items.append(([], lambda e: e.dma_start(dst, src).then_inc(s, 16), False))

        load(VEC[:, :], vecs_d, s_con)
        load(CON[:, :], const_d, s_con)
        in_tok = (s_con, 32)
        x_tok = (s_x, 32)

        st = {"blk": 0, "made": 0, "dma": 0}
        raw_rel = {}
        piece_rel = {}
        piece_tok = {}
        raw_kind = {at // CHUNK for at, blk in plan if blk[0] == "raw"}
        lo_queue = {"f": lambda p: V}

        def chunk_tok(c):
            return (s_raw[c % NRAW], 16 * (c // NRAW + 1))

        def dma_chunks(upto):
            while st["dma"] < min(upto, nchunk):
                c = st["dma"]
                if c >= NRAW and raw_rel.get(c - NRAW) is None:
                    return
                after = raw_rel[c - NRAW] if c >= NRAW else []
                s = s_raw[c % NRAW]
                S.items.append((flat(after), lambda e, c=c, s=s: e.dma_start(
                    raw[:, c % NRAW, :], wstream[c]).then_inc(s, 16), False))
                st["dma"] += 1
                if c == 1:
                    for seg in range(2):
                        load(X[:, seg, :, :], xin[seg], s_x)

        def make_pieces(upto):
            while st["made"] < min(upto, total // PIECE):
                p = st["made"]
                c = p // 2
                dma_chunks(c + NRAW)
                if c in raw_kind:
                    st["made"] += 1
                    continue
                if p >= NPIECE and piece_rel.get(p - NPIECE) is None:
                    if (p - NPIECE) // 2 not in raw_kind:
                        return
                    free = []
                else:
                    free = piece_rel[p - NPIECE] if p >= NPIECE else []
                last = p - NPIECE
                while last >= 0 and last // 2 in raw_kind:
                    last -= NPIECE
                if last != p - NPIECE and last >= 0:
                    free = piece_rel[last]
                src = raw[:, c % NRAW, (p % 2) * PIECE:(p % 2 + 1) * PIECE]
                hi, lo = whi[:, p % NPIECE, :], wlo[:, p % NPIECE, :]
                a = act(hi, src, ACT.Copy, chunk_tok(c), free)
                q = lo_queue["f"](p)
                b = tt(lo, src, f32(hi), ALU.subtract, a, free, q=q)
                piece_tok[p] = [a, b]
                if p % 2 == 1:
                    raw_rel[c] = [a, b, piece_tok[p - 1]]
                    dma_chunks(c + NRAW + 1)
                st["made"] += 1

        def take(kind, width):
            at, blk = plan[st["blk"]]
            st["blk"] += 1
            assert blk[0] == kind and blk[6] == width, (blk, kind, width)
            p = at // PIECE
            o = at % PIECE
            make_pieces(p + NPIECE)
            end = o + width == PIECE
            nxt = plan[st["blk"]][0] if st["blk"] < len(plan) else total
            if nxt // PIECE != p:
                end = True
            return (whi[:, p % NPIECE, o:o + width], wlo[:, p % NPIECE, o:o + width], piece_tok[p], p, end)

        def take_raw(n):
            at, blk = plan[st["blk"]]
            assert blk[0] == "raw" and at % CHUNK == 0
            st["blk"] += n
            c = at // CHUNK
            dma_chunks(c + 1)
            assert st["dma"] > c
            return raw[:, c % NRAW, :], chunk_tok(c), c

        def done(p, tok):
            piece_rel[p] = [tok]

        def lin(kt, xh, xl, n, xtok):
            i, bank, w = pm.get()
            tok = None
            for k in range(kt):
                hi, lo, pk, p, end = take("w", 128)
                o = bank[:, 0:n]
                mm(o, hi, xh(k), k == 0, False, pk, w, xtok(k))
                mm(o, hi, xl(k), False, False)
                tok = mm(o, lo, xh(k), False, k == kt - 1, inc=end or k == kt - 1)
                if end:
                    done(p, tok)
            return i, bank[:, 0:n], tok

        def lin_tok(kind, width, n, xh, xl, tiles, xtok):
            got = [pm.get() for _ in range(tiles)]
            for k in range(8):
                hi, lo, pk, p, end = take(kind, width)
                for s, (i, bank, w) in enumerate(got):
                    o = bank[:, 0:n]
                    xa, xb = xh(k)[:, s * 128:(s + 1) * 128], xl(k)[:, s * 128:(s + 1) * 128]
                    mm(o, xa, hi[:, 0:n], k == 0, False, pk, w, xtok(k))
                    mm(o, xb, hi[:, 0:n], False, False)
                    tok = mm(o, xa, lo[:, 0:n], False, k == 7, inc=k == 7 or (end and s == tiles - 1))
                if end:
                    done(p, tok)
            return [(i, bank[:, 0:n]) for i, bank, w in got], tok

        def split(hi, lo, src, *after):
            a = act(hi, src, ACT.Copy, *after)
            b = tt(lo, src, f32(hi), ALU.subtract, a, *after)
            return [a, b]

        def rstd(bank, n, tok, eps):
            ia, ta, wa = tmp.get()
            ir, r, wr = tmp.get()
            t0 = act(ta[:, 0:n], bank[:, 0:n], ACT.Sqrt, tok, wa, in_tok, bias=con(eps))
            t1 = recip(r[:, 0:n], ta[:, 0:n], t0, wr)
            tmp.free(ia, t1)
            return ir, r[:, 0:n], t1, t0

        class Stat:

            def __init__(self, n, mat="mean", kt=8):
                self.n, self.mat, self.kt, self.k = n, mat, kt, 0
                self.i, self.bank, self.w = pst.get()
                self.bank = self.bank[:, 0:n]

            def add(self, tile, tok):
                k = self.k
                self.k += 1
                return mm(self.bank, con(self.mat), tile, k == 0, k == self.kt - 1, tok, self.w, in_tok, inc=True)

            def square(self, src, tok, bias=None):
                i, t, w = tmp.get()
                a = act(t[:, 0:self.n], src, ACT.Square, tok, w, bias=bias) if bias is not None else \
                    act(t[:, 0:self.n], src, ACT.Square, tok, w)
                self.tok = self.add(t[:, 0:self.n], a)
                tmp.free(i, self.tok)
                return a

        sil = SM[:, 0:16]
        t_sil = act(sil, vec("c", 0, 16), ACT.Silu, in_tok)
        csv = sil.rearrange("p (s k) -> p k s", s=2)
        t_cs = act(CS[:, :, 0:2], csv, ACT.Copy, t_sil)
        t_cs2 = tt(CS[:, :, 2:4], csv, f32(CS[:, :, 0:2]), ALU.subtract, t_cs)
        mod_tok = {}
        mrow = {}

        def mod_group(l, g):
            i, bank, w = pm.get()
            for k in range(8):
                hi, lo, pk, p, end = take("w", 512)
                mm(bank[0:4, :], CS[:, k, :], hi, k == 0, False, pk, w, t_cs, t_cs2)
                tok = mm(bank[0:4, :], CS[:, k, :], lo, False, k == 7, inc=end)
                if end:
                    done(p, tok)
            it, t, wt = tmp.get()
            a = act(t[0:4, :], bank[0:4, :], ACT.Copy, tok, wt)
            pm.free(i, a)
            ip, pb, wp = pt.get()
            for j in range(4):
                tk = tr(pb[:, 4 * j:4 * j + 4], t[0:4, j * 128:(j + 1) * 128], con("ident", 0, 4, 0, 4), a, wp, in_tok,
                        inc=j == 3)
            tmp.free(it, tk)
            pv = pb[:, 0:16].rearrange("p (j s) -> p j s", j=4)
            dst = MOD[:, l, 4 * g:4 * g + 4, :]
            bm = vec("b_mod", l * 48 + 4 * g, 4).rearrange("p (j o) -> p j o", o=1).broadcast_to((128, 4, 2))
            v1 = tt(dst, pv[:, :, 0:2], bm, ALU.add, tk)
            v2 = tt(dst, pv[:, :, 2:4], dst, ALU.add, v1)
            pt.free(ip, v2)
            mod_tok[l, g] = v2

        def mvec(l, which, s, k):
            return MOD[:, l, which * 8 + k, s:s + 1]

        def mod_scale(l, slot, which, gi, plus):
            toks = []
            for s in range(2):
                toks.append(stt(MA[:, l, slot, s, :], MOD[:, l, which * 8:which * 8 + 8, s], plus,
                                vec("norm_g", (l * 4 + gi) * 8, 8), ALU.add, ALU.mult,
                                [mod_tok[l, 2 * which], mod_tok[l, 2 * which + 1]], in_tok))
            return toks

        def Hx(k, n=512):
            return Hh[:, k * 512:k * 512 + n], Hl[:, k * 512:k * 512 + n]

        xt = [[x_tok] for _ in range(8)]
        hfree = {"t": []}

        def modulated(l, slot, shift, sctoks, segs):
            n = 256 * segs
            stat = Stat(n)
            for k in range(8):
                stat.square(X[:, 0:segs, k, :], xt[k])
            ir, r, t1, t0 = rstd(stat.bank, n, stat.tok, "eps6")
            pst.free(stat.i, t0)
            toks, last = [], []
            sh_t = [mod_tok[l, 2 * shift], mod_tok[l, 2 * shift + 1]]
            for k in range(8):
                i, t, w = tmp.get()
                tk, rd = [], []
                for s in range(segs):
                    sl = slice(s * 256, (s + 1) * 256)
                    a = stt(t[:, sl], X[:, s, k, :], MA[:, l, slot, s, k:k + 1], r[:, sl], ALU.mult, ALU.mult,
                            t1, w, sctoks, xt[k])
                    hi, lo = Hh[:, k * 512 + s * 256:k * 512 + (s + 1) * 256], Hl[:, k * 512 + s * 256:k * 512 + (s + 1) * 256]
                    b = act(hi, t[:, sl], ACT.Identity, a, hfree["t"], sh_t, bias=mvec(l, shift, s, k))
                    c_ = stt(lo, t[:, sl], mvec(l, shift, s, k), f32(hi), ALU.add, ALU.subtract, a, b, hfree["t"])
                    tk += [b, c_]
                    last = [a]
                tmp.free(i, tk)
                toks.append(tk)
            tmp.free(ir, last)
            return toks

        def residual(l, slot, sctoks, stat, ytoks, segs):
            n = 256 * segs
            ir, r, t1, t0 = rstd(stat.bank, n, stat.tok, "eps6")
            pst.free(stat.i, t0)
            for k in range(8):
                i, t, w = tmp.get()
                last = []
                for s in range(segs):
                    sl = slice(s * 256, (s + 1) * 256)
                    a = stt(t[:, sl], Y[:, k * 512 + s * 256:k * 512 + (s + 1) * 256], MA[:, l, slot, s, k:k + 1], r[:, sl],
                            ALU.mult, ALU.mult, t1, w, sctoks, ytoks[k])
                    last.append(tt(X[:, s, k, :], X[:, s, k, :], t[:, sl], ALU.add, a, xt[k]))
                tmp.free(i, last)
                xt[k] = last
            tmp.free(ir, last)

        yfree = {"t": []}

        def swiglu(l, parts, htoks, segs):
            n = 256 * segs
            cap = 4096 // n
            HIh, HIl = arena_open([(f"hid_h{l}", [128, 4096], F32R), (f"hid_l{l}", [128, 4096], F32R)])
            hidfree = list(arena_free["t"])
            ytoks = [None] * 8
            stat = None
            for pi, cnt in enumerate(parts):
                assert cnt <= cap
                gt = []
                for j in range(cnt):
                    i1, b1, t1 = lin(8, lambda k: Hx(k, n)[0], lambda k: Hx(k, n)[1], n, lambda k: htoks[k])
                    i3, b3, t3 = lin(8, lambda k: Hx(k, n)[0], lambda k: Hx(k, n)[1], n, lambda k: htoks[k])
                    it, s1, w = tmp.get()
                    a = act(s1[:, 0:n], b1, ACT.Silu, t1, w)
                    pm.free(i1, a)
                    b = tt(s1[:, 0:n], b3, s1[:, 0:n], ALU.mult, a, t3)
                    pm.free(i3, b)
                    tk = split(HIh[:, j * n:(j + 1) * n], HIl[:, j * n:(j + 1) * n], s1[:, 0:n], b, hidfree)
                    tmp.free(it, tk)
                    gt.append(tk)
                hfree["t"] = [t3]
                final = pi == len(parts) - 1
                if final:
                    stat = Stat(n)
                for m in range(8):
                    i, bk, t = lin(cnt, lambda k: HIh[:, k * n:(k + 1) * n], lambda k: HIl[:, k * n:(k + 1) * n], n,
                                   lambda k: gt[k])
                    y = Y[:, m * 512:m * 512 + n]
                    if pi == 0:
                        ytoks[m] = act(y, bk, ACT.Copy, t, yfree["t"])
                        rd = ytoks[m]
                    else:
                        rd = ytoks[m] = tt(y, bk, y, ALU.add, t, ytoks[m])
                    pm.free(i, rd)
                    if final:
                        stat.square(y, ytoks[m])
                hidfree = [t]
            arena_free["t"] = [t]
            return stat, ytoks

        arena_free = {"t": []}

        dma_chunks(NRAW)
        for g in range(4):
            mod_group(0, g)
        sc = mod_scale(0, 0, 1, 0, 1.0)
        htoks = modulated(0, 0, 0, sc, 2)

        U, = arena_open([("U", [128, 8, 2, 286], F32)])
        t_pad = [G(lambda e: e.memset(U[:, :, :, 0:PAD], 0.0)), G(lambda e: e.memset(U[:, :, :, PAD + T:], 0.0)),
                 G(lambda e: e.memset(cbb[:, :, :], 0.0))]
        cb_zero = t_pad[2]
        lo_queue["f"] = lambda p: G if p % 2 else V
        utoks = []
        for j in range(8):
            ig, bg, tg = lin(8, lambda k: Hx(k)[0], lambda k: Hx(k)[1], 512, lambda k: htoks[k])
            ia, ba, ta = lin(8, lambda k: Hx(k)[0], lambda k: Hx(k)[1], 512, lambda k: htoks[k])
            i, t, w = tmp.get()
            a = act(t, bg, ACT.Sigmoid, tg, w, bias=vec("conv_b_pw1", 8 + j))
            pm.free(ig, a)
            b = stt(U[:, j, :, PAD:PAD + T], ba.rearrange("p (s t) -> p s t", s=2), vec("conv_b_pw1", j),
                    t.rearrange("p (s t) -> p s t", s=2), ALU.add, ALU.mult, a, ta, t_pad)
            pm.free(ia, b)
            tmp.free(i, b)
            utoks.append(b)
        hfree["t"] = [ta]

        lo_queue["f"] = lambda p: G if p % 2 else V
        stat = Stat(512)
        vt = []
        todo = [(0, g) for g in range(4, 12)] + [(1, g) for g in range(12)]

        def conv_tile(k):
            y = Y[:, k * 512:(k + 1) * 512].rearrange("p (s t) -> p s t", s=2)
            tk = None
            for i in range(CONVW):
                u = U[:, k, :, i:i + T]
                w = vec("conv_w_dw", i * 8 + k)
                if i == 0:
                    bias = vec("conv_b_dw", k).rearrange("p (a b) -> p a b", a=1).broadcast_to((128, 2, T))
                    tk = stt(y, u, w, bias, ALU.mult, ALU.add, utoks[k], t_pad)
                else:
                    tk = stt(y, u, w, y, ALU.mult, ALU.add, tk)
            return tk

        for k in range(8):
            vt.append(conv_tile(k))
            for _ in range(3 if k < 4 else 2):
                if todo:
                    mod_group(*todo.pop(0))
        while todo:
            mod_group(*todo.pop(0))
        for k in range(8):
            stat.tok = stat.add(Y[:, k * 512:(k + 1) * 512], vt[k])
        lo_queue["f"] = lambda p: V
        arena_free["t"] = list(vt)

        def center(stat, n, toks, stride):
            im, mu, w = tmp.get()
            t0 = act(mu[:, 0:n], stat.bank, ACT.Copy, stat.tok, w)
            pst.free(stat.i, t0)
            s2 = Stat(n)
            out_ = []
            for k in range(8):
                y = Y[:, k * stride:k * stride + n]
                a = tt(y, y, mu[:, 0:n], ALU.subtract, t0, toks[k], stat.tok)
                s2.square(y, a)
                out_.append(a)
            tmp.free(im, out_[-1])
            return s2, out_

        s2, ct = center(stat, 512, vt, 512)
        ir, r, t1, t0 = rstd(s2.bank, 512, s2.tok, "eps6")
        pst.free(s2.i, t0)
        htoks = []
        for k in range(8):
            i, t, w = tmp.get()
            a = tt(t, Y[:, k * 512:(k + 1) * 512], r, ALU.mult, t1, w, ct[k])
            b = act(t, t, ACT.Silu, a, in_tok, bias=vec("conv_ln_b", k), scale=vec("conv_ln_g", k))
            tk = split(Hx(k)[0], Hx(k)[1], t, b, hfree["t"])
            tmp.free(i, tk)
            htoks.append(tk)
        tmp.free(ir, a)
        yread = [a, s2.tok]

        stat = Stat(512)
        ytoks = []
        for m in range(8):
            i, bk, t = lin(8, lambda k: Hx(k)[0], lambda k: Hx(k)[1], 512, lambda k: htoks[k])
            a = act(Y[:, m * 512:(m + 1) * 512], bk, ACT.Identity, t, yread, bias=vec("conv_b_pw2", m))
            pm.free(i, a)
            stat.square(Y[:, m * 512:(m + 1) * 512], a)
            ytoks.append(a)
        hfree["t"] = [t]
        sc = mod_scale(0, 1, 2, 1, 0.0)
        residual(0, 1, sc, stat, ytoks, 2)

        def ffn_first(l, parts, segs):
            yfree["t"] = [xt[k] for k in range(8)]
            sc = mod_scale(l, 2, 4, 2, 1.0)
            ht = modulated(l, 2, 3, sc, segs)
            stat, yt = swiglu(l, parts, ht, segs)
            sc = mod_scale(l, 3, 5, 3, 0.0)
            residual(l, 3, sc, stat, yt, segs)

        ffn_first(0, FFN0, 2)

        sc = mod_scale(1, 0, 1, 0, 1.0)
        htoks = modulated(1, 0, 0, sc, 2)
        afree = list(arena_free["t"])
        Q1, K1, V1 = arena_open([("Q1", [128, 8, T], F32), ("K1", [128, 4, 512], F32), ("V1", [128, 4, 4, 128], F32)])

        def head_norm(src, n, tok, gain):
            s_ = Stat(n, "mean64", 1)
            s_.square(src, tok)
            ir, r, t1, t0 = rstd(s_.bank, n, s_.tok, "eps6")
            pst.free(s_.i, t0)
            a = stt(src, src, gain, r, ALU.mult, ALU.mult, t1)
            tmp.free(ir, a)
            return a

        def rope(dst, src, tok, rot, cs, sn, *after):
            i, b, w = pt.get()
            t0 = mm(b[:, 0:T], con(rot), src, True, True, tok, w, in_tok, inc=True)
            it, t, wt = tmp.get()
            t1 = tt(t[:, 0:T], b[:, 0:T], con(sn), ALU.mult, t0, wt)
            pt.free(i, t1)
            t2 = tt(dst, src, con(cs), ALU.mult, tok, t0, *after)
            t3 = tt(dst, dst, t[:, 0:T], ALU.add, t1, t2)
            tmp.free(it, t3)
            return t3

        ktok = [None] * 4
        for m in range(2):
            i, bk, t = lin(8, lambda k: Hx(k)[0], lambda k: Hx(k)[1], 512, lambda k: htoks[k])
            it, kr, w = tmp.get()
            a = act(kr, bk, ACT.Copy, t, w)
            pm.free(i, a)
            a = head_norm(kr, 512, a, vec("attn_k_g"))
            a = rope(kr[:, 0:T], kr[:, 0:T], a, "rot1", "cos1", "sin1")
            for g in range(2):
                i, b, w = pt.get()
                t0 = mm(b, con(f"dup{g}"), kr, True, True, a, w, inc=True)
                ktok[2 * m + g] = act(K1[:, 2 * m + g, :], b, ACT.Copy, t0, afree)
                pt.free(i, ktok[2 * m + g])
            tmp.free(it, t0)
        got, t = lin_tok("w", 256, 256, lambda k: Hx(k)[0], lambda k: Hx(k)[1], 4, lambda k: htoks[k])
        vtok = []
        for s, (i, bk) in enumerate(got):
            b3 = bk.rearrange("p (g d) -> p g d", g=4)
            a = act(V1[:, s, :, 0:64], b3, ACT.Copy, t, afree)
            b = vcopy(V1[:, s, :, 64:128], b3, t, a, afree)
            pm.free(i, a, b)
            vtok.append([a, b])

        pT1 = Ring([Y[:, 2048 + 1024 * i:3072 + 1024 * i].rearrange("p (s q) -> p s q", s=4) for i in range(2)])
        pT1.rel = [[xt[k] for k in range(8)] for _ in range(2)]
        smr = Ring([SM[:, 16 + 12 * i:28 + 12 * i] for i in range(8)])
        otok = {}
        qtok = [None] * 8

        def q_tile(j):
            i, bk, t = lin(8, lambda k: Hx(k, T)[0], lambda k: Hx(k, T)[1], T, lambda k: htoks[k])
            it, qr, w = tmp.get()
            a = act(qr[:, 0:T], bk, ACT.Copy, t, w)
            pm.free(i, a)
            a = head_norm(qr[:, 0:T], T, a, vec("attn_q_g"))
            qtok[j] = rope(Q1[:, j, :], qr[:, 0:T], a, "rot1", "cos1", "sin1", afree)
            tmp.free(it, qtok[j])
            return t

        SC = HD ** -0.5

        def a1_scores(h, qt):
            i, b, w = pm.get()
            o = (h % 2) * 64
            t0 = mm(b, Q1[o:o + 64, h // 2, qt * 128:(qt + 1) * 128], K1[o:o + 64, h // 4, :], True, True,
                    qtok[h // 2], ktok[h // 4], w, inc=True)
            im, sm, wm = smr.get()
            t1 = V(lambda e: e.reduce_max(sm[:, 0:1], b, AX), t0, wm)
            t2 = ts(sm[:, 1:2], sm[:, 0:1], -SC, None, ALU.mult, None, t1)
            ip, p, wp = tmp.get()
            t3 = act(p, b, ACT.Exp, t2, wp, bias=sm[:, 1:2], scale=SC, accum=sm[:, 2:3])
            pm.free(i, t3)
            t4 = recip(sm[:, 3:4], sm[:, 2:3], t3)
            t5 = ts(p, p, sm[:, 3:4], None, ALU.mult, None, t4)
            smr.free(im, t5)
            return ip, p, t5

        cur = {}

        def a1_turn(h, qt, ip, p, t5):
            if qt == 0:
                cur["pT"] = pT1.get()
                cur["tok"] = []
            it, pT, wT = cur["pT"]
            i, b, w = pt.get()
            for s in range(4):
                t0 = tr(b[:, s * 128:(s + 1) * 128], p[:, s * 128:(s + 1) * 128], con("ident"), t5, w, inc=s == 3)
            tmp.free(ip, t0)
            t1 = act(pT[:, :, qt * 128:(qt + 1) * 128], b.rearrange("p (s q) -> p s q", s=4), ACT.Copy, t0, wT)
            pt.free(i, t1)
            cur["tok"].append(t1)
            if qt == 1:
                o = (h % 2) * 64
                i, b, w = pm.get()
                for s in range(4):
                    t0 = mm(b[:, 0:T], V1[:, s, h // 4, :], pT[:, s, :], s == 0, s == 3, cur["tok"], vtok[s], w, inc=s == 3)
                pT1.free(it, t0)
                a = act(Y[o:o + 64, (h // 2) * T:(h // 2 + 1) * T], b[o:o + 64, 0:T], ACT.Copy, t0, [xt[k] for k in range(8)])
                pm.free(i, a)
                otok.setdefault(h // 2, []).append(a)

        tq = q_tile(0)
        pend = []
        for h in range(16):
            for qt in range(2):
                pend.append((h, qt, *a1_scores(h, qt)))
                if len(pend) > 2:
                    a1_turn(*pend.pop(0))
            if h % 2 == 0 and h // 2 + 1 < 8:
                tq = q_tile(h // 2 + 1)
        while pend:
            a1_turn(*pend.pop(0))
        hfree["t"] = [tq]
        arena_free["t"] = [otok[7], (P.sem, P.n)]
        otk = []
        for j in range(8):
            otk.append(split(Hx(j, T)[0], Hx(j, T)[1], Y[:, j * T:(j + 1) * T], otok[j], hfree["t"]))
        stat = Stat(T)
        ytoks = []
        for m in range(8):
            i, bk, t = lin(8, lambda k: Hx(k, T)[0], lambda k: Hx(k, T)[1], T, lambda k: otk[k])
            a = act(Y[:, m * 512:m * 512 + T], bk, ACT.Copy, t, otk, otok[7], (P.sem, P.n))
            pm.free(i, a)
            stat.square(Y[:, m * 512:m * 512 + T], a)
            ytoks.append(a)
        hfree["t"] = [t]
        sc = mod_scale(1, 1, 2, 1, 0.0)
        residual(1, 1, sc, stat, ytoks, 1)
        ffn_first(1, FFN1, 1)

        def xh(k):
            return Hh[:, k * T:(k + 1) * T]

        def xl(k):
            return Hl[:, k * T:(k + 1) * T]

        xtoks = []
        for k in range(8):
            xtoks.append(split(xh(k), xl(k), X[:, 0, k, :], xt[k], hfree["t"]))
        GT = [X[:, 1, k, :] for k in range(8)] + [Y[:, 2048 + k * T:2048 + (k + 1) * T] for k in range(8)]
        xt = [[xt[k]] for k in range(8)]
        y2free = [xt[k] for k in range(8)]

        def layer_norm(toks, stat, gname, bname, l, hwait):
            s2, ct = center(stat, T, toks, T)
            ir, r, t1, t0 = rstd(s2.bank, T, s2.tok, "eps5")
            pst.free(s2.i, t0)
            ht = []
            for k in range(8):
                i, t, w = tmp.get()
                g, b = vec(gname, l * 8 + k), vec(bname, l * 8 + k)
                a = stt(t[:, 0:T], Y[:, k * T:(k + 1) * T], g, r, ALU.mult, ALU.mult, t1, w, ct[k])
                c1 = act(xh(k), t[:, 0:T], ACT.Identity, a, hwait, bias=b)
                c2 = stt(xl(k), t[:, 0:T], b, f32(xh(k)), ALU.add, ALU.subtract, a, c1, hwait)
                c3 = act(X[:, 0, k, :], t[:, 0:T], ACT.Identity, a, xt[k], bias=b)
                xt[k] = [c3]
                tmp.free(i, c1, c2, c3)
                ht.append([c1, c2])
            tmp.free(ir, a)
            return ht, [a, s2.tok]

        for l in range(2):
            af = [arena_free["t"]]
            DQ, DK, DV, NQ, KD, VD, YCh, YCl = arena_open([
                (f"DQ{l}", [128, 4, T], F32), (f"DK{l}", [128, 4, T], F32), (f"DV{l}", [128, 2, 512], F32),
                (f"NQ{l}", [128, 4, T], F32), (f"KD{l}", [128, 2, 2, T], F32), (f"VD{l}", [128, 2, 2, 2, 128], F32),
                (f"YCh{l}", [128, 4, T], F32R), (f"YCl{l}", [128, 4, T], F32R)])

            lv = SM[:, 112:116]
            dl = vec("diff_lambda_2", 4 * l, 4)
            t0 = tt(lv[:, 0:1], dl[:, 0:1], dl[:, 1:2], ALU.mult, in_tok)
            t1 = tt(lv[:, 1:2], dl[:, 2:3], dl[:, 3:4], ALU.mult, in_tok)
            i, b, w = pst.get()
            t2 = mm(b[:, 0:2], con("ones"), lv[:, 0:2], True, True, t0, t1, w, inc=True)
            lam = SM[:, 116:120]
            t3 = act(lam[:, 0:2], b[:, 0:2], ACT.Exp, t2)
            pst.free(i, t3)
            t4 = tt(lam[:, 2:3], lam[:, 0:1], lam[:, 1:2], ALU.subtract, t3)
            lam_t = ts(lam[:, 3:4], lam[:, 2:3], LAM_INIT[l], None, ALU.add, None, t4)
            subln = SM[:, 120:121]
            sub_t = ts(subln, vec("diff_subln_2", l), 1.0 - LAM_INIT[l], None, ALU.mult, None, in_tok)

            def xlin():
                return lin(8, xh, xl, T, lambda k: xtoks[k])

            def roped(dst):
                i, bk, t = xlin()
                it, r_, w = tmp.get()
                a = act(r_[:, 0:T], bk, ACT.Copy, t, w)
                pm.free(i, a)
                tk = rope(dst, r_[:, 0:T], a, "rot2", "cos2", "sin2", af)
                tmp.free(it, tk)
                return tk

            dkt, dqt = [], []
            for m in range(4):
                dkt.append(roped(DK[:, m, :]))
                dqt.append(roped(DQ[:, m, :]))
            got, t = lin_tok("w", 512, 512, xh, xl, 2, lambda k: xtoks[k])
            dvt = []
            for s, (i, bk) in enumerate(got):
                a = act(DV[:, s, :], bk, ACT.Copy, t, af)
                pm.free(i, a)
                dvt.append(a)

            kvi = [tmp.get() for _ in range(2)]
            KC, VC = kvi[0][1][:, 0:T], kvi[1][1][:, 0:T]
            i, bk, t = xlin()
            ir_, r_, w = tmp.get()
            a = act(r_[:, 0:T], bk, ACT.Copy, t, w)
            pm.free(i, a)
            kct = rope(KC, r_[:, 0:T], a, "rot2", "cos2", "sin2", kvi[0][2])
            tmp.free(ir_, kct)
            kdt = []
            for br in range(2):
                i, bk, t = xlin()
                ir_, r_, w = tmp.get()
                a = act(r_[:, 0:T], bk, ACT.Copy, t, w)
                pm.free(i, a)
                a = rope(r_[:, 0:T], r_[:, 0:T], a, "rot2", "cos2", "sin2")
                for g in range(2):
                    i, b, w = pt.get()
                    t0 = mm(b[:, 0:T], con(f"dup{g}"), r_[:, 0:T], True, True, a, w, inc=True)
                    a2 = act(KD[:, br, g, :], b[:, 0:T], ACT.Copy, t0, af)
                    pt.free(i, a2)
                    kdt.append(a2)
                tmp.free(ir_, t0)
            i, bk, t = xlin()
            vct = act(VC, bk, ACT.Copy, t, kvi[1][2])
            pm.free(i, vct)

            kb = []
            for kv, (src, tok) in enumerate(((KC, kct), (VC, vct))):
                i, kbt, w = tmp.get()
                kbv = kbt[:, 0:480].rearrange("p (l g n) -> p l g n", l=16, g=2)
                tks = []
                for par in range(2):
                    for g in range(2):
                        for half in range(2):
                            sv = src[g * 64:(g + 1) * 64, half * 16:half * 16 + 240].rearrange("p (n l) -> p l n", l=16)
                            sv = sv[:, par:16:2, :]
                            dv = kbv[par * 64:(par + 1) * 64, half * 8:half * 8 + 8, g, :]
                            tks.append(vcopy(dv, sv, tok, w))
                pos = vec("nsa_cmp_pos_2", (l * 2 + kv) * 16, 16).rearrange("p (l o) -> p l o", o=1).broadcast_to((128, 16, 30))
                kb3 = kbt[:, 0:480].rearrange("p (l m) -> p l m", l=16)
                tk = tt(kb3, kb3, pos, ALU.add, tks)
                kb.append((i, kb3, tk))
                tmp.free(kvi[kv][0], tks)

            got, t = lin_tok("vvg", 512, 280, xh, xl, 2, lambda k: xtoks[k])
            gate = SM[:, 128:176].rearrange("p (s c) -> p s c", s=2)
            vdt, gat = [], []
            for s, (i, bk) in enumerate(got):
                b4 = bk[:, 0:256].rearrange("p (b g d) -> p b g d", b=2, g=2)
                a = act(VD[:, s, :, :, 0:64], b4, ACT.Copy, t, af)
                d_ = act(gate[:, s, :], bk[:, 256:280], ACT.Sigmoid, t, gate_free["t"] if l else None)
                c_ = vcopy(VD[:, s, :, :, 64:128], b4, t, d_, af)
                pm.free(i, a, c_, d_)
                vdt.append([a, c_])
                gat.append(d_)
            nqt = []
            for m in range(4):
                nqt.append(roped(NQ[:, m, :]))

            hT = []
            for kv in range(2):
                w1, wt_, c_ = take_raw(16)
                ib, b, w = pst.get()
                i, kb3, tk = kb[kv]
                for k in range(16):
                    t0 = mm(b[0:30, 0:128], kb3[:, k, :], w1[:, k * 128:(k + 1) * 128], k == 0, k == 15, tk, wt_, w, inc=k == 15)
                raw_rel[c_] = [t0]
                dma_chunks(c_ + NRAW + 1)
                tmp.free(i, t0)
                ig_, gl, wg = tmp.get()
                a = act(gl[0:30, 0:128], b[0:30, 0:128], ACT.Gelu, t0, wg)
                t1 = tr(b[:, 256:286], gl[0:30, 0:128], con("ident", 0, 30, 0, 30), a, inc=True)
                a2 = act(gl[:, 128:158], b[:, 256:286], ACT.Copy, t1)
                pst.free(ib, a2)
                hT.append((ig_, gl[:, 128:158], a2, gl))
            w2k = vec("nsa_phi_w2_2", (l * 2) * 128, 128)
            w2v = vec("nsa_phi_w2_2", (l * 2 + 1) * 128, 128)
            ib, b, w = pst.get()
            t0 = mm(b[:, 0:30], w2k, hT[0][1], True, True, hT[0][2], w, inc=True)
            kcc = hT[0][3][:, 160:190]
            kcct = act(kcc, b[:, 0:30], ACT.Copy, t0)
            for g in range(2):
                t0 = mm(b[0:15, 128 + g * 128:256 + g * 128], hT[1][1][:, g * 15:(g + 1) * 15], w2v, True, True, hT[1][2], kcct, inc=True)
            vcc = hT[1][3][0:15, 160:416].rearrange("p (g d) -> p g d", g=2)
            vcct = act(vcc, b[0:15, 128:384].rearrange("p (g d) -> p g d", g=2), ACT.Copy, t0)
            pst.free(ib, kcct, vcct)

            YA = lambda j: (Hh[:, 2048 + j * T:2048 + (j + 1) * T], Hl[:, 2048 + j * T:2048 + (j + 1) * T])
            yat = [None] * 12
            ga_t = [None] * 16

            def conv3(src, dst, w, bias, tok, wdst):
                if bias is None:
                    a = ts(dst, src[:, 0:T], w[0], None, ALU.mult, None, tok, wdst)
                else:
                    a = stt(dst, src[:, 0:T], w[0], bias.broadcast_to((128, T)), ALU.mult, ALU.add, tok, wdst)
                for i in (1, 2):
                    a = stt(dst, src[:, i:i + T], w[i], dst, ALU.mult, ALU.add, a)
                return a

            def fill_a(j):
                iv, bv, tv = xlin()
                ic, bc, tc = xlin()
                ix, bx, tx = xlin()
                i, t, w = tmp.get()
                a = act(t[:, 0:T], bv, ACT.Copy, tv, w)
                pm.free(iv, a)
                icb, cb, wc = cbr.get()
                b = tt(cb[:, 2:2 + T], bc, t[:, 0:T], ALU.mult, a, tc, wc, cb_zero)
                pm.free(ic, b)
                c_ = conv3(cb, t[:, 256:512], [vec("conv_a_w_2", l * 12 + q * 4 + j) for q in range(3)], None, b, w)
                cbr.free(icb, c_)
                d_ = tt(t[:, 0:T], bx, t[:, 256:512], ALU.mult, c_, tx)
                pm.free(ix, d_)
                yat[j] = split(*YA(j), t[:, 0:T], d_, y2read["t"])
                tmp.free(i, yat[j])

            def fill_g(m):
                i, bk, t = xlin()
                ga_t[m] = act(GT[m], bk, ACT.Sigmoid, t, y2free)
                pm.free(i, ga_t[m])

            if l == 0:
                y2read = {"t": [hfree["t"]]}
            fills = [(fill_a, j) for j in range(4)] + [(fill_g, m) for m in range(16)]

            def fill(n=1):
                for _ in range(n):
                    if fills:
                        f, a = fills.pop(0)
                        f(a)

            def masked(b, n, qt, p, mx, tok, wait):
                mask = con("causal", 128, 256) if qt == 0 else con("causal")
                t1 = V(lambda e: e.tensor_tensor_reduce(p, b, mask, 1.0, 0.0, ALU.add, ALU.max, mx[:, 0:1]), tok, wait, in_tok)
                t2 = ts(mx[:, 1:2], mx[:, 0:1], -SC, None, ALU.mult, None, t1)
                return t1, act(p, p, ACT.Exp, t2, bias=mx[:, 1:2], scale=SC, accum=mx[:, 2:3])

            PC = Y[0:15, 0:2048].rearrange("p (h q) -> p h q", h=8)
            pct = []
            for qt in range(2):
                pair = [pm.get() for _ in range(2)]
                for h in range(8):
                    o = (h % 2) * 64
                    g = h // 4
                    _, b, w = pair[h % 2]
                    t0 = mm(b[:, (h // 2) * 15:(h // 2) * 15 + 15], NQ[o:o + 64, h // 2, qt * 128:(qt + 1) * 128],
                            kcc[o:o + 64, g * 15:(g + 1) * 15], True, True, nqt, kcct, w, inc=h == 7)
                ic, t, wc = tmp.get()
                im, sm, wm = smr.get()
                ir_, rr, wr_ = tmp.get()
                v3 = lambda ap: ap.rearrange("p (h n) -> p h n", h=8)
                s3 = v3(t[:, 0:120])
                bro = lambda ap: ap.rearrange("p (o n) -> p o n", o=1).broadcast_to((128, 8, 15))
                bro4 = lambda ap: ap.rearrange("p (o n) -> p o n", o=1).broadcast_to((128, 4, 15))
                col = lambda ap: ap.rearrange("p (h o) -> p h o", o=1).broadcast_to((128, 8, 15))
                for par, (i, b, _) in enumerate(pair):
                    a = tt(s3[:, par:8:2, :], b[:, 0:60].rearrange("p (h n) -> p h n", h=4),
                           bro4(con("cmpadd", qt * 15, qt * 15 + 15)), ALU.add, t0, wc, in_tok)
                    pm.free(i, a)
                a = V(lambda e, s3=s3, rr=rr: e.tensor_reduce(rr[:, 0:8], s3, AX, ALU.max), a, wr_)
                a = tt(s3, s3, col(rr[:, 0:8]), ALU.subtract, a)
                a = act(t[:, 0:120], t[:, 0:120], ACT.Exp, a, scale=SC)
                a = V(lambda e, s3=s3, rr=rr: e.tensor_reduce(rr[:, 8:16], s3, AX, ALU.add), a)
                a = recip(rr[:, 16:24], rr[:, 8:16], a)
                a = tt(rr[:, 24:32], rr[:, 16:24], gate[:, qt, 0:24:3], ALU.mult, a, gat[qt])
                b2 = tt(s3, s3, bro(con("cmpok", qt * 15, qt * 15 + 15)), ALU.mult, a)
                a = tt(s3, s3, col(rr[:, 24:32]), ALU.mult, a, b2)
                tmp.free(ir_, a)
                smr.free(im)
                cpt = []
                for hh in range(2):
                    i, b, w = pt.get()
                    for h in range(4):
                        t0 = tr(b[0:15, h * 128:(h + 1) * 128], s3[:, hh * 4 + h, :], con("ident"), a, w, inc=h == 3)
                    c_ = act(PC[:, hh * 4:hh * 4 + 4, qt * 128:(qt + 1) * 128],
                             b[0:15, :].rearrange("p (h q) -> p h q", h=4), ACT.Copy, t0, y2free, yrest["t"] if l else None)
                    pt.free(i, c_)
                    pct.append(c_)
                tmp.free(ic, t0)
                fill()

            def d_scores(h, qt):
                n = 128 * (qt + 1)
                pair = [pm.get() for _ in range(2)]
                im, sm, wm = smr.get()
                ip, p, wp = tmp.get()
                sc_ = []
                for m, (i, b, w) in enumerate(pair):
                    o = m * 64
                    sc_.append(mm(b[:, 0:n], DQ[o:o + 64, h, qt * 128:(qt + 1) * 128], DK[o:o + 64, h, 0:n],
                                  True, True, dqt[h], dkt[h], w, inc=True))
                e = []
                for m, (i, b, w) in enumerate(pair):
                    t1, t2 = masked(b[:, 0:n], n, qt, p[:, m * 256:m * 256 + n], sm[:, 4 * m:4 * m + 4], sc_[m], [wp, wm])
                    e.append(t2)
                    pm.free(i, t1)
                a = recip(sm[:, 8:10], sm[:, 2:7:4], e)
                a2 = tt(sm[:, 10:11], sm[:, 9:10], lam[:, 3:4], ALU.mult, a, lam_t)
                a3 = ts(p[:, 256:256 + n], p[:, 256:256 + n], sm[:, 10:11], None, ALU.mult, None, a2)
                a4 = stt(p[:, 0:n], p[:, 0:n], sm[:, 8:9], p[:, 256:256 + n], ALU.mult, ALU.subtract, a3)
                smr.free(im, a4)
                return ip, p, a4

            def d_turn(h, qt, ip, p, tok):
                if qt == 0:
                    cur["aT"] = tmp.get()
                    cur["at"] = []
                ia, aT, wa = cur["aT"]
                i, b, w = pt.get()
                for s in range(qt + 1):
                    t0 = tr(b[:, s * 128:(s + 1) * 128], p[:, s * 128:(s + 1) * 128], con("ident"), tok, w, inc=s == qt)
                tmp.free(ip, t0)
                a3 = aT.rearrange("p (s q) -> p s q", s=2)
                t1 = act(a3[:, 0:qt + 1, qt * 128:(qt + 1) * 128], b[:, 0:128 * (qt + 1)].rearrange("p (s q) -> p s q", q=128),
                         ACT.Copy, t0, wa)
                pt.free(i, t1)
                cur["at"].append(t1)
                if qt == 1:
                    i, b, w = pm.get()
                    mm(b[:, 0:T], DV[:, 0, h * 128:(h + 1) * 128], a3[:, 0, :], True, False, cur["at"], dvt, w)
                    t0 = mm(b[:, 128:T], DV[:, 1, h * 128:(h + 1) * 128], a3[:, 1, 128:T], False, True, inc=True)
                    tmp.free(ia, t0)
                    io, o_, wo_ = tmp.get()
                    a = act(o_[:, 0:T], b[:, 0:T], ACT.Copy, t0, wo_)
                    pm.free(i, a)
                    s_ = Stat(T, "mean128", 1)
                    s_.square(o_[:, 0:T], a)
                    ir, r, t1, t0 = rstd(s_.bank, T, s_.tok, "eps5")
                    pst.free(s_.i, t0)
                    c_ = stt(o_[:, 0:T], o_[:, 0:T], subln, r, ALU.mult, ALU.mult, t1, sub_t)
                    tmp.free(ir, c_)
                    yat[4 + h] = split(*YA(4 + h), o_[:, 0:T], c_, y2read["t"])
                    tmp.free(io, yat[4 + h])

            def n_scores(h, qt):
                n = 128 * (qt + 1)
                o = (h % 2) * 64
                g = h // 4
                i, b, w = pm.get()
                im, sm, wm = smr.get()
                ip, p, wp = tmp.get()
                for br in range(2):
                    t0 = mm(b[:, br * 256:br * 256 + n], NQ[o:o + 64, h // 2, qt * 128:(qt + 1) * 128], KD[o:o + 64, br, g, 0:n],
                            True, True, nqt, kdt, w, inc=True)
                e, rd = [], []
                for br in range(2):
                    t1, t2 = masked(b[:, br * 256:br * 256 + n], n, qt, p[:, br * 256:br * 256 + n], sm[:, 4 * br:4 * br + 4], t0, [wp, wm])
                    e.append(t2)
                    rd.append(t1)
                pm.free(i, rd)
                a = recip(sm[:, 8:10], sm[:, 2:7:4], e)
                a = tt(sm[:, 10:12], sm[:, 8:10], gate[:, qt, 3 * h + 1:3 * h + 3], ALU.mult, a, gat[qt])
                for br in range(2):
                    c_ = ts(p[:, br * 256:br * 256 + n], p[:, br * 256:br * 256 + n], sm[:, 10 + br:11 + br], None, ALU.mult, None, a)
                smr.free(im, c_)
                return ip, p, c_

            yct = [[] for _ in range(4)]

            def n_turn(h, qt, ip, p, tok):
                if qt == 0:
                    cur["nT"] = [tmp.get(), tmp.get()]
                    cur["nt"] = []
                i, b, w = pt.get()
                for br in range(2):
                    for s in range(qt + 1):
                        t0 = tr(b[:, br * 256 + s * 128:br * 256 + (s + 1) * 128], p[:, br * 256 + s * 128:br * 256 + (s + 1) * 128],
                                con("ident"), tok, w, inc=br == 1 and s == qt)
                tmp.free(ip, t0)
                rd = []
                for br in range(2):
                    ia, aT, wa = cur["nT"][br]
                    a3 = aT.rearrange("p (s q) -> p s q", s=2)
                    rd.append(act(a3[:, 0:qt + 1, qt * 128:(qt + 1) * 128],
                                  b[:, br * 256:br * 256 + 128 * (qt + 1)].rearrange("p (s q) -> p s q", q=128), ACT.Copy, t0, wa))
                pt.free(i, rd)
                cur["nt"] += rd
                if qt == 1:
                    o = (h % 2) * 64
                    g = h // 4
                    i, b, w = pm.get()
                    mm(b[:, 0:T], vcc[:, g, :], PC[:, h, :], True, False, pct, vcct, w)
                    for br in range(2):
                        a3 = cur["nT"][br][1].rearrange("p (s q) -> p s q", s=2)
                        mm(b[:, 0:T], VD[:, 0, br, g, :], a3[:, 0, :], False, False, cur["nt"], vdt)
                        t0 = mm(b[:, 128:T], VD[:, 1, br, g, :], a3[:, 1, 128:T], False, br == 1, inc=br == 1)
                    for br in range(2):
                        tmp.free(cur["nT"][br][0], t0)
                    hi, lo = YCh[o:o + 64, h // 2, :], YCl[o:o + 64, h // 2, :]
                    c1 = act(hi, b[o:o + 64, 0:T], ACT.Copy, t0, af)
                    c2 = tt(lo, b[o:o + 64, 0:T], f32(hi), ALU.subtract, t0, c1, af)
                    pm.free(i, c1, c2)
                    yct[h // 2] += [c1, c2]

            work = [(d_scores, d_turn, h, qt) for h in range(4) for qt in range(2)]
            work += [(n_scores, n_turn, h, qt) for h in range(8) for qt in range(2)]
            pend = []
            for n_, (f, g_, h, qt) in enumerate(work):
                pend.append((g_, h, qt, *f(h, qt)))
                if n_ % 4 != 3:
                    fill()
                if len(pend) > 1:
                    g_, *rest = pend.pop(0)
                    g_(*rest)
            while pend:
                g_, *rest = pend.pop(0)
                g_(*rest)
                fill()
            fill(100)
            for i, _, _, _ in hT:
                tmp.free(i, (P.sem, P.n))
            gate_free = {"t": [(V.sem, V.n)]}

            zdone = [(P.sem, P.n)]
            mgt = []
            for m in range(8):
                i2, b2_, t2 = xlin()
                i, t, w = tmp.get()
                g2 = act(t[:, 256:512], b2_, ACT.Sigmoid, t2, w)
                pm.free(i2, g2)
                acc = None
                im_, mg, wm_ = tmp.get()
                for br in range(3):
                    if br < 2:
                        ib, bb, tb = lin(4, lambda k: YA(4 * br + k)[0], lambda k: YA(4 * br + k)[1], T, lambda k: yat[4 * br + k])
                        gt_, gtk = GT[8 * br + m], ga_t[8 * br + m]
                    else:
                        ib, bb, tb = lin(4, lambda k: YCh[:, k, :], lambda k: YCl[:, k, :], T, lambda k: yct[k])
                        gt_, gtk = t[:, 256:512], g2
                    if br == 0:
                        acc = tt(mg[:, 0:T], bb, gt_, ALU.mult, tb, gtk, wm_)
                        pm.free(ib, acc)
                    else:
                        a = tt(t[:, 0:T], bb, gt_, ALU.mult, tb, gtk, w, acc)
                        pm.free(ib, a)
                        acc = tt(mg[:, 0:T], mg[:, 0:T], t[:, 0:T], ALU.add, acc, a)
                tmp.free(i, acc)
                mgc = act(Y[:, m * T:(m + 1) * T], mg[:, 0:T], ACT.Copy, acc, zdone)
                tmp.free(im_, mgc)
                mgt.append(mgc)
            xdone = [t2]
            y2read = {"t": [(P.sem, P.n)]}
            arena_free["t"] = [(P.sem, P.n), (V.sem, V.n)]
            ot = []
            for k in range(8):
                ot.append(split(xh(k), xl(k), Y[:, k * T:(k + 1) * T], mgt[k], xdone))
            stat = Stat(T)
            toks = []
            for m in range(8):
                i, bk, t = lin(8, xh, xl, T, lambda k: ot[k])
                y = Y[:, m * T:(m + 1) * T]
                a = stt(y, X[:, 0, m, :], ALPHA, bk, ALU.mult, ALU.add, t, ot, xt[m])
                pm.free(i, a)
                stat.tok = stat.add(y, a)
                toks.append(a)
            ht, ydone = layer_norm(toks, stat, "ln1_g_2", "ln1_b_2", l, [t])

            HIh, HIl = arena_open([(f"fh{l}", [128, 16, T], F32R), (f"fl{l}", [128, 16, T], F32R)])
            hidfree = list(arena_free["t"])
            lo_queue["f"] = lambda p: G if p % 3 == 2 else V
            j0 = 0
            toks = [None] * 8
            for pi, cnt in enumerate(FFN1):
                gt = []
                for j in range(cnt):
                    jj = j0 + j
                    res = []
                    for half in range(2):
                        c_ = jj + 22 * half
                        i, bk, t = lin(8, xh, xl, T, lambda k: ht[k])
                        icb, cb, wc = cbr.get()
                        a = act(cb[:, 2:2 + T], bk, ACT.Copy, t, wc, cb_zero)
                        pm.free(i, a)
                        it, tb, wt_ = tmp.get()
                        a = conv3(cb, tb[:, 0:T], [vec("ffn_conv_w_2", l * 132 + q * 44 + c_) for q in range(3)],
                                  vec("ffn_conv_b_2", l * 44 + c_), a, wt_)
                        cbr.free(icb, a)
                        res.append((it, tb, a))
                    (ia, ta_, aa), (iu, tu, au) = res
                    b = act(ta_[:, 0:T], ta_[:, 0:T], ACT.Gelu, aa)
                    c_ = tt(tu[:, 0:T], ta_[:, 0:T], tu[:, 0:T], ALU.mult, b, au)
                    tmp.free(ia, c_)
                    tk = split(HIh[:, j, :], HIl[:, j, :], tu[:, 0:T], c_, hidfree)
                    tmp.free(iu, tk)
                    gt.append(tk)
                if pi == 1:
                    stat = Stat(T)
                for m in range(8):
                    i, bk, t = lin(cnt, lambda k: HIh[:, k, :], lambda k: HIl[:, k, :], T, lambda k: gt[k])
                    y = Y[:, m * T:(m + 1) * T]
                    if pi == 0:
                        toks[m] = stt(y, X[:, 0, m, :], ALPHA, bk, ALU.mult, ALU.add, t, ydone, xt[m])
                    else:
                        toks[m] = tt(y, bk, y, ALU.add, t, toks[m])
                        stat.tok = stat.add(y, toks[m])
                    pm.free(i, toks[m])
                hidfree = [t]
                j0 += cnt
            lo_queue["f"] = lambda p: V
            arena_free["t"] = [t]
            xtoks, yd = layer_norm(toks, stat, "ln2_g_2", "ln2_b_2", l, [t])
            yrest = {"t": yd}
            y2free = [yd]

        assert st["blk"] == len(plan)
        for k in range(8):
            S.items.append((flat(xt[k]), lambda e, k=k: e.dma_start(
                out[k * 128:(k + 1) * 128, :], X[:, 0, k, :]).then_inc(s_out, 16), False))
        for cm in reversed(arena):
            cm.__exit__(None, None, None)

        block = ctx.enter_context(nc.Block())

        @block.sync
        def _(eng):
            S.play(eng)
            eng.wait_ge(s_out, 16 * 8)

        @block.scalar
        def _(eng):
            A.play(eng)

        @block.vector
        def _(eng):
            V.play(eng)

        @block.gpsimd
        def _(eng):
            G.play(eng)

        @block.tensor
        def _(eng):
            P.play(eng)


def const_array():
    off, n = const_plan()
    c = np.zeros((128, n), np.float32)

    def put(name, a):
        c[:, off[name]:off[name] + a.shape[1]] = a

    i = np.arange(128)
    put("ident", np.eye(128))
    put("ones", np.ones((128, 128)))
    put("mean", np.full((128, 128), 1.0 / 1024))
    put("mean128", np.full((128, 128), 1.0 / 128))
    put("mean64", (i[:, None] // 64 == i[None, :] // 64) / 64.0)
    r1 = np.zeros((128, 128))
    for j in range(0, 128, 2):
        r1[j + 1, j] = -1
        r1[j, j + 1] = 1
    put("rot1", r1)
    r2 = np.zeros((128, 128))
    for b in (0, 64):
        for j in range(8):
            r2[b + 8 + j, b + j] = -1
            r2[b + j, b + 8 + j] = 1
    put("rot2", r2)
    for g in range(2):
        put(f"dup{g}", (i[:, None] == g * 64 + i[None, :] % 64).astype(np.float32))
    f = np.float32
    t = np.arange(T)
    freq = (f(10000.0) ** (-np.arange(16, dtype=f) / f(16))).astype(f)
    ang = np.concatenate([(t // 64).astype(f)[:, None] * freq, (t % 64).astype(f)[:, None] * freq], 1)
    put("cos1", np.cos(ang).T[(i % 64) // 2])
    put("sin1", np.sin(ang).T[(i % 64) // 2])
    inv = (f(500000.0) ** (-np.arange(0, 16, 2, dtype=f) / f(16))).astype(f)
    ang = t.astype(f)[:, None] * inv
    d = i % 64
    put("cos2", np.where(d[:, None] < 16, np.cos(ang).T[d % 8], 1.0))
    put("sin2", np.where(d[:, None] < 16, np.sin(ang).T[d % 8], 0.0))
    put("causal", np.concatenate([np.zeros((128, 128)), np.where(i[None, :] <= i[:, None], 0.0, -1e30)], 1))
    ok = np.concatenate([(np.arange(15) * 16 + 31)[None, :] <= (q * 128 + i)[:, None] for q in range(2)], 1)
    put("cmpok", ok.astype(np.float32))
    put("cmpadd", np.where(ok, 0.0, -1e30))
    put("eps6", np.full((128, 1), 1e-6))
    put("eps5", np.full((128, 1), 1e-5))
    return c


def vec_array(a):
    off, n = vec_plan()
    v = np.zeros((128, n), np.float32)

    def put(name, m):
        v[:m.shape[0], off[name]:off[name] + m.shape[1]] = m

    def cols(x):
        return np.asarray(x).reshape(-1, 128).T

    for name in ("c", "c_ctx", "b_mod", "norm_g", "conv_b_pw1", "conv_w_dw", "conv_b_dw", "conv_ln_g", "conv_ln_b",
                 "conv_b_pw2", "conv_a_w_2", "diff_subln_2", "ln1_g_2", "ln1_b_2", "ln2_g_2", "ln2_b_2",
                 "ffn_conv_w_2", "ffn_conv_b_2"):
        put(name, cols(a[name]))
    for name in ("attn_q_g", "attn_k_g"):
        g = np.asarray(a[name]).reshape(64, 1)
        put(name, np.concatenate([g, g], 0))
    put("diff_lambda_2", np.asarray(a["diff_lambda_2"]).reshape(8, 64).T)
    put("nsa_cmp_pos_2", cols(a["nsa_cmp_pos_2"]))
    w2 = np.asarray(a["nsa_phi_w2_2"]).reshape(4, 128, 64).transpose(1, 0, 2)
    put("nsa_phi_w2_2", np.concatenate([w2, w2], 2).reshape(128, 512))
    return v


def stream_array(a):
    plan, total = stream_plan()
    w = np.zeros((total // CHUNK, 128, CHUNK), np.float32)
    for at, (kind, name, idx, r0, c0, n, width) in plan:
        dst = w[at // CHUNK, :, at % CHUNK:at % CHUNK + n]
        src = np.asarray(a[name])[idx]
        rows = src[r0:r0 + 128]
        if kind == "vvg":
            dst[:, 0:128] = rows[:, 3584 + 3 * 128:3584 + 4 * 128]
            dst[:, 128:256] = rows[:, 3584 + 5 * 128:3584 + 6 * 128]
            dst[:, 256:280] = rows[:, 4352:4376]
        else:
            dst[:] = rows[:, c0:c0 + n]
    return w


def kernel(**inputs):
    import concourse.bacc as bacc
    from concourse.bass_utils import run_bass_kernel_spmd

    a = {k: np.asarray(v) for k, v in inputs.items()}

    def feat(x):
        return np.ascontiguousarray(x[0].T.reshape(8, 128, T).transpose(1, 0, 2))

    arrays = {
        "wstream": stream_array(a),
        "vecs": vec_array(a),
        "consts": const_array(),
        "xin": np.stack([feat(a["x"]), feat(a["ctx"])]),
    }
    nc = bacc.Bacc("TRN2", target_bir_lowering=False, num_devices=1)
    aps = [nc.dram_tensor(n, v.shape, F32, kind="ExternalInput").ap() for n, v in arrays.items()]
    out = nc.dram_tensor("out", (D, T), F32, kind="ExternalOutput").ap()
    build(nc, *aps, out)
    r = run_bass_kernel_spmd(nc, [arrays], core_ids=[0])
    got = np.asarray(r.results[0]["out"])
    return np.ascontiguousarray(got.T)[None]
```

```python
import numpy as np
from contextlib import ExitStack

import concourse.bass as bass
from concourse import mybir

F32 = mybir.dt.float32
F32R = mybir.dt.float32r
ACT = mybir.ActivationFunctionType
ALU = mybir.AluOpType
AX = mybir.AxisListType.X

D = 1024
T = 256
FT = 22
PIECE = 1024
NRAW = 7
NPIECE = 5
NTMP = 11
NCB = 3
ALPHA = 4 ** 0.25
HD = 64
LAM_INIT = [0.8 - 0.6 * float(np.exp(-0.3 * l)) for l in range(2)]
CONVW = 31
PAD = 15
FFN0 = [8, 7, 7]
FFN1 = [11, 11]


def stream_blocks():
    b = []

    def cols(name, idx, c0, n, width, k0=0, kt=8):
        b.extend(("w", name, idx, (k0 + k) * 128, c0, n, width) for k in range(kt))

    def group(tiles, k0=0, kt=8):
        for k in range(k0, k0 + kt):
            b.extend(("w", name, idx, k * 128, c0, 128, 128) for name, idx, c0 in tiles)

    def run(tiles, first, k0=0, kt=8):
        group(tiles[:first], k0, kt)
        for t in tiles[first:]:
            group([t], k0, kt)

    def mod(l, g0, g1):
        for g in range(g0, g1):
            cols("w_mod", (l,), g * 512, 512, 512)

    def ffn(up, down, l, parts):
        j0 = 0
        for n in parts:
            run([(name, (l,), c0 + j * 128) for j in range(j0, j0 + n) for name, c0 in up], 4)
            run([(down, (l,), m * 128) for m in range(8)], 4, j0, n)
            j0 += n

    w13 = (("ffn_w1", 0), ("ffn_w3", 0))
    mod(0, 0, 4)
    run([("conv_w_pw1", (0,), (o + j) * 128) for j in range(8) for o in (8, 0)], 4)
    mod(0, 4, 12)
    mod(1, 0, 4)
    run([("conv_w_pw2", (0,), m * 128) for m in range(8)], 4)
    ffn(w13, "ffn_w2", 0, FFN0)
    run([("attn_wk", (0,), m * 128) for m in range(2)], 2)
    cols("attn_wv", (0,), 0, 256, 256)
    run([("attn_wq", (0,), m * 128) for m in range(8)], 1)
    mod(1, 4, 12)
    run([("attn_wo", (0,), m * 128) for m in range(8)], 4)
    ffn(w13, "ffn_w2", 1, FFN1)
    for l in range(2):
        def z(*tiles, first=1):
            run([("w_in_2", (l,), c0) for c0 in tiles], first)

        z(*[o + 128 * m for m in range(4) for o in (2048, 1536)], first=4)
        cols("w_in_2", (l,), 2560, 512, 512)
        z(*[128 * m for m in (28, 30, 32, 29)])
        for k in range(8):
            b.append(("vvg", "w_in_2", (l,), k * 128, 0, 280, 512))
        z(*[3072 + 128 * m for m in range(4)])
        for kv in range(2):
            for k in range(16):
                b.append(("raw", "nsa_phi_w1_2", (l, kv), k * 128, 0, 128, 128))
        z(*[o + 128 * j for j in range(4) for o in (1024, 512, 0)])
        z(*[4376 + 128 * m for m in range(16)])
        for m in range(8):
            z(4376 + (16 + m) * 128)
            for br in range(3):
                group([("w_branch_2", (l, br), m * 128)], 0, 4)
        run([("w_o_2", (l,), m * 128) for m in range(8)], 4)
        ffn((("ffn_w_up_2", 0), ("ffn_w_up_2", 2816)), "ffn_w_down_2", l, FFN1)
    return b


def stream_plan():
    out, at = [], 0
    for blk in stream_blocks():
        width = blk[6]
        assert at % PIECE + width <= PIECE
        out.append((at, blk))
        at += width
    assert at % PIECE == 0
    return out, at


def vec_plan():
    off, at = {}, 0
    for name, n in (("c", 8), ("c_ctx", 8), ("b_mod", 96), ("norm_g", 64), ("conv_b_pw1", 16), ("conv_w_dw", 248),
                    ("conv_b_dw", 8), ("conv_ln_g", 8), ("conv_ln_b", 8), ("conv_b_pw2", 8), ("attn_q_g", 1),
                    ("attn_k_g", 1), ("conv_a_w_2", 24), ("diff_lambda_2", 8), ("diff_subln_2", 2),
                    ("nsa_cmp_pos_2", 64), ("ln1_g_2", 16), ("ln1_b_2", 16), ("ln2_g_2", 16), ("ln2_b_2", 16),
                    ("ffn_conv_w_2", 264), ("ffn_conv_b_2", 88), ("nsa_phi_w2_2", 512)):
        off[name] = at
        at += n
    return off, at


CONSTS = (("ident", 128), ("ones", 128), ("mean", 128), ("mean128", 128), ("mean64", 128), ("rot1", 128), ("rot2", 128),
          ("dup0", 128), ("dup1", 128), ("cos1", 256), ("sin1", 256), ("cos2", 256), ("sin2", 256), ("causal", 256),
          ("cmpadd", 30), ("cmpok", 30), ("eps6", 1), ("eps5", 1))


def const_plan():
    off, at = {}, 0
    for name, n in CONSTS:
        off[name] = at
        at += n
    return off, at


class Queue:
    def __init__(self, sem):
        self.sem, self.items, self.n = sem, [], 0

    def __call__(self, fn, *after, inc=True):
        self.items.append((flat(after), fn, inc))
        if inc:
            self.n += 1
        return (self.sem, self.n)

    def play(self, eng):
        seen = {}
        for waits, fn, inc in self.items:
            most = {}
            for s, v in waits:
                if v > seen.get(id(s), 0) and v > most.get(id(s), (s, 0))[1]:
                    most[id(s)] = (s, v)
            for key, (s, v) in most.items():
                eng.wait_ge(s, v)
                seen[key] = v
            ins = fn(eng)
            if inc:
                ins.then_inc(self.sem, 1)


def flat(x):
    if x is None:
        return []
    if isinstance(x, tuple) and len(x) == 2 and isinstance(x[1], int):
        return [x]
    return [t for y in x for t in flat(y)]


class Ring:

    def __init__(self, bufs):
        self.bufs, self.rel, self.at = bufs, [[] for _ in bufs], 0

    def get(self):
        i = next(j % len(self.bufs) for j in range(self.at, self.at + len(self.bufs)) if self.rel[j % len(self.bufs)] is not None)
        self.at = i + 1
        w = self.rel[i]
        self.rel[i] = None
        return i, self.bufs[i], w

    def free(self, i, *toks):
        assert self.rel[i] is None
        self.rel[i] = flat(toks)


class Pipe:

    def __init__(self):
        self.tasks = []

    def run(self, task):
        old, self.tasks = self.tasks, []
        for t in [task] + old:
            if next(t, self) is not self:
                self.tasks.append(t)
        if task in self.tasks:
            self.tasks.remove(task)
            self.tasks.append(task)

    def step(self):
        self.tasks = [t for t in self.tasks if next(t, self) is not self]

    def drain(self):
        while self.tasks:
            self.step()


def build(nc, wstream, vecs_d, const_d, xin, out):
    plan, total = stream_plan()
    voff, nvec = vec_plan()
    coff, ncon = const_plan()
    npiece = total // PIECE
    ctx = ExitStack()
    with ctx:
        def sb(name, shape, dt=F32):
            return ctx.enter_context(nc.sbuf_tensor(name, shape, dt))

        def sem(name):
            return ctx.enter_context(nc.semaphore(name))

        raw = sb("raw", [128, NRAW, PIECE])
        whi = sb("whi", [128, NPIECE, PIECE], F32R)
        wlo = sb("wlo", [128, NPIECE, PIECE], F32R)
        X = sb("X", [128, 2, 8, T])
        Hh = sb("Hh", [128, 4096], F32R)
        Hl = sb("Hl", [128, 4096], F32R)
        Y = sb("Y", [128, 4096])
        VEC = sb("VEC", [128, nvec])
        CON = sb("CON", [128, ncon])
        MOD = sb("MOD", [128, 2, 48, 2])
        MA = sb("MA", [128, 2, 4, 2, 8])
        CS = sb("CS", [128, 8, 4], F32R)
        SM = sb("SM", [128, 256])
        tmpb = sb("tmpb", [128, NTMP, 512])
        cbb = sb("cbb", [128, NCB, 260])
        arena = []

        def arena_open(specs):
            for cm in reversed(arena):
                cm.__exit__(None, None, None)
            arena.clear()
            got = []
            for name, shape, dt in specs:
                cm = nc.sbuf_tensor(name, shape, dt)
                got.append(cm.__enter__())
                arena.append(cm)
            return got

        banks = [ctx.enter_context(nc.psum_tensor(f"pb{i}", [128, 512], F32)) for i in range(8)]

        S, A, V, G, P = (Queue(sem(n)) for n in ("s_sync", "s_act", "s_dve", "s_pool", "s_pe"))
        s_raw = [sem(f"s_raw{i}") for i in range(NRAW)]
        s_con = sem("s_con")
        s_x = sem("s_x")
        s_out = sem("s_out")

        tmp = Ring([tmpb[:, i, :] for i in range(NTMP)])
        cbr = Ring([cbb[:, i, :] for i in range(NCB)])
        pm = Ring([b[:, :] for b in banks[0:5]])
        pt = Ring([b[:, :] for b in banks[5:7]])
        pst = Ring([b[:, :] for b in banks[7:8]])

        def con(name, a=0, b=None, p0=0, p1=128):
            n = dict(CONSTS)[name]
            return CON[p0:p1, coff[name] + a:coff[name] + (n if b is None else b)]

        def vec(name, i=0, n=1):
            return VEC[:, voff[name] + i:voff[name] + i + n]

        def act(out_, in_, func, *after, bias=None, scale=None, accum=None):
            kw = {}
            if bias is not None:
                kw["bias"] = bias
            if scale is not None:
                kw["scale"] = scale
            if accum is not None:
                kw["accum_out"] = accum
            return A(lambda e: e.activation(out_, in_, func, **kw), *after)

        def tt(out_, a, b, op, *after, q=None):
            return (q or V)(lambda e: e.tensor_tensor(out_, a, b, op), *after)

        def stt(out_, a, s, b, op0, op1, *after):
            return V(lambda e: e.scalar_tensor_tensor(out=out_, in0=a, scalar=s, in1=b, op0=op0, op1=op1), *after)

        def ts(out_, a, s1, s2, op0, op1, *after):
            if op1 is None:
                return V(lambda e: e.tensor_scalar(out_, a, s1, None, op0), *after)
            return V(lambda e: e.tensor_scalar(out_, a, s1, s2, op0, op1), *after)

        def vcopy(out_, a, *after):
            return V(lambda e: e.tensor_copy(out_, a), *after)

        def recip(out_, a, *after):
            return V(lambda e: e.reciprocal(out_, a), *after)

        def rmax(out_, a, *after):
            return V(lambda e: e.reduce_max(out_, a, AX), *after)

        def mm(out_, lhsT, rhs, start, stop, *after, inc=False):
            return P(lambda e: e.matmul(out_, lhsT, rhs, start=start, stop=stop), *after, inc=inc)

        def tr(out_, in_, idn, *after, inc=False):
            return P(lambda e: e.transpose(out_, in_, idn), *after, inc=inc)

        def f32(ap):
            return ap.bitcast(F32)

        def load(dst, src, s):
            S.items.append(([], lambda e: e.dma_start(dst, src).then_inc(s, 16), False))

        load(VEC[:, :], vecs_d, s_con)
        load(CON[:, :], const_d, s_con)
        in_tok = (s_con, 32)
        x_tok = (s_x, 32)

        st = {"blk": 0, "made": 0, "dma": 0, "parts": 0}
        raw_rel = {}
        owner = [None] * NPIECE
        piece = {}
        piece_rel = {}
        raw_kind = {at // PIECE for at, blk in plan if blk[0] == "raw"}
        lo_queue = {"f": lambda p: V}
        hook = {"f": lambda: None}

        def raw_tok(p):
            return (s_raw[p % NRAW], 16 * (p // NRAW + 1))

        def dma_pieces():
            while st["dma"] < npiece:
                p = st["dma"]
                if p >= NRAW and p - NRAW not in raw_rel:
                    return
                s = s_raw[p % NRAW]
                S.items.append((flat(raw_rel.get(p - NRAW)), lambda e, p=p, s=s: e.dma_start(
                    raw[:, p % NRAW, :], wstream[p]).then_inc(s, 16), False))
                st["dma"] += 1
                if p == 3:
                    for seg in range(2):
                        load(X[:, seg, :, :], xin[seg], s_x)

        def make_pieces(upto):
            while st["made"] < min(upto, npiece):
                p = st["made"]
                dma_pieces()
                if p in raw_kind:
                    st["made"] += 1
                    continue
                i = st["parts"] % NPIECE
                if owner[i] is not None and owner[i] not in piece_rel:
                    return
                free = piece_rel[owner[i]] if owner[i] is not None else []
                src, hi, lo = raw[:, p % NRAW, :], whi[:, i, :], wlo[:, i, :]
                a = act(hi, src, ACT.Copy, raw_tok(p), free)
                b = tt(lo, src, f32(hi), ALU.subtract, a, free, q=lo_queue["f"](p))
                owner[i] = p
                piece[p] = (hi, lo, [a, b])
                raw_rel[p] = [a, b]
                st["made"] += 1
                st["parts"] += 1
                dma_pieces()

        def take(kind, width):
            at, blk = plan[st["blk"]]
            st["blk"] += 1
            assert blk[0] == kind and blk[6] == width, (blk, kind, width)
            p, o = at // PIECE, at % PIECE
            make_pieces(p + NPIECE)
            if o == 0:
                hook["f"]()
            hi, lo, toks = piece[p]
            return hi[:, o:o + width], lo[:, o:o + width], toks, p, o + width == PIECE

        def take_raw(n):
            at, blk = plan[st["blk"]]
            assert blk[0] == "raw" and at % PIECE == 0
            st["blk"] += n
            p = at // PIECE
            dma_pieces()
            assert st["dma"] > p
            return raw[:, p % NRAW, :], raw_tok(p), p

        def done(p, tok):
            piece_rel[p] = [tok]

        def lins(g, kt, xh, xl, n, xtok):
            got = [pm.get() for _ in range(g)]
            toks = [None] * g
            for k in range(kt):
                for m, (i, bank, w) in enumerate(got):
                    hi, lo, pk, p, end = take("w", 128)
                    o = bank[:, 0:n]
                    mm(o, hi, xh(k), k == 0, False, pk, w, xtok(k))
                    mm(o, hi, xl(k), False, False)
                    toks[m] = mm(o, lo, xh(k), False, k == kt - 1, inc=end or k == kt - 1)
                    if end:
                        done(p, toks[m])
            return [(i, bank[:, 0:n], t) for (i, bank, w), t in zip(got, toks)]

        def lin(kt, xh, xl, n, xtok):
            return lins(1, kt, xh, xl, n, xtok)[0]

        def lin_run(count, first, *a):
            yield from lins(first, *a)
            for _ in range(count - first):
                yield lin(*a)

        def lin_tok(kind, width, n, xh, xl, tiles, xtok):
            got = [pm.get() for _ in range(tiles)]
            for k in range(8):
                hi, lo, pk, p, end = take(kind, width)
                for s, (i, bank, w) in enumerate(got):
                    o = bank[:, 0:n]
                    xa, xb = xh(k)[:, s * 128:(s + 1) * 128], xl(k)[:, s * 128:(s + 1) * 128]
                    mm(o, xa, hi[:, 0:n], k == 0, False, pk, w, xtok(k))
                    mm(o, xb, hi[:, 0:n], False, False)
                    tok = mm(o, xa, lo[:, 0:n], False, k == 7, inc=k == 7 or (end and s == tiles - 1))
                if end:
                    done(p, tok)
            return [(i, bank[:, 0:n]) for i, bank, w in got], tok

        def split(hi, lo, src, *after):
            a = act(hi, src, ACT.Copy, *after)
            b = tt(lo, src, f32(hi), ALU.subtract, a, *after)
            return [a, b]

        def rstd(bank, n, tok, eps):
            ia, ta, wa = tmp.get()
            ir, r, wr = tmp.get()
            t0 = act(ta[:, 0:n], bank[:, 0:n], ACT.Sqrt, tok, wa, in_tok, bias=con(eps))
            t1 = recip(r[:, 0:n], ta[:, 0:n], t0, wr)
            tmp.free(ia, t1)
            return ir, r[:, 0:n], t1, t0

        def preload(func):
            A(lambda e: e.activation(SM[:, 255:256], CON[:, coff["eps6"]:coff["eps6"] + 1], func), in_tok)

        class Stat:

            def __init__(self, n, mat="mean", kt=8, adds=False, ring=None):
                self.n, self.mat, self.kt, self.k, self.adds = n, mat, kt, 0, adds
                self.ring = ring or pst
                self.i = None

            def open(self):
                if self.i is None:
                    self.i, self.bank, self.w = self.ring.get()
                    self.bank = self.bank[:, 0:self.n]

            def add(self, tile, tok):
                k = self.k
                self.k += 1
                if not self.adds:
                    self.open()
                    self.tok = mm(self.bank, con(self.mat), tile, k == 0, k == self.kt - 1, tok, self.w, in_tok, inc=True)
                    return self.tok
                if k == 0:
                    self.ia, t, w = tmp.get()
                    self.acc = t[:, 0:self.n]
                    self.at = vcopy(self.acc, tile, tok, w)
                else:
                    self.at = tt(self.acc, self.acc, tile, ALU.add, tok, self.at)
                rd = self.at
                self.close()
                return rd

            def close(self):
                if self.k == self.kt:
                    self.open()
                    self.tok = mm(self.bank, con(self.mat), self.acc, True, True, self.at, self.w, in_tok, inc=True)
                    tmp.free(self.ia, self.tok)

            def square(self, src, tok):
                if self.k == self.kt - 1:
                    preload(ACT.Sqrt)
                if self.adds and self.k == 0:
                    self.k = 1
                    self.ia, t, w = tmp.get()
                    self.acc = t[:, 0:self.n]
                    self.at = act(self.acc, src, ACT.Square, tok, w)
                    return self.at
                i, t, w = tmp.get()
                a = act(t[:, 0:self.n], src, ACT.Square, tok, w)
                tmp.free(i, self.add(t[:, 0:self.n], a))
                return a

            def free(self, *toks):
                self.ring.free(self.i, *toks)

        sil = SM[:, 0:16]
        t_sil = act(sil, vec("c", 0, 16), ACT.Silu, in_tok)
        csv = sil.rearrange("p (s k) -> p k s", s=2)
        t_cs = act(CS[:, :, 0:2], csv, ACT.Copy, t_sil)
        t_cs2 = tt(CS[:, :, 2:4], csv, f32(CS[:, :, 0:2]), ALU.subtract, t_cs)
        mod_tok = {}
        pipe = Pipe()
        mrow = {}

        def mod_group(l, g):
            i, bank, w = pm.get()
            for k in range(8):
                hi, lo, pk, p, end = take("w", 512)
                mm(bank[0:4, :], CS[:, k, :], hi, k == 0, False, pk, w, t_cs, t_cs2)
                tok = mm(bank[0:4, :], CS[:, k, :], lo, False, k == 7, inc=end)
                if end:
                    done(p, tok)
            it, t, wt = tmp.get()
            a = act(t[0:4, :], bank[0:4, :], ACT.Copy, tok, wt)
            pm.free(i, a)
            yield
            ip, pb, wp = pt.get()
            for j in range(4):
                tk = tr(pb[:, 4 * j:4 * j + 4], t[0:4, j * 128:(j + 1) * 128], con("ident", 0, 4, 0, 4), a, wp, in_tok,
                        inc=j == 3)
            tmp.free(it, tk)
            pv = pb[:, 0:16].rearrange("p (j s) -> p j s", j=4)
            dst = MOD[:, l, 4 * g:4 * g + 4, :]
            bm = vec("b_mod", l * 48 + 4 * g, 4).rearrange("p (j o) -> p j o", o=1).broadcast_to((128, 4, 2))
            v1 = tt(dst, pv[:, :, 0:2], bm, ALU.add, tk)
            v2 = tt(dst, pv[:, :, 2:4], dst, ALU.add, v1)
            pt.free(ip, v2)
            mod_tok[l, g] = v2

        def mvec(l, which, s, k):
            return MOD[:, l, which * 8 + k, s:s + 1]

        def mod_scale(l, slot, which, gi, plus):
            toks = []
            for s in range(2):
                toks.append(stt(MA[:, l, slot, s, :], MOD[:, l, which * 8:which * 8 + 8, s], plus,
                                vec("norm_g", (l * 4 + gi) * 8, 8), ALU.add, ALU.mult,
                                [mod_tok[l, 2 * which], mod_tok[l, 2 * which + 1]], in_tok))
            return toks

        def Hx(k, n=512):
            return Hh[:, k * 512:k * 512 + n], Hl[:, k * 512:k * 512 + n]

        xt = [[x_tok] for _ in range(8)]
        hfree = {"t": []}

        def x_stat(segs, then):
            n = 256 * segs
            stat = Stat(n)
            for k in range(8):
                stat.square(X[:, 0:segs, k, :], xt[k])
            ir, r, t1, t0 = rstd(stat.bank, n, stat.tok, "eps6")
            stat.free(t0)
            preload(then)
            return ir, r, t1

        def modulated(l, slot, shift, sctoks, segs, rs):
            ir, r, t1 = rs
            toks, last = [], []
            sh_t = [mod_tok[l, 2 * shift], mod_tok[l, 2 * shift + 1]]
            for k in range(8):
                i, t, w = tmp.get()
                tk, rd = [], []
                for s in range(segs):
                    sl = slice(s * 256, (s + 1) * 256)
                    a = stt(t[:, sl], X[:, s, k, :], MA[:, l, slot, s, k:k + 1], r[:, sl], ALU.mult, ALU.mult,
                            t1, w, sctoks, xt[k])
                    hi, lo = Hh[:, k * 512 + s * 256:k * 512 + (s + 1) * 256], Hl[:, k * 512 + s * 256:k * 512 + (s + 1) * 256]
                    b = act(hi, t[:, sl], ACT.Identity, a, hfree["t"], sh_t, bias=mvec(l, shift, s, k))
                    c_ = stt(lo, t[:, sl], mvec(l, shift, s, k), f32(hi), ALU.add, ALU.subtract, a, b, hfree["t"])
                    tk += [b, c_]
                    last = [a]
                tmp.free(i, tk)
                toks.append(tk)
            tmp.free(ir, last)
            return toks

        def residual(l, slot, sctoks, stat, ytoks, segs):
            n = 256 * segs
            ir, r, t1, t0 = rstd(stat.bank, n, stat.tok, "eps6")
            stat.free(t0)
            for k in range(8):
                i, t, w = tmp.get()
                last = []
                for s in range(segs):
                    sl = slice(s * 256, (s + 1) * 256)
                    a = stt(t[:, sl], Y[:, k * 512 + s * 256:k * 512 + (s + 1) * 256], MA[:, l, slot, s, k:k + 1], r[:, sl],
                            ALU.mult, ALU.mult, t1, w, sctoks, ytoks[k])
                    last.append(a)
                xs = X[:, 0:segs, k, :]
                xt[k] = [tt(xs, xs, t[:, 0:n].rearrange("p (s t) -> p s t", s=segs), ALU.add, last, xt[k],
                            q=G if k % 2 else V)]
                tmp.free(i, xt[k])
            tmp.free(ir, last)

        yfree = {"t": []}

        def swiglu(l, parts, htoks, segs):
            n = 256 * segs
            cap = 4096 // n
            HIh, HIl = arena_open([(f"hid_h{l}", [128, 4096], F32R), (f"hid_l{l}", [128, 4096], F32R)])
            hidfree = list(arena_free["t"])
            ytoks = [None] * 8
            stat = None
            for pi, cnt in enumerate(parts):
                assert cnt <= cap
                gt = []
                tiles = lin_run(2 * cnt, 4, 8, lambda k: Hx(k, n)[0], lambda k: Hx(k, n)[1], n, lambda k: htoks[k])
                for j in range(cnt):
                    i1, b1, t1 = next(tiles)
                    i3, b3, t3 = next(tiles)
                    it, s1, w = tmp.get()
                    a = act(s1[:, 0:n], b1, ACT.Silu, t1, w)
                    pm.free(i1, a)
                    b = tt(s1[:, 0:n], b3, s1[:, 0:n], ALU.mult, a, t3)
                    pm.free(i3, b)
                    tk = split(HIh[:, j * n:(j + 1) * n], HIl[:, j * n:(j + 1) * n], s1[:, 0:n], b, hidfree)
                    tmp.free(it, tk)
                    gt.append(tk)
                hfree["t"] = [t3]
                final = pi == len(parts) - 1
                if final:
                    stat = Stat(n, adds=True)
                for m, (i, bk, t) in enumerate(lin_run(8, 4, cnt, lambda k: HIh[:, k * n:(k + 1) * n],
                                                       lambda k: HIl[:, k * n:(k + 1) * n], n, lambda k: gt[k])):
                    y = Y[:, m * 512:m * 512 + n]
                    if pi == 0:
                        ytoks[m] = act(y, bk, ACT.Copy, t, yfree["t"])
                    else:
                        ytoks[m] = tt(y, bk, y, ALU.add, t, ytoks[m])
                    pm.free(i, ytoks[m])
                    if final:
                        stat.square(y, ytoks[m])
                hidfree = [t]
            arena_free["t"] = [t]
            return stat, ytoks

        arena_free = {"t": []}

        dma_pieces()
        rs = x_stat(2, ACT.Sigmoid)
        for g in range(4):
            pipe.run(mod_group(0, g))
        pipe.drain()
        sc = mod_scale(0, 0, 1, 0, 1.0)
        htoks = modulated(0, 0, 0, sc, 2, rs)

        U, DG = arena_open([("U", [128, 8, 2, 286], F32), ("DG", [128, 3, 8, 128], F32)])
        t_pad = [G(lambda e: e.memset(U[:, :, :, 0:PAD], 0.0)), G(lambda e: e.memset(U[:, :, :, PAD + T:], 0.0)),
                 G(lambda e: e.memset(cbb[:, :, :], 0.0))]
        cb_zero = t_pad[2]
        utoks = {}

        taps = [(k, i) for k in range(6) for i in range(CONVW)]
        vt = [None] * 8

        def conv_taps(n):
            for _ in range(n):
                if not taps or taps[0][0] not in utoks:
                    return
                k, i = taps.pop(0)
                y = Y[:, k * 512:(k + 1) * 512].rearrange("p (s t) -> p s t", s=2)
                u = U[:, k, :, i:i + T]
                w = vec("conv_w_dw", i * 8 + k)
                if i == 0:
                    vt[k] = ts(y, u, w, vec("conv_b_dw", k), ALU.mult, ALU.add, utoks[k], t_pad)
                else:
                    vt[k] = stt(y, u, w, y, ALU.mult, ALU.add, vt[k])

        dgr = Ring([DG[:, i, :, :] for i in range(3)])

        def conv_diag(k, i0):
            n = min(8, CONVW - i0)
            i, dg, w = dgr.get()
            idn = con("ident").rearrange("p (o c) -> p o c", o=1).broadcast_to((128, n, 128))
            wv = VEC[:, voff["conv_w_dw"] + i0 * 8 + k:voff["conv_w_dw"] + (i0 + n - 1) * 8 + k + 1:8]
            wv = wv.rearrange("p (i o) -> p i o", o=1).broadcast_to((128, n, 128))
            return i, dg, n, tt(dg[:, 0:n, :], idn, wv, ALU.mult, w, in_tok, q=G)

        diag = [(k, i0) for k in (6, 7) for i0 in range(0, CONVW, 8)]
        ready = [conv_diag(*diag.pop(0)) for _ in range(3)]
        hook["f"] = lambda: conv_taps(5)
        lo_queue["f"] = lambda p: V
        tiles = lin_run(16, 4, 8, lambda k: Hx(k)[0], lambda k: Hx(k)[1], 512, lambda k: htoks[k])
        for j in range(8):
            ig, bg, tg = next(tiles)
            ia, ba, ta = next(tiles)
            i, t, w = tmp.get()
            a = act(t, bg, ACT.Sigmoid, tg, w, bias=vec("conv_b_pw1", 8 + j))
            pm.free(ig, a)
            b = stt(U[:, j, :, PAD:PAD + T], ba.rearrange("p (s t) -> p s t", s=2), vec("conv_b_pw1", j),
                    t.rearrange("p (s t) -> p s t", s=2), ALU.add, ALU.mult, a, ta, t_pad)
            pm.free(ia, b)
            tmp.free(i, b)
            utoks[j] = b
        hfree["t"] = [ta]

        hook["f"] = lambda: conv_taps(1)
        lo_queue["f"] = lambda p: G if p % 2 else V
        todo = [(0, g) for g in range(4, 12)] + [(1, g) for g in range(4)]
        conv_taps(60)
        for k in (6, 7):
            ib, bk, w = pm.get()
            for i0 in range(0, CONVW, 8):
                i, dg, n, tk = ready.pop(0)
                for q in range(n):
                    t0 = mm(bk.rearrange("p (s t) -> p s t", s=2), dg[:, q, :], U[:, k, :, i0 + q:i0 + q + T],
                            i0 + q == 0, i0 + q == CONVW - 1, tk, utoks[k], t_pad, w, inc=q == n - 1)
                dgr.free(i, t0)
                if diag:
                    ready.append(conv_diag(*diag.pop(0)))
            vt[k] = act(Y[:, k * 512:(k + 1) * 512], bk, ACT.Identity, t0, in_tok, bias=vec("conv_b_dw", k))
            pm.free(ib, vt[k])
        while todo:
            pipe.run(mod_group(*todo.pop(0)))
        pipe.drain()
        hook["f"] = lambda: None
        conv_taps(1000)
        stat = Stat(512)
        for k in (6, 7, 0, 1, 2, 3, 4, 5):
            stat.add(Y[:, k * 512:(k + 1) * 512], vt[k])
        lo_queue["f"] = lambda p: V
        arena_free["t"] = list(vt)

        def center(stat, n, toks, stride):
            s2 = Stat(n, ring=pt)
            out_ = []
            for k in range(8):
                y = Y[:, k * stride:k * stride + n]
                a = tt(y, y, stat.bank, ALU.subtract, toks[k], stat.tok)
                s2.square(y, a)
                out_.append(a)
            stat.free(out_[-1])
            return s2, out_

        s2, ct = center(stat, 512, vt, 512)
        ir, r, t1, t0 = rstd(s2.bank, 512, s2.tok, "eps6")
        s2.free(t0)
        preload(ACT.Silu)
        htoks = []
        for k in range(8):
            i, t, w = tmp.get()
            a = tt(t, Y[:, k * 512:(k + 1) * 512], r, ALU.mult, t1, w, ct[k])
            b = act(t, t, ACT.Silu, a, in_tok, bias=vec("conv_ln_b", k), scale=vec("conv_ln_g", k))
            tk = split(Hx(k)[0], Hx(k)[1], t, b, hfree["t"])
            tmp.free(i, tk)
            htoks.append(tk)
        tmp.free(ir, a)
        yread = [a, s2.tok]

        stat = Stat(512, adds=True)
        ytoks = []
        for m, (i, bk, t) in enumerate(lin_run(8, 4, 8, lambda k: Hx(k)[0], lambda k: Hx(k)[1], 512, lambda k: htoks[k])):
            a = act(Y[:, m * 512:(m + 1) * 512], bk, ACT.Identity, t, yread, bias=vec("conv_b_pw2", m))
            pm.free(i, a)
            stat.square(Y[:, m * 512:(m + 1) * 512], a)
            ytoks.append(a)
        hfree["t"] = [t]
        sc = mod_scale(0, 1, 2, 1, 0.0)
        residual(0, 1, sc, stat, ytoks, 2)

        def ffn_first(l, parts, segs):
            yfree["t"] = [xt[k] for k in range(8)]
            sc = mod_scale(l, 2, 4, 2, 1.0)
            ht = modulated(l, 2, 3, sc, segs, x_stat(segs, ACT.Silu))
            stat, yt = swiglu(l, parts, ht, segs)
            sc = mod_scale(l, 3, 5, 3, 0.0)
            residual(l, 3, sc, stat, yt, segs)

        ffn_first(0, FFN0, 2)

        sc = mod_scale(1, 0, 1, 0, 1.0)
        htoks = modulated(1, 0, 0, sc, 2, x_stat(2, ACT.Sqrt))
        afree = list(arena_free["t"])
        Q1, K1, V1 = arena_open([("Q1", [128, 8, T], F32), ("K1", [128, 4, 512], F32), ("V1", [128, 4, 4, 128], F32)])

        def headed(got, n, gain, finish):
            i, bk, t = got
            it, r_, w = tmp.get()
            src = r_[:, 0:n]
            a = act(src, bk, ACT.Copy, t, w)
            iq, sq, wq = tmp.get()
            b = act(sq[:, 0:n], bk, ACT.Square, t, wq)
            pm.free(i, a, b)
            yield
            s_ = Stat(n, "mean64", 1)
            tmp.free(iq, s_.add(sq[:, 0:n], b))
            ir, r, t1, t0 = rstd(s_.bank, n, s_.tok, "eps6")
            s_.free(t0)
            a = stt(src, src, gain, r, ALU.mult, ALU.mult, t1, a)
            tmp.free(ir, a)
            yield
            yield from finish(it, src, a)

        def rope(dst, src, tok, rot, cs, sn, *after):
            i, b, w = pt.get()
            t0 = mm(b[:, 0:T], con(rot), src, True, True, tok, w, in_tok, inc=True)
            it, t, wt = tmp.get()
            t1 = tt(t[:, 0:T], b[:, 0:T], con(sn), ALU.mult, t0, wt)
            pt.free(i, t1)
            t2 = tt(dst, src, con(cs), ALU.mult, tok, t0, *after)
            t3 = tt(dst, dst, t[:, 0:T], ALU.add, t1, t2)
            tmp.free(it, t3)
            return t3

        ktok = [None] * 4

        def k_finish(m):
            def f(it, kr, a):
                a = rope(kr[:, 0:T], kr[:, 0:T], a, "rot1", "cos1", "sin1")
                yield
                for g in range(2):
                    i, b, w = pt.get()
                    t0 = mm(b, con(f"dup{g}"), kr, True, True, a, w, inc=True)
                    ktok[2 * m + g] = act(K1[:, 2 * m + g, :], b, ACT.Copy, t0, afree)
                    pt.free(i, ktok[2 * m + g])
                tmp.free(it, t0)
            return f

        for m, got in enumerate(lins(2, 8, lambda k: Hx(k)[0], lambda k: Hx(k)[1], 512, lambda k: htoks[k])):
            pipe.run(headed(got, 512, vec("attn_k_g"), k_finish(m)))
        got, t = lin_tok("w", 256, 256, lambda k: Hx(k)[0], lambda k: Hx(k)[1], 4, lambda k: htoks[k])
        vtok = []
        for s, (i, bk) in enumerate(got):
            b3 = bk.rearrange("p (g d) -> p g d", g=4)
            a = act(V1[:, s, :, 0:64], b3, ACT.Copy, t, afree)
            b = vcopy(V1[:, s, :, 64:128], b3, t, a, afree)
            pm.free(i, a, b)
            vtok.append([a, b])

        pT1 = Ring([Y[:, 2048 + 1024 * i:3072 + 1024 * i].rearrange("p (s q) -> p s q", s=4) for i in range(2)])
        pT1.rel = [[xt[k] for k in range(8)] for _ in range(2)]
        smr = Ring([SM[:, 16 + 12 * i:28 + 12 * i] for i in range(8)])
        otok = {}
        qtok = [None] * 8

        def q_finish(j):
            def f(it, qr, a):
                qtok[j] = rope(Q1[:, j, :], qr, a, "rot1", "cos1", "sin1", afree)
                tmp.free(it, qtok[j])
                yield from ()
            return f

        SC = HD ** -0.5

        def a1_item(h, qt):
            i, b, w = pm.get()
            o = (h % 2) * 64
            t0 = mm(b, Q1[o:o + 64, h // 2, qt * 128:(qt + 1) * 128], K1[o:o + 64, h // 4, :], True, True,
                    qtok[h // 2], ktok[h // 4], w, inc=True)
            im, sm, wm = smr.get()
            t1 = rmax(sm[:, 0:1], b, t0, wm)
            t2 = ts(sm[:, 1:2], sm[:, 0:1], -SC, None, ALU.mult, None, t1)
            ip, p, wp = tmp.get()
            t3 = act(p, b, ACT.Exp, t2, wp, bias=sm[:, 1:2], scale=SC, accum=sm[:, 2:3])
            pm.free(i, t3)
            t4 = recip(sm[:, 3:4], sm[:, 2:3], t3)
            t5 = ts(p, p, sm[:, 3:4], None, ALU.mult, None, t4)
            smr.free(im, t5)
            yield
            yield
            if qt == 0:
                cur[h] = [pT1.get(), []]
            (it, pT, wT), done_ = cur[h]
            i, b, w = pt.get()
            for s in range(4):
                t0 = tr(b[:, s * 128:(s + 1) * 128], p[:, s * 128:(s + 1) * 128], con("ident"), t5, w, inc=s == 3)
            tmp.free(ip, t0)
            done_.append(act(pT[:, :, qt * 128:(qt + 1) * 128], b.rearrange("p (s q) -> p s q", s=4), ACT.Copy, t0, wT))
            pt.free(i, done_[-1])
            yield
            if qt == 1:
                o = (h % 2) * 64
                i, b, w = pm.get()
                for s in range(4):
                    t0 = mm(b[:, 0:T], V1[:, s, h // 4, :], pT[:, s, :], s == 0, s == 3, done_, vtok[s], w, inc=s == 3)
                pT1.free(it, t0)
                a = act(Y[o:o + 64, (h // 2) * T:(h // 2 + 1) * T], b[o:o + 64, 0:T], ACT.Copy, t0, [xt[k] for k in range(8)])
                pm.free(i, a)
                otok.setdefault(h // 2, []).append(a)

        cur = {}
        for j in range(8):
            got = lin(8, lambda k: Hx(k, T)[0], lambda k: Hx(k, T)[1], T, lambda k: htoks[k])
            tq = got[2]
            pipe.run(headed(got, T, vec("attn_q_g"), q_finish(j)))
        pipe.drain()
        preload(ACT.Exp)
        todo = [(1, g) for g in range(4, 12)]
        lo_queue["f"] = lambda p: G if p % 2 else V
        for h in range(16):
            for qt in range(2):
                pipe.run(a1_item(h, qt))
            if h % 2 and todo:
                pipe.run(mod_group(*todo.pop(0)))
        pipe.drain()
        lo_queue["f"] = lambda p: V
        hfree["t"] = [tq]
        arena_free["t"] = [otok[7], (P.sem, P.n)]
        otk = []
        for j in range(8):
            otk.append(split(Hx(j, T)[0], Hx(j, T)[1], Y[:, j * T:(j + 1) * T], otok[j], hfree["t"]))
        stat = Stat(T, adds=True)
        ytoks = []
        for m, (i, bk, t) in enumerate(lin_run(8, 4, 8, lambda k: Hx(k, T)[0], lambda k: Hx(k, T)[1], T, lambda k: otk[k])):
            a = act(Y[:, m * 512:m * 512 + T], bk, ACT.Copy, t, otk, otok[7], (P.sem, P.n))
            pm.free(i, a)
            stat.square(Y[:, m * 512:m * 512 + T], a)
            ytoks.append(a)
        hfree["t"] = [t]
        sc = mod_scale(1, 1, 2, 1, 0.0)
        residual(1, 1, sc, stat, ytoks, 1)
        ffn_first(1, FFN1, 1)

        def xh(k):
            return Hh[:, k * T:(k + 1) * T]

        def xl(k):
            return Hl[:, k * T:(k + 1) * T]

        xtoks = []
        for k in range(8):
            xtoks.append(split(xh(k), xl(k), X[:, 0, k, :], xt[k], hfree["t"]))
        GT = [X[:, 1, k, :] for k in range(8)] + [Y[:, 2048 + k * T:2048 + (k + 1) * T] for k in range(8)]
        xt = [[xt[k]] for k in range(8)]
        y2free = [xt[k] for k in range(8)]

        def layer_norm(toks, stat, gname, bname, l, hwait, then):
            s2, ct = center(stat, T, toks, T)
            ir, r, t1, t0 = rstd(s2.bank, T, s2.tok, "eps5")
            s2.free(t0)
            preload(then)
            ht = []
            for k in range(8):
                i, t, w = tmp.get()
                g, b = vec(gname, l * 8 + k), vec(bname, l * 8 + k)
                a = stt(t[:, 0:T], Y[:, k * T:(k + 1) * T], g, r, ALU.mult, ALU.mult, t1, w, ct[k])
                c1 = act(xh(k), t[:, 0:T], ACT.Identity, a, hwait, bias=b)
                c2 = stt(xl(k), t[:, 0:T], b, f32(xh(k)), ALU.add, ALU.subtract, a, c1, hwait)
                c3 = act(X[:, 0, k, :], t[:, 0:T], ACT.Identity, a, xt[k], bias=b)
                xt[k] = [c3]
                tmp.free(i, c1, c2, c3)
                ht.append([c1, c2])
            tmp.free(ir, a)
            return ht, [a, s2.tok]

        gate_free = {"t": []}
        yrest = {"t": []}
        for l in range(2):
            af = [arena_free["t"]]
            DQ, DK, DV, NQ, KD, VD, YCh, YCl = arena_open([
                (f"DQ{l}", [128, 4, T], F32), (f"DK{l}", [128, 4, T], F32), (f"DV{l}", [128, 2, 512], F32),
                (f"NQ{l}", [128, 4, T], F32), (f"KD{l}", [128, 2, 2, T], F32), (f"VD{l}", [128, 2, 2, 2, 128], F32),
                (f"YCh{l}", [128, 4, T], F32R), (f"YCl{l}", [128, 4, T], F32R)])

            lv = SM[:, 112:116]
            dl = vec("diff_lambda_2", 4 * l, 4)
            t0 = tt(lv[:, 0:1], dl[:, 0:1], dl[:, 1:2], ALU.mult, in_tok)
            t1 = tt(lv[:, 1:2], dl[:, 2:3], dl[:, 3:4], ALU.mult, in_tok)
            i, b, w = pst.get()
            t2 = mm(b[:, 0:2], con("ones"), lv[:, 0:2], True, True, t0, t1, w, inc=True)
            lam = SM[:, 116:120]
            t3 = act(lam[:, 0:2], b[:, 0:2], ACT.Exp, t2)
            pst.free(i, t3)
            t4 = tt(lam[:, 2:3], lam[:, 0:1], lam[:, 1:2], ALU.subtract, t3)
            lam_t = ts(lam[:, 3:4], lam[:, 2:3], LAM_INIT[l], None, ALU.add, None, t4)
            subln = SM[:, 120:121]
            sub_t = ts(subln, vec("diff_subln_2", l), 1.0 - LAM_INIT[l], None, ALU.mult, None, in_tok)

            def xlin():
                return lin(8, xh, xl, T, lambda k: xtoks[k])

            def roped(dst, got, *after):
                i, bk, t = got
                it, r_, w = tmp.get()
                a = act(r_[:, 0:T], bk, ACT.Copy, t, w)
                pm.free(i, a)
                yield
                tk = rope(dst, r_[:, 0:T], a, "rot2", "cos2", "sin2", *after)
                tmp.free(it, tk)
                return tk

            dkt, dqt = [], []

            def d_tile(dst, got, toks):
                toks.append((yield from roped(dst, got, af)))

            tiles = lin_run(8, 4, 8, xh, xl, T, lambda k: xtoks[k])
            for m in range(4):
                pipe.run(d_tile(DK[:, m, :], next(tiles), dkt))
                pipe.run(d_tile(DQ[:, m, :], next(tiles), dqt))
            preload(ACT.Exp)
            got, t = lin_tok("w", 512, 512, xh, xl, 2, lambda k: xtoks[k])
            dvt = []
            for s, (i, bk) in enumerate(got):
                a = act(DV[:, s, :], bk, ACT.Copy, t, af)
                pm.free(i, a)
                dvt.append(a)

            kb, kdt, vdt, gat, nqt, hT, cmpt = {}, [], [], [], [], {}, {}
            gate = SM[:, 128:176].rearrange("p (s c) -> p s c", s=2)

            def compress_blocks(kv, src, tok):
                i, kbt, w = tmp.get()
                kbv = kbt[:, 0:480].rearrange("p (l g n) -> p l g n", l=16, g=2)
                tks = []
                for par in range(2):
                    for g in range(2):
                        for half in range(2):
                            sv = src[g * 64:(g + 1) * 64, half * 16:half * 16 + 240].rearrange("p (n l) -> p l n", l=16)
                            sv = sv[:, par:16:2, :]
                            dv = kbv[par * 64:(par + 1) * 64, half * 8:half * 8 + 8, g, :]
                            tks.append(vcopy(dv, sv, tok, w))
                pos = vec("nsa_cmp_pos_2", (l * 2 + kv) * 16, 16).rearrange("p (l o) -> p l o", o=1).broadcast_to((128, 16, 30))
                kb3 = kbt[:, 0:480].rearrange("p (l m) -> p l m", l=16)
                kb[kv] = (i, kb3, tt(kb3, kb3, pos, ALU.add, tks))
                return tks

            def z_kc():
                got = xlin()
                i, t, w = tmp.get()
                tok = yield from roped(t[:, 0:T], got, w)
                tmp.free(i, compress_blocks(0, t[:, 0:T], tok))

            def z_kdup(br):
                got = xlin()
                i, r_, w = tmp.get()
                a = yield from roped(r_[:, 0:T], got, w)
                yield
                for g in range(2):
                    ib, b, wb = pt.get()
                    t0 = mm(b[:, 0:T], con(f"dup{g}"), r_[:, 0:T], True, True, a, wb, inc=True)
                    kdt.append(act(KD[:, br, g, :], b[:, 0:T], ACT.Copy, t0, af))
                    pt.free(ib, kdt[-1])
                tmp.free(i, t0)

            def z_vc():
                i, bk, t = xlin()
                it, v, w = tmp.get()
                tok = act(v[:, 0:T], bk, ACT.Copy, t, w)
                pm.free(i, tok)
                tmp.free(it, compress_blocks(1, v[:, 0:T], tok))
                yield from ()

            def z_values():
                got, t = lin_tok("vvg", 512, 280, xh, xl, 2, lambda k: xtoks[k])
                for s, (i, bk) in enumerate(got):
                    b4 = bk[:, 0:256].rearrange("p (b g d) -> p b g d", b=2, g=2)
                    a = act(VD[:, s, :, :, 0:64], b4, ACT.Copy, t, af)
                    d_ = act(gate[:, s, :], bk[:, 256:280], ACT.Tanh, t, gate_free["t"], scale=0.5)
                    c_ = vcopy(VD[:, s, :, :, 64:128], b4, t, d_, af)
                    pm.free(i, a, c_)
                    vdt.append([a, c_])
                    gat.append(ts(gate[:, s, :], gate[:, s, :], 0.5, 0.5, ALU.mult, ALU.add, d_))
                yield from ()

            def z_nq(m):
                nqt.append((yield from roped(NQ[:, m, :], xlin(), af)))

            def z_hidden(kv):
                ib, b, w = pst.get()
                i, kb3, tk = kb[kv]
                for half in range(2):
                    w1, wt_, p = take_raw(8)
                    for k in range(8):
                        t0 = mm(b[0:30, 0:128], kb3[:, half * 8 + k, :], w1[:, k * 128:(k + 1) * 128], half == 0 and k == 0,
                                half == 1 and k == 7, tk, wt_, w, inc=k == 7)
                    raw_rel[p] = [t0]
                    dma_pieces()
                tmp.free(i, t0)
                ig_, gl, wg = tmp.get()
                a = act(gl[0:30, 0:128], b[0:30, 0:128], ACT.Gelu, t0, wg)
                pst.free(ib, a)
                yield
                ib, b, w = pst.get()
                t1 = tr(b[:, 256:286], gl[0:30, 0:128], con("ident", 0, 30, 0, 30), a, w, inc=True)
                a2 = act(gl[:, 128:158], b[:, 256:286], ACT.Copy, t1)
                pst.free(ib, a2)
                yield
                w2 = vec("nsa_phi_w2_2", (l * 2 + kv) * 128, 128)
                ib, b, w = pst.get()
                if kv == 0:
                    t0 = mm(b[:, 0:30], w2, gl[:, 128:158], True, True, a2, w, inc=True)
                    cmpt["k"] = SM[:, 176:206]
                    cmpt["kt"] = a = act(cmpt["k"], b[:, 0:30], ACT.Copy, t0, af)
                else:
                    for g in range(2):
                        t0 = mm(b[0:15, g * 128:g * 128 + 128], gl[:, 128 + g * 15:128 + (g + 1) * 15], w2, True, True, a2, w,
                                inc=True)
                    cmpt["v"] = [MOD[0:15].rearrange("p a b c -> p (a b c)")[:, 0:128], MA[0:15].rearrange("p a b c d -> p (a b c d)")[:, 0:128]]
                    cmpt["vt"] = [act(cmpt["v"][g], b[0:15, g * 128:g * 128 + 128], ACT.Copy, t0, af) for g in range(2)]
                    a = cmpt["vt"][-1]
                pst.free(ib, a)
                tmp.free(ig_, a)

            YA = lambda j: (Hh[:, 2048 + j * T:2048 + (j + 1) * T], Hl[:, 2048 + j * T:2048 + (j + 1) * T])
            yat = [None] * 12
            ga_t = [None] * 16

            def conv3(src, dst, w, bias, tok, wdst):
                if bias is None:
                    a = ts(dst, src[:, 0:T], w[0], None, ALU.mult, None, tok, wdst)
                else:
                    a = ts(dst, src[:, 0:T], w[0], bias, ALU.mult, ALU.add, tok, wdst)
                for i in (1, 2):
                    a = stt(dst, src[:, i:i + T], w[i], dst, ALU.mult, ALU.add, a)
                return a

            def fill_a(j):
                iv, bv, tv = xlin()
                ic, bc, tc = xlin()
                ix, bx, tx = xlin()
                i, t, w = tmp.get()
                a = act(t[:, 0:T], bv, ACT.Copy, tv, w)
                pm.free(iv, a)
                icb, cb, wc = cbr.get()
                b = tt(cb[:, 2:2 + T], bc, t[:, 0:T], ALU.mult, a, tc, wc, cb_zero)
                pm.free(ic, b)
                c_ = conv3(cb, t[:, 256:512], [vec("conv_a_w_2", l * 12 + q * 4 + j) for q in range(3)], None, b, w)
                cbr.free(icb, c_)
                d_ = tt(t[:, 0:T], bx, t[:, 256:512], ALU.mult, c_, tx)
                pm.free(ix, d_)
                yat[j] = split(*YA(j), t[:, 0:T], d_, y2read["t"])
                tmp.free(i, yat[j])
                yield from ()

            def fill_g(m):
                i, bk, t = xlin()
                ga_t[m] = act(GT[m], bk, ACT.Tanh, t, y2free, scale=0.5)
                pm.free(i, ga_t[m])
                yield from ()

            if l == 0:
                y2read = {"t": [hfree["t"]]}
            early = [(z_kc,), (z_kdup, 0), (z_kdup, 1), (z_vc,), (z_values,), (z_nq, 0), (z_nq, 1), (z_nq, 2), (z_nq, 3),
                     (z_hidden, 0), (z_hidden, 1)]
            late = [(fill_a, j) for j in range(4)] + [(fill_g, m) for m in range(16)]

            def fill(what, n=1):
                for _ in range(n):
                    if what:
                        f, *a = what.pop(0)
                        pipe.run(f(*a))

            def masked(b, n, qt, p, mx, tok, wait):
                mask = con("causal", 128, 256) if qt == 0 else con("causal")
                t1 = V(lambda e: e.tensor_tensor_reduce(p, b, mask, 1.0, 0.0, ALU.add, ALU.max, mx[:, 0:1]), tok, wait, in_tok)
                t2 = ts(mx[:, 1:2], mx[:, 0:1], -SC, None, ALU.mult, None, t1)
                return t1, act(p, p, ACT.Exp, t2, bias=mx[:, 1:2], scale=SC, accum=mx[:, 2:3])

            PC = Y[0:15, 0:2048].rearrange("p (h q) -> p h q", h=8)
            pct = []
            def compressed(qt):
                pair = [pm.get() for _ in range(2)]
                for h in range(8):
                    o = (h % 2) * 64
                    g = h // 4
                    _, b, w = pair[h % 2]
                    t0 = mm(b[:, (h // 2) * 15:(h // 2) * 15 + 15], NQ[o:o + 64, h // 2, qt * 128:(qt + 1) * 128],
                            cmpt["k"][o:o + 64, g * 15:(g + 1) * 15], True, True, nqt, cmpt["kt"], w, inc=h == 7)
                ic, t, wc = tmp.get()
                im, sm, wm = smr.get()
                ir_, rr, wr_ = tmp.get()
                v3 = lambda ap: ap.rearrange("p (h n) -> p h n", h=8)
                s3 = v3(t[:, 0:120])
                bro = lambda ap: ap.rearrange("p (o n) -> p o n", o=1).broadcast_to((128, 8, 15))
                bro4 = lambda ap: ap.rearrange("p (o n) -> p o n", o=1).broadcast_to((128, 4, 15))
                col = lambda ap: ap.rearrange("p (h o) -> p h o", o=1).broadcast_to((128, 8, 15))
                for par, (i, b, _) in enumerate(pair):
                    a = tt(s3[:, par:8:2, :], b[:, 0:60].rearrange("p (h n) -> p h n", h=4),
                           bro4(con("cmpadd", qt * 15, qt * 15 + 15)), ALU.add, t0, wc, in_tok)
                    pm.free(i, a)
                a = V(lambda e, s3=s3, rr=rr: e.tensor_reduce(rr[:, 0:8], s3, AX, ALU.max), a, wr_)
                a = tt(s3, s3, col(rr[:, 0:8]), ALU.subtract, a)
                a = act(t[:, 0:120], t[:, 0:120], ACT.Exp, a, scale=SC)
                a = V(lambda e, s3=s3, rr=rr: e.tensor_reduce(rr[:, 8:16], s3, AX, ALU.add), a)
                a = recip(rr[:, 16:24], rr[:, 8:16], a)
                a = tt(rr[:, 24:32], rr[:, 16:24], gate[:, qt, 0:24:3], ALU.mult, a, gat[qt])
                b2 = tt(s3, s3, bro(con("cmpok", qt * 15, qt * 15 + 15)), ALU.mult, a)
                a = tt(s3, s3, col(rr[:, 24:32]), ALU.mult, a, b2)
                tmp.free(ir_, a)
                smr.free(im)
                yield
                cpt = []
                for hh in range(2):
                    i, b, w = pt.get()
                    for h in range(4):
                        t0 = tr(b[0:15, h * 128:(h + 1) * 128], s3[:, hh * 4 + h, :], con("ident"), a, w, inc=h == 3)
                    c_ = act(PC[:, hh * 4:hh * 4 + 4, qt * 128:(qt + 1) * 128],
                             b[0:15, :].rearrange("p (h q) -> p h q", h=4), ACT.Copy, t0, y2free, yrest["t"])
                    pt.free(i, c_)
                    pct.append(c_)
                tmp.free(ic, t0)

            def d_item(h, qt):
                n = 128 * (qt + 1)
                pair = [pm.get() for _ in range(2)]
                im, sm, wm = smr.get()
                ip, p, wp = tmp.get()
                sc_ = []
                for m, (i, b, w) in enumerate(pair):
                    o = m * 64
                    sc_.append(mm(b[:, 0:n], DQ[o:o + 64, h, qt * 128:(qt + 1) * 128], DK[o:o + 64, h, 0:n],
                                  True, True, dqt[h], dkt[h], w, inc=True))
                d_done.setdefault(h, []).extend(sc_)
                e = []
                for m, (i, b, w) in enumerate(pair):
                    t1, t2 = masked(b[:, 0:n], n, qt, p[:, m * 256:m * 256 + n], sm[:, 4 * m:4 * m + 4], sc_[m], [wp, wm])
                    e.append(t2)
                    pm.free(i, t1)
                a = recip(sm[:, 8:10], sm[:, 2:7:4], e)
                a2 = tt(sm[:, 10:11], sm[:, 9:10], lam[:, 3:4], ALU.mult, a, lam_t)
                a3 = ts(p[:, 256:256 + n], p[:, 256:256 + n], sm[:, 10:11], None, ALU.mult, None, a2)
                a4 = stt(p[:, 0:n], p[:, 0:n], sm[:, 8:9], p[:, 256:256 + n], ALU.mult, ALU.subtract, a3)
                smr.free(im, a4)
                yield
                if qt == 0:
                    cur[h] = [tmp.get(), []]
                (ia, aT, wa), at_ = cur[h]
                i, b, w = pt.get()
                for s in range(qt + 1):
                    t0 = tr(b[:, s * 128:(s + 1) * 128], p[:, s * 128:(s + 1) * 128], con("ident"), a4, w, inc=s == qt)
                tmp.free(ip, t0)
                a3 = aT.rearrange("p (s q) -> p s q", s=2)
                at_.append(act(a3[:, 0:qt + 1, qt * 128:(qt + 1) * 128],
                               b[:, 0:128 * (qt + 1)].rearrange("p (s q) -> p s q", q=128), ACT.Copy, t0, wa))
                pt.free(i, at_[-1])
                yield
                if qt == 1:
                    i, b, w = pm.get()
                    mm(b[:, 0:T], DV[:, 0, h * 128:(h + 1) * 128], a3[:, 0, :], True, False, at_, dvt, w)
                    t0 = mm(b[:, 128:T], DV[:, 1, h * 128:(h + 1) * 128], a3[:, 1, 128:T], False, True, inc=True)
                    tmp.free(ia, t0)
                    o_ = DQ[:, h, :]
                    a = act(o_, b[:, 0:T], ACT.Copy, t0, d_done[h])
                    pm.free(i, a)
                    v = DK[:, h, :]
                    i, t, w = tmp.get()
                    a2 = act(t[:, 0:T], o_, ACT.Square, a, w)
                    yield
                    s_ = Stat(T, "mean128", 1)
                    tmp.free(i, s_.add(t[:, 0:T], a2))
                    a3 = act(v, s_.bank, ACT.Copy, s_.tok, d_done[h])
                    s_.free(a3)
                    d_out.append((h, a, a3))

            d_done, d_out = {}, []

            def d_norm():
                roots = [act(DK[:, h, :], DK[:, h, :], ACT.Sqrt, a3, in_tok, bias=con("eps5")) for h, _, a3 in d_out]
                preload(ACT.Exp)
                for (h, a, _), t0 in zip(d_out, roots):
                    o_, v = DQ[:, h, :], DK[:, h, :]
                    t1 = recip(v, v, t0)
                    c_ = stt(o_, o_, subln, v, ALU.mult, ALU.mult, t1, a, sub_t)
                    yat[4 + h] = split(*YA(4 + h), o_, c_, y2read["t"])

            yct = [[] for _ in range(4)]

            def n_item(h, qt):
                n = 128 * (qt + 1)
                o = (h % 2) * 64
                g = h // 4
                i, b, w = pm.get()
                im, sm, wm = smr.get()
                ip, p, wp = tmp.get()
                for br in range(2):
                    t0 = mm(b[:, br * 256:br * 256 + n], NQ[o:o + 64, h // 2, qt * 128:(qt + 1) * 128], KD[o:o + 64, br, g, 0:n],
                            True, True, nqt, kdt, w, inc=True)
                e, rd = [], []
                for br in range(2):
                    t1, t2 = masked(b[:, br * 256:br * 256 + n], n, qt, p[:, br * 256:br * 256 + n], sm[:, 4 * br:4 * br + 4], t0, [wp, wm])
                    e.append(t2)
                    rd.append(t1)
                pm.free(i, rd)
                a = recip(sm[:, 8:10], sm[:, 2:7:4], e)
                a = tt(sm[:, 10:12], sm[:, 8:10], gate[:, qt, 3 * h + 1:3 * h + 3], ALU.mult, a, gat[qt])
                for br in range(2):
                    c_ = ts(p[:, br * 256:br * 256 + n], p[:, br * 256:br * 256 + n], sm[:, 10 + br:11 + br], None, ALU.mult, None, a)
                smr.free(im, c_)
                yield
                yield
                if qt == 0:
                    cur[h] = [[tmp.get(), tmp.get()], []]
                nT, nt = cur[h]
                i, b, w = pt.get()
                for br in range(2):
                    for s in range(qt + 1):
                        t0 = tr(b[:, br * 256 + s * 128:br * 256 + (s + 1) * 128], p[:, br * 256 + s * 128:br * 256 + (s + 1) * 128],
                                con("ident"), c_, w, inc=br == 1 and s == qt)
                tmp.free(ip, t0)
                rd = []
                for br in range(2):
                    ia, aT, wa = nT[br]
                    a3 = aT.rearrange("p (s q) -> p s q", s=2)
                    rd.append(act(a3[:, 0:qt + 1, qt * 128:(qt + 1) * 128],
                                  b[:, br * 256:br * 256 + 128 * (qt + 1)].rearrange("p (s q) -> p s q", q=128), ACT.Copy, t0, wa))
                pt.free(i, rd)
                nt += rd
                yield
                if qt == 1:
                    i, b, w = pm.get()
                    mm(b[:, 0:T], cmpt["v"][g], PC[:, h, :], True, False, pct, cmpt["vt"], w)
                    for br in range(2):
                        a3 = nT[br][1].rearrange("p (s q) -> p s q", s=2)
                        mm(b[:, 0:T], VD[:, 0, br, g, :], a3[:, 0, :], False, False, nt, vdt)
                        t0 = mm(b[:, 128:T], VD[:, 1, br, g, :], a3[:, 1, 128:T], False, br == 1, inc=br == 1)
                    for br in range(2):
                        tmp.free(nT[br][0], t0)
                    hi, lo = YCh[o:o + 64, h // 2, :], YCl[o:o + 64, h // 2, :]
                    c1 = act(hi, b[o:o + 64, 0:T], ACT.Copy, t0, af)
                    c2 = tt(lo, b[o:o + 64, 0:T], f32(hi), ALU.subtract, t0, c1, af)
                    pm.free(i, c1, c2)
                    yct[h // 2] += [c1, c2]

            for h in range(4):
                for qt in range(2):
                    pipe.run(d_item(h, qt))
                    fill(early)
            fill(early, 100)
            pipe.drain()
            preload(ACT.Exp)
            for qt in range(2):
                pipe.run(compressed(qt))
                fill(late)
            pipe.drain()
            d_norm()
            for h in range(8):
                for qt in range(2):
                    pipe.run(n_item(h, qt))
                    if len(late) > 2:
                        fill(late)
            while pipe.tasks:
                if late:
                    fill(late)
                else:
                    pipe.step()
            gate_free = {"t": [(V.sem, V.n)]}

            zdone = [(P.sem, P.n)]
            mgt = []
            for m in range(8):
                i2, b2_, t2 = xlin()
                i, t, w = tmp.get()
                g2 = act(t[:, 256:512], b2_, ACT.Tanh, t2, w, scale=0.5)
                pm.free(i2, g2)
                acc = None
                im_, mg, wm_ = tmp.get()
                for br in range(3):
                    if br < 2:
                        ib, bb, tb = lin(4, lambda k: YA(4 * br + k)[0], lambda k: YA(4 * br + k)[1], T, lambda k: yat[4 * br + k])
                        gt_, gtk = GT[8 * br + m], ga_t[8 * br + m]
                    else:
                        ib, bb, tb = lin(4, lambda k: YCh[:, k, :], lambda k: YCl[:, k, :], T, lambda k: yct[k])
                        gt_, gtk = t[:, 256:512], g2
                    if br == 0:
                        acc = stt(mg[:, 0:T], gt_, 1.0, bb, ALU.add, ALU.mult, tb, gtk, wm_)
                        pm.free(ib, acc)
                    else:
                        a = stt(t[:, 0:T], gt_, 1.0, bb, ALU.add, ALU.mult, tb, gtk, w, acc)
                        pm.free(ib, a)
                        acc = tt(mg[:, 0:T], mg[:, 0:T], t[:, 0:T], ALU.add, acc, a)
                tmp.free(i, acc)
                mgc = act(Y[:, m * T:(m + 1) * T], mg[:, 0:T], ACT.Copy, acc, zdone, scale=0.5)
                tmp.free(im_, mgc)
                mgt.append(mgc)
            xdone = [t2]
            y2read = {"t": [(P.sem, P.n)]}
            arena_free["t"] = [(P.sem, P.n), (V.sem, V.n)]
            ot = []
            for k in range(8):
                ot.append(split(xh(k), xl(k), Y[:, k * T:(k + 1) * T], mgt[k], xdone))
            stat = Stat(T, adds=True)
            toks = []
            for m, (i, bk, t) in enumerate(lin_run(8, 4, 8, xh, xl, T, lambda k: ot[k])):
                y = Y[:, m * T:(m + 1) * T]
                a = stt(y, X[:, 0, m, :], ALPHA, bk, ALU.mult, ALU.add, t, ot, xt[m])
                pm.free(i, a)
                stat.add(y, a)
                toks.append(a)
            ht, ydone = layer_norm(toks, stat, "ln1_g_2", "ln1_b_2", l, [t], ACT.Gelu)

            HIh, HIl = arena_open([(f"fh{l}", [128, 16, T], F32R), (f"fl{l}", [128, 16, T], F32R)])
            hidfree = list(arena_free["t"])
            lo_queue["f"] = lambda p: G if p % 3 == 2 else V
            j0 = 0
            toks = [None] * 8
            for pi, cnt in enumerate(FFN1):
                gt = []
                tiles = lin_run(2 * cnt, 4, 8, xh, xl, T, lambda k: ht[k])
                for j in range(cnt):
                    jj = j0 + j
                    res = []
                    for half in range(2):
                        c_ = jj + 22 * half
                        i, bk, t = next(tiles)
                        icb, cb, wc = cbr.get()
                        a = act(cb[:, 2:2 + T], bk, ACT.Copy, t, wc, cb_zero)
                        pm.free(i, a)
                        it, tb, wt_ = tmp.get()
                        a = conv3(cb, tb[:, 0:T], [vec("ffn_conv_w_2", l * 132 + q * 44 + c_) for q in range(3)],
                                  vec("ffn_conv_b_2", l * 44 + c_), a, wt_)
                        cbr.free(icb, a)
                        res.append((it, tb, a))
                    (ia, ta_, aa), (iu, tu, au) = res
                    b = act(ta_[:, 0:T], ta_[:, 0:T], ACT.Gelu, aa)
                    c_ = tt(tu[:, 0:T], ta_[:, 0:T], tu[:, 0:T], ALU.mult, b, au)
                    tmp.free(ia, c_)
                    tk = split(HIh[:, j, :], HIl[:, j, :], tu[:, 0:T], c_, hidfree)
                    tmp.free(iu, tk)
                    gt.append(tk)
                if pi == 1:
                    stat = Stat(T, adds=True)
                for m, (i, bk, t) in enumerate(lin_run(8, 4, cnt, lambda k: HIh[:, k, :], lambda k: HIl[:, k, :], T,
                                                       lambda k: gt[k])):
                    y = Y[:, m * T:(m + 1) * T]
                    if pi == 0:
                        toks[m] = stt(y, X[:, 0, m, :], ALPHA, bk, ALU.mult, ALU.add, t, ydone, xt[m])
                    else:
                        toks[m] = tt(y, bk, y, ALU.add, t, toks[m])
                        stat.add(y, toks[m])
                    pm.free(i, toks[m])
                hidfree = [t]
                j0 += cnt
            lo_queue["f"] = lambda p: V
            arena_free["t"] = [t]
            xtoks, yd = layer_norm(toks, stat, "ln2_g_2", "ln2_b_2", l, [t], ACT.Exp)
            yrest = {"t": yd}
            y2free = [yd]

        assert st["blk"] == len(plan)
        for k in range(8):
            S.items.append((flat(xt[k]), lambda e, k=k: e.dma_start(
                out[k * 128:(k + 1) * 128, :], X[:, 0, k, :]).then_inc(s_out, 16), False))
        for cm in reversed(arena):
            cm.__exit__(None, None, None)

        block = ctx.enter_context(nc.Block())

        @block.sync
        def _(eng):
            S.play(eng)
            eng.wait_ge(s_out, 16 * 8)

        @block.scalar
        def _(eng):
            A.play(eng)

        @block.vector
        def _(eng):
            V.play(eng)

        @block.gpsimd
        def _(eng):
            G.play(eng)

        @block.tensor
        def _(eng):
            P.play(eng)


def const_array():
    off, n = const_plan()
    c = np.zeros((128, n), np.float32)

    def put(name, a):
        c[:, off[name]:off[name] + a.shape[1]] = a

    i = np.arange(128)
    put("ident", np.eye(128))
    put("ones", np.ones((128, 128)))
    put("mean", np.full((128, 128), 1.0 / 1024))
    put("mean128", np.full((128, 128), 1.0 / 128))
    put("mean64", (i[:, None] // 64 == i[None, :] // 64) / 64.0)
    r1 = np.zeros((128, 128))
    for j in range(0, 128, 2):
        r1[j + 1, j] = -1
        r1[j, j + 1] = 1
    put("rot1", r1)
    r2 = np.zeros((128, 128))
    for b in (0, 64):
        for j in range(8):
            r2[b + 8 + j, b + j] = -1
            r2[b + j, b + 8 + j] = 1
    put("rot2", r2)
    for g in range(2):
        put(f"dup{g}", (i[:, None] == g * 64 + i[None, :] % 64).astype(np.float32))
    f = np.float32
    t = np.arange(T)
    freq = (f(10000.0) ** (-np.arange(16, dtype=f) / f(16))).astype(f)
    ang = np.concatenate([(t // 64).astype(f)[:, None] * freq, (t % 64).astype(f)[:, None] * freq], 1)
    put("cos1", np.cos(ang).T[(i % 64) // 2])
    put("sin1", np.sin(ang).T[(i % 64) // 2])
    inv = (f(500000.0) ** (-np.arange(0, 16, 2, dtype=f) / f(16))).astype(f)
    ang = t.astype(f)[:, None] * inv
    d = i % 64
    put("cos2", np.where(d[:, None] < 16, np.cos(ang).T[d % 8], 1.0))
    put("sin2", np.where(d[:, None] < 16, np.sin(ang).T[d % 8], 0.0))
    put("causal", np.concatenate([np.zeros((128, 128)), np.where(i[None, :] <= i[:, None], 0.0, -1e30)], 1))
    ok = np.concatenate([(np.arange(15) * 16 + 31)[None, :] <= (q * 128 + i)[:, None] for q in range(2)], 1)
    put("cmpok", ok.astype(np.float32))
    put("cmpadd", np.where(ok, 0.0, -1e30))
    put("eps6", np.full((128, 1), 1e-6))
    put("eps5", np.full((128, 1), 1e-5))
    return c


def vec_array(a):
    off, n = vec_plan()
    v = np.zeros((128, n), np.float32)

    def put(name, m):
        v[:m.shape[0], off[name]:off[name] + m.shape[1]] = m

    def cols(x):
        return np.asarray(x).reshape(-1, 128).T

    for name in ("c", "c_ctx", "b_mod", "norm_g", "conv_b_pw1", "conv_w_dw", "conv_b_dw", "conv_ln_g", "conv_ln_b",
                 "conv_b_pw2", "conv_a_w_2", "diff_subln_2", "ln1_g_2", "ln1_b_2", "ln2_g_2", "ln2_b_2",
                 "ffn_conv_w_2", "ffn_conv_b_2"):
        put(name, cols(a[name]))
    for name in ("attn_q_g", "attn_k_g"):
        g = np.asarray(a[name]).reshape(64, 1)
        put(name, np.concatenate([g, g], 0))
    put("diff_lambda_2", np.asarray(a["diff_lambda_2"]).reshape(8, 64).T)
    put("nsa_cmp_pos_2", cols(a["nsa_cmp_pos_2"]))
    w2 = np.asarray(a["nsa_phi_w2_2"]).reshape(4, 128, 64).transpose(1, 0, 2)
    put("nsa_phi_w2_2", np.concatenate([w2, w2], 2).reshape(128, 512))
    return v


def stream_array(a):
    plan, total = stream_plan()
    w = np.zeros((total // PIECE, 128, PIECE), np.float32)
    for at, (kind, name, idx, r0, c0, n, width) in plan:
        dst = w[at // PIECE, :, at % PIECE:at % PIECE + n]
        src = np.asarray(a[name])[idx]
        rows = src[r0:r0 + 128]
        if kind == "vvg":
            dst[:, 0:128] = rows[:, 3584 + 3 * 128:3584 + 4 * 128]
            dst[:, 128:256] = rows[:, 3584 + 5 * 128:3584 + 6 * 128]
            dst[:, 256:280] = rows[:, 4352:4376]
        else:
            dst[:] = rows[:, c0:c0 + n]
    return w


def kernel(**inputs):
    import concourse.bacc as bacc
    from concourse.bass_utils import run_bass_kernel_spmd

    a = {k: np.asarray(v) for k, v in inputs.items()}

    def feat(x):
        return np.ascontiguousarray(x[0].T.reshape(8, 128, T).transpose(1, 0, 2))

    arrays = {
        "wstream": stream_array(a),
        "vecs": vec_array(a),
        "consts": const_array(),
        "xin": np.stack([feat(a["x"]), feat(a["ctx"])]),
    }
    nc = bacc.Bacc("TRN2", target_bir_lowering=False, num_devices=1)
    aps = [nc.dram_tensor(n, v.shape, F32, kind="ExternalInput").ap() for n, v in arrays.items()]
    out = nc.dram_tensor("out", (D, T), F32, kind="ExternalOutput").ap()
    build(nc, *aps, out)
    r = run_bass_kernel_spmd(nc, [arrays], core_ids=[0])
    got = np.asarray(r.results[0]["out"])
    return np.ascontiguousarray(got.T)[None]
```

```python
import numpy as np
from contextlib import ExitStack

import concourse.bass as bass
from concourse import mybir

F32 = mybir.dt.float32
F32R = mybir.dt.float32r
ACT = mybir.ActivationFunctionType
ALU = mybir.AluOpType
AX = mybir.AxisListType.X

D = 1024
T = 256
FT = 22
PIECE = 1024
NRAW = 7
NPIECE = 5
NTMP = 11
NCB = 3
ALPHA = 4 ** 0.25
HD = 64
LAM_INIT = [0.8 - 0.6 * float(np.exp(-0.3 * l)) for l in range(2)]
CONVW = 31
PAD = 15
TAPS6 = 20
FFN0 = [8, 7, 7]
FFN1 = [11, 11]

MOD_S = [[(0, 0), (0, 1)], [(0, 2), (0, 3)]]
MOD_C = [(0, 4), (0, 5), (0, 6), (0, 7), (0, 8)]
MOD_N = [(0, 9), (1, 1)]
MOD_F = [(0, 10), (0, 11), (1, 0)]
MOD_A = [(1, 2), (1, 3)]
MOD_T = [(1, 4), (1, 5), (1, 6), (1, 7), (1, 8), (1, 9)]
MOD_G = [(1, 10), (1, 11)]


def stream_blocks():
    b = []

    def cols(name, idx, c0, n, width, k0=0, kt=8):
        b.extend(("w", name, idx, (k0 + k) * 128, c0, n, width) for k in range(kt))

    def group(tiles, k0=0, kt=8):
        for k in range(k0, k0 + kt):
            b.extend(("w", name, idx, k * 128, c0, 128, 128) for name, idx, c0 in tiles)

    def run(tiles, first, k0=0, kt=8):
        group(tiles[:first], k0, kt)
        for t in tiles[first:]:
            group([t], k0, kt)

    def mod(groups, kind="raw"):
        for l, g in groups:
            b.extend((kind, "w_mod", (l,), k * 128, g * 512, 512, 512) for k in range(8))

    def ffn(up, down, l, parts):
        j0 = 0
        for n in parts:
            run([(name, (l,), c0 + j * 128) for j in range(j0, j0 + n) for name, c0 in up], 4)
            run([(down, (l,), m * 128) for m in range(8)], 4, j0, n)
            j0 += n

    w13 = (("ffn_w1", 0), ("ffn_w3", 0))
    mod(MOD_S[0])
    mod(MOD_S[1], "w")
    run([("conv_w_pw1", (0,), (o + j) * 128) for j in range(8) for o in (8, 0)], 4)
    mod(MOD_C)
    mod(MOD_N)
    run([("conv_w_pw2", (0,), m * 128) for m in range(8)], 4)
    mod(MOD_F)
    ffn(w13, "ffn_w2", 0, FFN0)
    mod(MOD_A)
    run([("attn_wk", (0,), m * 128) for m in range(2)], 2)
    cols("attn_wv", (0,), 0, 256, 256)
    run([("attn_wq", (0,), m * 128) for m in range(8)], 1)
    mod(MOD_T, "w")
    run([("attn_wo", (0,), m * 128) for m in range(8)], 4)
    mod(MOD_G)
    ffn(w13, "ffn_w2", 1, FFN1)
    for l in range(2):
        def z(*tiles, first=1):
            run([("w_in_2", (l,), c0) for c0 in tiles], first)

        z(*[o + 128 * m for m in range(4) for o in (2048, 1536)], first=4)
        cols("w_in_2", (l,), 2560, 512, 512)
        z(*[128 * m for m in (28, 30, 32, 29)])
        for k in range(8):
            b.append(("vvg", "w_in_2", (l,), k * 128, 0, 280, 512))
        z(*[3072 + 128 * m for m in range(4)])
        for kv in range(2):
            for k in range(16):
                b.append(("raw", "nsa_phi_w1_2", (l, kv), k * 128, 0, 128, 128))
        z(*[o + 128 * j for j in range(4) for o in (1024, 512, 0)])
        z(*[4376 + 128 * m for m in range(16)])
        for m in range(8):
            z(4376 + (16 + m) * 128)
            for br in range(3):
                group([("w_branch_2", (l, br), m * 128)], 0, 4)
        run([("w_o_2", (l,), m * 128) for m in range(8)], 4)
        ffn((("ffn_w_up_2", 0), ("ffn_w_up_2", 2816)), "ffn_w_down_2", l, FFN1)
    return b


def stream_plan():
    out, at = [], 0
    for blk in stream_blocks():
        width = blk[6]
        assert at % PIECE + width <= PIECE
        out.append((at, blk))
        at += width
    assert at % PIECE == 0
    return out, at


def vec_plan():
    off, at = {}, 0
    for name, n in (("c", 8), ("c_ctx", 8), ("b_mod", 96), ("norm_g", 64), ("conv_b_pw1", 16), ("conv_w_dw", 248),
                    ("conv_b_dw", 8), ("conv_ln_g", 8), ("conv_ln_b", 8), ("conv_b_pw2", 8), ("attn_q_g", 1),
                    ("attn_k_g", 1), ("conv_a_w_2", 24), ("diff_lambda_2", 8), ("diff_subln_2", 2),
                    ("nsa_cmp_pos_2", 64), ("ln1_g_2", 16), ("ln1_b_2", 16), ("ln2_g_2", 16), ("ln2_b_2", 16),
                    ("ffn_conv_w_2", 264), ("ffn_conv_b_2", 88), ("nsa_phi_w2_2", 512)):
        off[name] = at
        at += n
    return off, at


CONSTS = (("eps6", 1), ("eps5", 1), ("ident", 128), ("mean", 128), ("ones", 128), ("mean128", 128), ("mean64", 128), ("rot1", 128), ("rot2", 128),
          ("dup0", 128), ("dup1", 128), ("cos1", 256), ("sin1", 256), ("cos2", 256), ("sin2", 256), ("causal", 256),
          ("cmpadd", 30), ("cmpok", 30))


def const_plan():
    off, at = {}, 0
    for name, n in CONSTS:
        off[name] = at
        at += n
    return off, at


class Queue:
    def __init__(self, sem):
        self.sem, self.items, self.n = sem, [], 0

    def __call__(self, fn, *after, inc=True):
        self.items.append((flat(after), fn, inc))
        if inc:
            self.n += 1
        return (self.sem, self.n)

    def play(self, eng):
        seen = {}
        for waits, fn, inc in self.items:
            most = {}
            for s, v in waits:
                if v > seen.get(id(s), 0) and v > most.get(id(s), (s, 0))[1]:
                    most[id(s)] = (s, v)
            for key, (s, v) in most.items():
                eng.wait_ge(s, v)
                seen[key] = v
            ins = fn(eng)
            if inc:
                ins.then_inc(self.sem, 1)


def flat(x):
    if x is None:
        return []
    if isinstance(x, tuple) and len(x) == 2 and isinstance(x[1], int):
        return [x]
    return [t for y in x for t in flat(y)]


class Ring:

    def __init__(self, bufs):
        self.bufs, self.rel, self.at = bufs, [[] for _ in bufs], 0

    def get(self):
        i = next(j % len(self.bufs) for j in range(self.at, self.at + len(self.bufs)) if self.rel[j % len(self.bufs)] is not None)
        self.at = i + 1
        w = self.rel[i]
        self.rel[i] = None
        return i, self.bufs[i], w

    def free(self, i, *toks):
        assert self.rel[i] is None
        self.rel[i] = flat(toks)


class Pipe:

    def __init__(self):
        self.tasks = []

    def run(self, task):
        old, self.tasks = self.tasks, []
        for t in [task] + old:
            if next(t, self) is not self:
                self.tasks.append(t)
        if task in self.tasks:
            self.tasks.remove(task)
            self.tasks.append(task)

    def add(self, task):
        if next(task, self) is not self:
            self.tasks.append(task)

    def step(self):
        self.tasks = [t for t in self.tasks if next(t, self) is not self]

    def drain(self):
        while self.tasks:
            self.step()


def build(nc, wstream, vecs_d, const_d, xin, out):
    plan, total = stream_plan()
    voff, nvec = vec_plan()
    coff, ncon = const_plan()
    npiece = total // PIECE
    ctx = ExitStack()
    with ctx:
        def sb(name, shape, dt=F32):
            return ctx.enter_context(nc.sbuf_tensor(name, shape, dt))

        def sem(name):
            return ctx.enter_context(nc.semaphore(name))

        raw = sb("raw", [128, NRAW, PIECE])
        whi = sb("whi", [128, NPIECE, PIECE], F32R)
        wlo = sb("wlo", [128, NPIECE, PIECE], F32R)
        X = sb("X", [128, 2, 8, T])
        Hh = sb("Hh", [128, 4096], F32R)
        Hl = sb("Hl", [128, 4096], F32R)
        Y = sb("Y", [128, 4096])
        VEC = sb("VEC", [128, nvec])
        CON = sb("CON", [128, ncon])
        MOD = sb("MOD", [128, 2, 48, 2])
        MA = sb("MA", [128, 2, 4, 2, 8])
        CS = sb("CS", [128, 8, 4], F32R)
        SM = sb("SM", [128, 256])
        tmpb = sb("tmpb", [128, NTMP, 512])
        cbb = sb("cbb", [128, NCB, 260])
        arena = []

        def arena_open(specs):
            for cm in reversed(arena):
                cm.__exit__(None, None, None)
            arena.clear()
            got = []
            for name, shape, dt in specs:
                cm = nc.sbuf_tensor(name, shape, dt)
                got.append(cm.__enter__())
                arena.append(cm)
            return got

        banks = [ctx.enter_context(nc.psum_tensor(f"pb{i}", [128, 512], F32)) for i in range(8)]

        S, A, V, G, P = (Queue(sem(n)) for n in ("s_sync", "s_act", "s_dve", "s_pool", "s_pe"))
        s_raw = [sem(f"s_raw{i}") for i in range(NRAW)]
        s_vec = sem("s_vec")
        s_con = sem("s_con")
        s_rest = sem("s_rest")
        s_x = sem("s_x")
        s_out = sem("s_out")

        tmp = Ring([tmpb[:, i, :] for i in range(NTMP)])
        cbr = Ring([cbb[:, i, :] for i in range(NCB)])
        pm = Ring([b[:, :] for b in banks[0:5]])
        pt = Ring([b[:, :] for b in banks[5:7]])
        pst = Ring([b[:, :] for b in banks[7:8]])

        def con(name, a=0, b=None, p0=0, p1=128):
            n = dict(CONSTS)[name]
            return CON[p0:p1, coff[name] + a:coff[name] + (n if b is None else b)]

        def vec(name, i=0, n=1):
            return VEC[:, voff[name] + i:voff[name] + i + n]

        def act(out_, in_, func, *after, bias=None, scale=None, accum=None):
            kw = {}
            if bias is not None:
                kw["bias"] = bias
            if scale is not None:
                kw["scale"] = scale
            if accum is not None:
                kw["accum_out"] = accum
            return A(lambda e: e.activation(out_, in_, func, **kw), *after)

        def tt(out_, a, b, op, *after, q=None):
            return (q or V)(lambda e: e.tensor_tensor(out_, a, b, op), *after)

        def stt(out_, a, s, b, op0, op1, *after):
            return V(lambda e: e.scalar_tensor_tensor(out=out_, in0=a, scalar=s, in1=b, op0=op0, op1=op1), *after)

        def ts(out_, a, s1, s2, op0, op1, *after):
            if op1 is None:
                return V(lambda e: e.tensor_scalar(out_, a, s1, None, op0), *after)
            return V(lambda e: e.tensor_scalar(out_, a, s1, s2, op0, op1), *after)

        def vcopy(out_, a, *after):
            return V(lambda e: e.tensor_copy(out_, a), *after)

        def recip(out_, a, *after):
            return V(lambda e: e.reciprocal(out_, a), *after)

        def rmax(out_, a, *after):
            return V(lambda e: e.reduce_max(out_, a, AX), *after)

        def mm(out_, lhsT, rhs, start, stop, *after, inc=False):
            return P(lambda e: e.matmul(out_, lhsT, rhs, start=start, stop=stop), *after, inc=inc)

        def tr(out_, in_, idn, *after, inc=False):
            return P(lambda e: e.transpose(out_, in_, idn), *after, inc=inc)

        def f32(ap):
            return ap.bitcast(F32)

        def load(dst, src, s):
            S.items.append(([], lambda e: e.dma_start(dst, src).then_inc(s, 16), False))

        nv0 = voff["conv_b_pw1"]
        load(VEC[:, 0:nv0], vecs_d[:, 0:nv0], s_vec)
        vec_tok = (s_vec, 16)
        con_tok = (s_con, 16)
        rest_tok = (s_rest, 32)
        in_tok = [vec_tok, con_tok]
        nc0 = coff["ones"]
        x_tok = (s_x, 32)

        st = {"blk": 0, "made": 0, "dma": 0, "parts": 0}
        raw_rel = {}
        owner = [None] * NPIECE
        piece = {}
        piece_rel = {}
        raw_kind = {at // PIECE for at, blk in plan if blk[0] == "raw"}
        lo_queue = {"f": lambda p: V}
        hook = {"f": lambda: None}
        mid = {"f": lambda: None}
        eager = {"f": True}

        def raw_tok(p):
            return (s_raw[p % NRAW], 16 * (p // NRAW + 1))

        def dma_pieces():
            while st["dma"] < npiece:
                p = st["dma"]
                if p >= NRAW and p - NRAW not in raw_rel:
                    return
                s = s_raw[p % NRAW]
                S.items.append((flat(raw_rel.get(p - NRAW)), lambda e, p=p, s=s: e.dma_start(
                    raw[:, p % NRAW, :], wstream[p]).then_inc(s, 16), False))
                st["dma"] += 1
                if p == 2:
                    load(CON[:, 0:nc0], const_d[:, 0:nc0], s_con)
                    for seg in range(2):
                        load(X[:, seg, :, :], xin[seg], s_x)
                if p == 20:
                    load(CON[:, nc0:], const_d[:, nc0:], s_rest)
                    load(VEC[:, nv0:], vecs_d[:, nv0:], s_rest)

        def make_pieces(n, q=None):
            while n and st["made"] < npiece:
                p = st["made"]
                dma_pieces()
                if p in raw_kind:
                    st["made"] += 1
                    continue
                if st["dma"] <= p:
                    return
                n -= 1
                i = st["parts"] % NPIECE
                if owner[i] is not None and owner[i] not in piece_rel:
                    return
                free = piece_rel[owner[i]] if owner[i] is not None else []
                src, hi, lo = raw[:, p % NRAW, :], whi[:, i, :], wlo[:, i, :]
                a = act(hi, src, ACT.Copy, raw_tok(p), free)
                b = tt(lo, src, f32(hi), ALU.subtract, a, free, q=q or lo_queue["f"](p))
                owner[i] = p
                piece[p] = (hi, lo, [a, b])
                raw_rel[p] = [a, b]
                st["made"] += 1
                st["parts"] += 1
                dma_pieces()

        def take(kind, width):
            at, blk = plan[st["blk"]]
            st["blk"] += 1
            assert blk[0] == kind and blk[6] == width, (blk, kind, width)
            p, o = at // PIECE, at % PIECE
            make_pieces(NPIECE if eager["f"] else p + 1 - st["made"])
            if o == 0:
                hook["f"]()
            hi, lo, toks = piece[p]
            return hi[:, o:o + width], lo[:, o:o + width], toks, p, o + width == PIECE

        def take_raw(n):
            at, blk = plan[st["blk"]]
            assert blk[0] == "raw" and at % PIECE == 0
            st["blk"] += n
            p = at // PIECE
            dma_pieces()
            assert st["dma"] > p
            hook["f"]()
            return raw[:, p % NRAW, :], raw_tok(p), p

        def done(p, tok):
            piece_rel[p] = [tok]

        def lins(g, kt, xh, xl, n, xtok):
            got = [pm.get() for _ in range(g)]
            toks = [None] * g
            for k in range(kt):
                for m, (i, bank, w) in enumerate(got):
                    hi, lo, pk, p, end = take("w", 128)
                    o = bank[:, 0:n]
                    mm(o, hi, xh(k), k == 0, False, pk, w, xtok(k))
                    mm(o, hi, xl(k), False, False)
                    toks[m] = mm(o, lo, xh(k), False, k == kt - 1, inc=end or k == kt - 1)
                    if end:
                        done(p, toks[m])
                if k % 4 == 3:
                    mid["f"]()
            return [(i, bank[:, 0:n], t) for (i, bank, w), t in zip(got, toks)]

        def lin(kt, xh, xl, n, xtok):
            return lins(1, kt, xh, xl, n, xtok)[0]

        def lin_run(count, first, *a):
            yield from lins(first, *a)
            for _ in range(count - first):
                yield lin(*a)

        def lin_tok(kind, width, n, xh, xl, tiles, xtok):
            got = [pm.get() for _ in range(tiles)]
            for k in range(8):
                hi, lo, pk, p, end = take(kind, width)
                for s, (i, bank, w) in enumerate(got):
                    o = bank[:, 0:n]
                    xa, xb = xh(k)[:, s * 128:(s + 1) * 128], xl(k)[:, s * 128:(s + 1) * 128]
                    mm(o, xa, hi[:, 0:n], k == 0, False, pk, w, xtok(k))
                    mm(o, xb, hi[:, 0:n], False, False)
                    tok = mm(o, xa, lo[:, 0:n], False, k == 7, inc=k == 7 or (end and s == tiles - 1))
                if end:
                    done(p, tok)
            return [(i, bank[:, 0:n]) for i, bank, w in got], tok

        def split(hi, lo, src, *after):
            a = act(hi, src, ACT.Copy, *after)
            b = tt(lo, src, f32(hi), ALU.subtract, a, *after)
            return [a, b]

        rsr = Ring([SM[:, 218 + 8 * i:226 + 8 * i] for i in range(3)])

        def root(stat, eps):
            im, sm, w = rsr.get()
            n, col = stat.n // 128, sm[:, 0:stat.cols]
            t0 = act(col, stat.bank, ACT.Sqrt, stat.tok, w, in_tok, bias=con(eps))
            stat.free(t0)
            t = recip(col, col, t0)
            if stat.parts == 1:
                return rsr, im, [col[:, c:c + 1].broadcast_to((128, 128)) for c in range(n)], t
            ib, wide, wb = tmp.get()
            t = vcopy(wide[:, 0:128 * n].rearrange("p (c o) -> p c o", c=stat.cols),
                      col.rearrange("p (c o) -> p c o", o=1).broadcast_to((128, stat.cols, 128 // stat.parts)), t, wb)
            rsr.free(im, t)
            return tmp, ib, [wide[:, c * 128:(c + 1) * 128] for c in range(n)], t

        def spread(ring, im, cols, tok):
            ir, r, w = pt.get()
            for c, src in enumerate(cols):
                t = mm(r[:, c * 128:(c + 1) * 128], src, con("ident"), True, True, tok, w, in_tok, inc=c == len(cols) - 1)
            if ring:
                ring.free(im, t)
            return ir, r[:, 0:128 * len(cols)], t

        def rstd(stat, eps, ahead=False):
            got = root(stat, eps)
            bite(1)
            if ahead:
                make_pieces(1, V)
                make_pieces(1, G)
            return spread(*got)

        def preload(func):
            A(lambda e: e.activation(SM[:, 255:256], CON[:, coff["eps6"]:coff["eps6"] + 1], func), in_tok)

        class Stat:

            def __init__(self, n, mat="mean", kt=8, adds=False, ring=None, parts=1):
                self.n, self.mat, self.kt, self.k, self.adds = n, mat, kt, 0, adds
                self.parts, self.cols = parts, parts * n // 128
                self.ring = ring or pst
                self.i = None

            def open(self):
                if self.i is None:
                    self.i, self.bank, self.w = self.ring.get()
                    self.bank = self.bank[:, 0:self.cols or self.n]

            def sums(self, tile, first, last, tok):
                if not self.parts:
                    return mm(self.bank, con(self.mat), tile, first, last, tok, self.w, in_tok, inc=True)
                p, mean, nc = self.parts, con(self.mat)[:, 0:128:128 // self.parts], self.n // 128
                for c in range(nc):
                    t = mm(self.bank[:, c * p:(c + 1) * p], tile[:, c * 128:(c + 1) * 128], mean, first and c == 0,
                           last and c == nc - 1, tok, self.w, in_tok, inc=c == nc - 1)
                return t

            def add(self, tile, tok):
                k = self.k
                self.k += 1
                if not self.adds:
                    self.open()
                    self.tok = self.sums(tile, k == 0, k == self.kt - 1, tok)
                    return self.tok
                if k == 0:
                    self.ia, t, w = tmp.get()
                    self.acc = t[:, 0:self.n]
                    self.at = vcopy(self.acc, tile, tok, w)
                else:
                    self.at = tt(self.acc, self.acc, tile, ALU.add, tok, self.at)
                rd = self.at
                self.close()
                return rd

            def close(self):
                if self.k == self.kt:
                    self.open()
                    self.tok = self.sums(self.acc, True, True, self.at)
                    tmp.free(self.ia, self.tok)

            def square(self, src, tok):
                if self.k == self.kt - 1:
                    preload(ACT.Sqrt)
                if self.adds and self.k == 0:
                    self.k = 1
                    self.ia, t, w = tmp.get()
                    self.acc = t[:, 0:self.n]
                    self.at = act(self.acc, src, ACT.Square, tok, w)
                    return self.at
                i, t, w = tmp.get()
                a = act(t[:, 0:self.n], src, ACT.Square, tok, w)
                tmp.free(i, self.add(t[:, 0:self.n], a))
                return a

            def free(self, *toks):
                self.ring.free(self.i, *toks)

        sil = SM[:, 0:16]
        t_sil = act(sil, vec("c", 0, 16), ACT.Silu, vec_tok)
        csv = sil.rearrange("p (s k) -> p k s", s=2)
        t_cs = act(CS[:, :, 0:2], csv, ACT.Copy, t_sil)
        t_cs2 = tt(CS[:, :, 2:4], csv, f32(CS[:, :, 0:2]), ALU.subtract, t_cs)
        mod_tok = {}
        pipe = Pipe()
        mpipe = Pipe()
        mid["f"] = mpipe.step

        def mod_group(l, g):
            i, bank, w = pm.get()
            for k in range(8):
                hi, lo, pk, p, end = take("w", 512)
                mm(bank[0:4, :], CS[:, k, :], hi, k == 0, False, pk, w, t_cs, t_cs2)
                tok = mm(bank[0:4, :], CS[:, k, :], lo, False, k == 7, inc=end)
                if end:
                    done(p, tok)
            yield from mod_end(l, g, i, bank, tok)

        def mod_end(l, g, i, bank, tok):
            it, t, wt = tmp.get()
            a = act(t[0:4, :], bank[0:4, :], ACT.Copy, tok, wt)
            pm.free(i, a)
            yield
            ip, pb, wp = pt.get()
            for j in range(4):
                tk = tr(pb[:, 4 * j:4 * j + 4], t[0:4, j * 128:(j + 1) * 128], con("ident", 0, 4, 0, 4), a, wp, in_tok,
                        inc=j == 3)
            tmp.free(it, tk)
            pv = pb[:, 0:16].rearrange("p (j s) -> p j s", j=4)
            dst = MOD[:, l, 4 * g:4 * g + 4, :]
            bm = vec("b_mod", l * 48 + 4 * g, 4).rearrange("p (j o) -> p j o", o=1).broadcast_to((128, 4, 2))
            v1 = tt(dst, pv[:, :, 0:2], bm, ALU.add, tk)
            v2 = tt(dst, pv[:, :, 2:4], dst, ALU.add, v1)
            pt.free(ip, v2)
            mod_tok[l, g] = v2

        def mod_steps(groups):
            ends = Pipe()
            for l, g in groups:
                i, bank, w = pm.get()
                for k in range(8):
                    hi, lo, pk, p, end = take("w", 512)
                    mm(bank[0:4, :], CS[:, k, :], hi, k == 0, False, pk, w, t_cs, t_cs2)
                    tok = mm(bank[0:4, :], CS[:, k, :], lo, False, k == 7, inc=end)
                    if end:
                        done(p, tok)
                        if k == 7:
                            ends.add(mod_end(l, g, i, bank, tok))
                        yield
                        if k < 7:
                            ends.step()
            ends.drain()

        def mod_raw(l, g):
            i, bank, w = pm.get()
            for k in range(0, 8, 2):
                wt, tk, p = take_raw(2)
                for q in range(2):
                    tok = mm(bank[0:2, :], csv[:, k + q, :], wt[:, q * 512:(q + 1) * 512], k + q == 0, k + q == 7,
                             tk, w, t_sil, inc=q == 1)
                raw_rel[p] = [tok]
                dma_pieces()
                yield
            it, t, wt_ = tmp.get()
            a = act(t[0:2, :], bank[0:2, :], ACT.Copy, tok, wt_)
            pm.free(i, a)
            yield
            ip, pb, wp = pt.get()
            for j in range(4):
                tk = tr(pb[:, 2 * j:2 * j + 2], t[0:2, j * 128:(j + 1) * 128], con("ident", 0, 2, 0, 2), a, wp, in_tok,
                        inc=j == 3)
            tmp.free(it, tk)
            bm = vec("b_mod", l * 48 + 4 * g, 4).rearrange("p (j o) -> p j o", o=1).broadcast_to((128, 4, 2))
            mod_tok[l, g] = tt(MOD[:, l, 4 * g:4 * g + 4, :], pb[:, 0:8].rearrange("p (j s) -> p j s", j=4), bm, ALU.add, tk)
            pt.free(ip, mod_tok[l, g])

        pend = []

        def bite(n):
            for _ in range(n):
                if pend:
                    next(pend[0][0])
                    pend[0][1] -= 1
                    if not pend[0][1]:
                        mpipe.tasks.append(pend.pop(0)[0])

        def feed(groups):
            pend.extend([mod_raw(l, g), 4] for l, g in groups)

        def mods(groups):
            feed(groups)
            bite(4 * len(groups))

        def mvec(l, which, s, k):
            return MOD[:, l, which * 8 + k, s:s + 1]

        def mod_scale(l, slot, which, gi, plus):
            toks = []
            for s in range(2):
                toks.append(stt(MA[:, l, slot, s, :], MOD[:, l, which * 8:which * 8 + 8, s], plus,
                                vec("norm_g", (l * 4 + gi) * 8, 8), ALU.add, ALU.mult,
                                [mod_tok[l, 2 * which], mod_tok[l, 2 * which + 1]], in_tok))
            return toks

        def Hx(k, n=512):
            return Hh[:, k * 512:k * 512 + n], Hl[:, k * 512:k * 512 + n]

        xt = [[x_tok] for _ in range(8)]
        hfree = {"t": []}

        def x_stat(segs, then, stat=None):
            n = 256 * segs
            if stat is None:
                stat = Stat(n, adds=True)
                for k in range(8):
                    stat.square(X[:, 0:segs, k, :], xt[k])
            ir, r, t1 = rstd(stat, "eps6", True)
            preload(then)
            return ir, r, t1

        def modulated(l, slot, shift, sctoks, segs, rs):
            ir, r, t1 = rs
            toks, last = [[] for _ in range(8)], []
            sh_t = [mod_tok[l, 2 * shift], mod_tok[l, 2 * shift + 1]]
            line = Pipe()

            def tile(k):
                i, t, w = tmp.get()
                for s in range(segs):
                    sl = slice(s * 256, (s + 1) * 256)
                    a = stt(t[:, sl], X[:, s, k, :], MA[:, l, slot, s, k:k + 1], r[:, sl], ALU.mult, ALU.mult,
                            t1, w, sctoks, xt[k])
                last.append(a)
                hs = [slice(k * 512 + s * 256, k * 512 + (s + 1) * 256) for s in range(segs)]
                for s in range(segs):
                    toks[k].append(act(Hh[:, hs[s]], t[:, s * 256:(s + 1) * 256], ACT.Identity, a, hfree["t"], sh_t,
                                       bias=mvec(l, shift, s, k)))
                yield
                for s in range(segs):
                    toks[k].append(stt(Hl[:, hs[s]], t[:, s * 256:(s + 1) * 256], mvec(l, shift, s, k), f32(Hh[:, hs[s]]),
                                       ALU.add, ALU.subtract, toks[k][s], hfree["t"]))
                tmp.free(i, toks[k])

            for k in range(8):
                line.run(tile(k))
                if k == 0:
                    line.step()
                if k == 1:
                    mpipe.step()
                if k > 1:
                    make_pieces(1, G)
            line.drain()
            pt.free(ir, last)
            return toks

        def xh(k):
            return Hh[:, k * T:(k + 1) * T]

        def xl(k):
            return Hl[:, k * T:(k + 1) * T]

        parts = Pipe()
        xtoks = [None] * 8

        def xparts(k):
            a = act(xh(k), X[:, 0, k, :], ACT.Copy, xt[k], hfree["t"])
            yield
            xtoks[k] = [a, tt(xl(k), X[:, 0, k, :], f32(xh(k)), ALU.subtract, a, hfree["t"])]
            xt[k] = [xt[k], xtoks[k]]

        def residual(l, slot, sctoks, stat, ytoks, segs, next_=True):
            xs_ = Stat(256 * segs) if next_ else None
            n = 256 * segs
            ir, r, t1 = rstd(stat, "eps6")
            bite(1)
            for k in range(8):
                i, t, w = tmp.get()
                last = []
                for s in range(segs):
                    sl = slice(s * 256, (s + 1) * 256)
                    a = stt(t[:, sl], Y[:, k * 512 + s * 256:k * 512 + (s + 1) * 256], MA[:, l, slot, s, k:k + 1], r[:, sl],
                            ALU.mult, ALU.mult, t1, w, sctoks, ytoks[k])
                    last.append(a)
                xs = X[:, 0:segs, k, :]
                xt[k] = [tt(xs, xs, t[:, 0:n].rearrange("p (s t) -> p s t", s=segs), ALU.add, last, xt[k],
                            q=G if k % 2 else V)]
                tmp.free(i, xt[k])
                if next_:
                    xs_.square(xs, xt[k])
                    if k % 2 == 0:
                        bite(1)
                else:
                    parts.run(xparts(k))
                    if k < 5:
                        make_pieces(1, G)
            parts.drain()
            pt.free(ir, last)
            return xs_

        yfree = {"t": []}

        def swiglu(l, parts, htoks, segs):
            n = 256 * segs
            cap = 4096 // n
            HIh, HIl = arena_open([(f"hid_h{l}", [128, 4096], F32R), (f"hid_l{l}", [128, 4096], F32R)])
            hidfree = list(arena_free["t"])
            ytoks = [None] * 8
            stat = None
            for pi, cnt in enumerate(parts):
                assert cnt <= cap
                gt = [None] * cnt
                tiles = lin_run(2 * cnt, 4, 8, lambda k: Hx(k, n)[0], lambda k: Hx(k, n)[1], n, lambda k: htoks[k])

                def hidden(j, t1, t3):
                    i1, b1, t1 = t1
                    i3, b3, t3 = t3
                    it, s1, w = tmp.get()
                    a = act(s1[:, 0:n], b1, ACT.Silu, t1, w)
                    pm.free(i1, a)
                    b = tt(s1[:, 0:n], b3, s1[:, 0:n], ALU.mult, a, t3)
                    pm.free(i3, b)
                    yield
                    gt[j] = split(HIh[:, j * n:(j + 1) * n], HIl[:, j * n:(j + 1) * n], s1[:, 0:n], b, hidfree)
                    tmp.free(it, gt[j])

                for j in range(cnt):
                    t1, t3 = next(tiles), next(tiles)
                    pipe.run(hidden(j, t1, t3))
                pipe.drain()
                t3 = t3[2]
                hfree["t"] = [t3]
                final = pi == len(parts) - 1
                if final:
                    stat = Stat(n, adds=True)
                for m, (i, bk, t) in enumerate(lin_run(8, 4, cnt, lambda k: HIh[:, k * n:(k + 1) * n],
                                                       lambda k: HIl[:, k * n:(k + 1) * n], n, lambda k: gt[k])):
                    y = Y[:, m * 512:m * 512 + n]
                    if pi == 0:
                        ytoks[m] = act(y, bk, ACT.Copy, t, yfree["t"])
                    else:
                        ytoks[m] = tt(y, bk, y, ALU.add, t, ytoks[m])
                    pm.free(i, ytoks[m])
                    if final:
                        stat.square(y, ytoks[m])
                hidfree = [t]
            arena_free["t"] = [t]
            return stat, ytoks

        arena_free = {"t": []}

        dma_pieces()
        mods(MOD_S[0])
        rs = x_stat(2, ACT.Sigmoid)
        for g in MOD_S[1]:
            pipe.run(mod_group(*g))
        mpipe.drain()
        pipe.drain()
        sc = mod_scale(0, 0, 1, 0, 1.0)
        htoks = modulated(0, 0, 0, sc, 2, rs)

        in_tok.append(rest_tok)
        U, DG = arena_open([("U", [128, 8, 2, 286], F32), ("DG", [128, 3, 8, 128], F32)])
        t_pad = [G(lambda e: e.memset(U[:, :, :, 0:PAD], 0.0)), G(lambda e: e.memset(U[:, :, :, PAD + T:], 0.0)),
                 G(lambda e: e.memset(cbb[:, :, :], 0.0))]
        cb_zero = t_pad[2]
        utoks = {}

        taps = [(k, i) for ks in ((1, 2), (4, 5)) for i in range(CONVW) for k in ks]
        taps += [(6, i) for i in range(TAPS6, CONVW)]
        ptaps = [(k, i) for k, n in ((0, CONVW), (3, CONVW), (6, TAPS6)) for i in range(n)]
        vt = [None] * 8

        def conv_tap(k, i):
            y = Y[:, k * 512:(k + 1) * 512].rearrange("p (s t) -> p s t", s=2)
            u = U[:, k, :, i:i + T]
            w = vec("conv_w_dw", i * 8 + k)
            if k not in (0, 3, 6) or (k == 6 and i >= TAPS6):
                if i == 0:
                    vt[k] = ts(y, u, w, vec("conv_b_dw", k), ALU.mult, ALU.add, utoks[k], t_pad, in_tok)
                else:
                    vt[k] = stt(y, u, w, y, ALU.mult, ALU.add, vt[k])
            elif i == 0:
                vt[k] = act(y, u, ACT.Identity, utoks[k], t_pad, in_tok, bias=vec("conv_b_dw", k), scale=w)
            else:
                j, t, wt_ = tmp.get()
                t3 = t.rearrange("p (s t) -> p s t", s=2)
                a = act(t3, u, ACT.Copy, utoks[k], wt_, scale=w)
                vt[k] = tt(y, y, t3, ALU.add, a, vt[k], q=G)
                tmp.free(j, vt[k])

        def conv_taps(n, np_=0):
            for todo_, m in ((taps, n), (ptaps, np_)):
                for _ in range(m):
                    if todo_ and all(k in utoks for k, i in todo_[:2]) and (todo_[0] != (6, TAPS6) or not ptaps):
                        conv_tap(*todo_.pop(0))

        dgr = Ring([DG[:, i, :, :] for i in range(3)])

        def conv_diag(k, i0):
            n = min(8, CONVW - i0)
            i, dg, w = dgr.get()
            idn = con("ident").rearrange("p (o c) -> p o c", o=1).broadcast_to((128, n, 128))
            wv = VEC[:, voff["conv_w_dw"] + i0 * 8 + k:voff["conv_w_dw"] + (i0 + n - 1) * 8 + k + 1:8]
            wv = wv.rearrange("p (i o) -> p i o", o=1).broadcast_to((128, n, 128))
            return i, dg, n, tt(dg[:, 0:n, :], idn, wv, ALU.mult, w, in_tok, q=G)

        diag = [(k, i0) for k in (7,) for i0 in range(0, CONVW, 8)]
        ready = [conv_diag(*diag.pop(0)) for _ in range(3)]
        hook["f"] = lambda: conv_taps(5, 4)
        lo_queue["f"] = lambda p: V
        tiles = lin_run(16, 4, 8, lambda k: Hx(k)[0], lambda k: Hx(k)[1], 512, lambda k: htoks[k])
        for j in range(8):
            ig, bg, tg = next(tiles)
            ia, ba, ta = next(tiles)
            i, t, w = tmp.get()
            a = act(t, bg, ACT.Sigmoid, tg, w, bias=vec("conv_b_pw1", 8 + j))
            pm.free(ig, a)
            b = stt(U[:, j, :, PAD:PAD + T], ba.rearrange("p (s t) -> p s t", s=2), vec("conv_b_pw1", j),
                    t.rearrange("p (s t) -> p s t", s=2), ALU.add, ALU.mult, a, ta, t_pad)
            pm.free(ia, b)
            tmp.free(i, b)
            utoks[j] = b
        hfree["t"] = [ta]

        hook["f"] = lambda: conv_taps(3, 1)
        for k in (7,):
            ib, bk, w = pm.get()
            for i0 in range(0, CONVW, 8):
                conv_taps(8, 4)
                i, dg, n, tk = ready.pop(0)
                for q in range(n):
                    t0 = mm(bk.rearrange("p (s t) -> p s t", s=2), dg[:, q, :], U[:, k, :, i0 + q:i0 + q + T],
                            i0 + q == 0, i0 + q == CONVW - 1, tk, utoks[k], t_pad, w, inc=q == n - 1)
                dgr.free(i, t0)
                if diag:
                    ready.append(conv_diag(*diag.pop(0)))
            vt[k] = act(Y[:, k * 512:(k + 1) * 512], bk, ACT.Identity, t0, in_tok, bias=vec("conv_b_dw", k))
            pm.free(ib, vt[k])
        for g in MOD_C:
            mpipe.step()
            mods([g])
        hook["f"] = lambda: None
        while taps or ptaps:
            conv_taps(2, 1)
        mpipe.drain()
        stat = Stat(512, parts=0)
        for k in (0, 1, 2, 3, 7, 4, 5, 6):
            stat.add(Y[:, k * 512:(k + 1) * 512], vt[k])
        lo_queue["f"] = lambda p: V
        arena_free["t"] = list(vt)

        def center(stat, n, toks, stride):
            s2 = Stat(n, ring=pt)
            out_ = []
            for k in range(8):
                y = Y[:, k * stride:k * stride + n]
                a = tt(y, y, stat.bank, ALU.subtract, toks[k], stat.tok)
                s2.square(y, a)
                out_.append(a)
                if k % 2:
                    bite(1)
            stat.free(out_[-1])
            return s2, out_

        feed(MOD_N)
        s2, ct = center(stat, 512, vt, 512)
        ir, r, t1 = rstd(s2, "eps6")
        preload(ACT.Silu)
        bite(16)
        htoks = [None] * 8
        yr = []

        def conv_act(k):
            i, t, w = tmp.get()
            yr.append(tt(t, Y[:, k * 512:(k + 1) * 512], r, ALU.mult, t1, w, ct[k]))
            b = act(t, t, ACT.Silu, yr[-1], in_tok, bias=vec("conv_ln_b", k), scale=vec("conv_ln_g", k))
            c_ = act(Hx(k)[0], t, ACT.Copy, b, hfree["t"])
            yield
            htoks[k] = [c_, tt(Hx(k)[1], t, f32(Hx(k)[0]), ALU.subtract, c_, hfree["t"])]
            tmp.free(i, htoks[k])

        for k in range(8):
            pipe.run(conv_act(k))
            if k in (0, 2):
                mpipe.step()
            if k < 5:
                make_pieces(1, G)
        pipe.drain()
        a = yr[-1]
        pt.free(ir, a)
        yread = [a, s2.tok]

        stat = Stat(512, adds=True)
        ytoks = []
        for m, (i, bk, t) in enumerate(lin_run(8, 4, 8, lambda k: Hx(k)[0], lambda k: Hx(k)[1], 512, lambda k: htoks[k])):
            a = act(Y[:, m * 512:(m + 1) * 512], bk, ACT.Identity, t, yread, bias=vec("conv_b_pw2", m))
            pm.free(i, a)
            stat.square(Y[:, m * 512:(m + 1) * 512], a)
            ytoks.append(a)
        hfree["t"] = [t]
        sc = mod_scale(0, 1, 2, 1, 0.0)
        mpipe.drain()
        feed(MOD_F)
        xs_ = residual(0, 1, sc, stat, ytoks, 2)

        def ffn_first(l, parts, segs, xs_, after):
            yfree["t"] = [xt[k] for k in range(8)]
            rs = x_stat(segs, ACT.Silu, xs_)
            bite(16)
            sc = mod_scale(l, 2, 4, 2, 1.0)
            ht = modulated(l, 2, 3, sc, segs, rs)
            stat, yt = swiglu(l, parts, ht, segs)
            sc = mod_scale(l, 3, 5, 3, 0.0)
            mpipe.drain()
            feed(after)
            return residual(l, 3, sc, stat, yt, segs, l == 0)

        xs_ = ffn_first(0, FFN0, 2, xs_, MOD_A)

        rs = x_stat(2, ACT.Sqrt, xs_)
        bite(16)
        mpipe.drain()
        sc = mod_scale(1, 0, 1, 0, 1.0)
        htoks = modulated(1, 0, 0, sc, 2, rs)
        afree = list(arena_free["t"])
        K1h, K1l, V1h, V1l = arena_open([("K1h", [128, 4, 512], F32R), ("K1l", [128, 4, 512], F32R),
                                         ("V1h", [128, 4, 4, 128], F32R), ("V1l", [128, 4, 4, 128], F32R)])

        def Q1(j):
            return [x_[:, j * 512 + T:(j + 1) * 512] for x_ in (Hh, Hl)]


        def headed(got, n, gain, finish):
            i, bk, t = got
            it, r_, w = tmp.get()
            src = r_[:, 0:n]
            a = act(src, bk, ACT.Copy, t, w)
            iq, sq, wq = tmp.get()
            b = act(sq[:, 0:n], bk, ACT.Square, t, wq)
            pm.free(i, a, b)
            yield
            s_ = Stat(n, "mean64", 1, parts=2)
            tmp.free(iq, s_.add(sq[:, 0:n], b))
            got = root(s_, "eps6")
            yield
            ir, r, t1 = spread(*got)
            a = stt(src, src, gain, r, ALU.mult, ALU.mult, t1, a)
            pt.free(ir, a)
            yield
            yield from finish(it, src, a)

        def rope(dst, src, tok, rot, cs, sn, *after):
            i, b, w = pt.get()
            t0 = mm(b[:, 0:T], con(rot), src, True, True, tok, w, in_tok, inc=True)
            it, t, wt = tmp.get()
            t1 = tt(t[:, 0:T], b[:, 0:T], con(sn), ALU.mult, t0, wt)
            pt.free(i, t1)
            t2 = tt(dst, src, con(cs), ALU.mult, tok, t0, *after)
            t3 = tt(dst, dst, t[:, 0:T], ALU.add, t1, t2)
            tmp.free(it, t3)
            return t3

        ktok = [None] * 4

        def k_finish(m):
            def f(it, kr, a):
                a = rope(kr[:, 0:T], kr[:, 0:T], a, "rot1", "cos1", "sin1")
                yield
                for g in range(2):
                    i, b, w = pt.get()
                    t0 = mm(b, con(f"dup{g}"), kr, True, True, a, w, inc=True)
                    ktok[2 * m + g] = split(K1h[:, 2 * m + g, :], K1l[:, 2 * m + g, :], b, t0, afree)
                    pt.free(i, ktok[2 * m + g])
                tmp.free(it, t0)
            return f

        for m, got in enumerate(lins(2, 8, lambda k: Hx(k)[0], lambda k: Hx(k)[1], 512, lambda k: htoks[k])):
            pipe.run(headed(got, 512, vec("attn_k_g"), k_finish(m)))
        got, t = lin_tok("w", 256, 256, lambda k: Hx(k)[0], lambda k: Hx(k)[1], 4, lambda k: htoks[k])
        vtok = []

        def vdup(dst, src, tok):
            return G(lambda e: e.tensor_copy(dst, f32(src)), tok, afree)

        for s, (i, bk) in enumerate(got):
            b3 = bk.rearrange("p (g d) -> p g d", g=4)
            ab = split(V1h[:, s, :, 0:64], V1l[:, s, :, 0:64], b3, t, afree)
            pm.free(i, ab)
            vtok.append([ab] + [vdup(v[:, s, :, 64:128], v[:, s, :, 0:64], tk) for v, tk in zip((V1h, V1l), ab)])

        pT1 = Ring([[x_[:, 2048 * i:2048 * (i + 1)].rearrange("p (s q) -> p s q", s=4)[:, :, 0:T] for x_ in (Hh, Hl)]
                    for i in range(2)])
        ctxfree = [t]
        smr = Ring([SM[:, 16 + 12 * i:28 + 12 * i] for i in range(8)])
        oat, otok = {}, {}
        qtok = [None] * 8

        def q_finish(j):
            def f(it, qr, a):
                a = rope(qr, qr, a, "rot1", "cos1", "sin1")
                yield
                qtok[j] = split(*Q1(j), qr, a, ctxfree)
                tmp.free(it, qtok[j])
            return f

        SC = HD ** -0.5

        def a1_item(h, qt):
            i, b, w = pm.get()
            o = (h % 2) * 64
            qh, ql = (q_[o:o + 64, qt * 128:(qt + 1) * 128] for q_ in Q1(h // 2))
            kh, kl = K1h[o:o + 64, h // 4, :], K1l[o:o + 64, h // 4, :]
            mm(b, qh, kh, True, False, qtok[h // 2], ktok[h // 4], w)
            mm(b, ql, kh, False, False)
            t0 = mm(b, qh, kl, False, True, inc=True)
            im, sm, wm = smr.get()
            t1 = rmax(sm[:, 0:1], b, t0, wm)
            t2 = ts(sm[:, 1:2], sm[:, 0:1], -SC, None, ALU.mult, None, t1)
            ip, p, wp = tmp.get()
            t3 = act(p, b, ACT.Exp, t2, wp, bias=sm[:, 1:2], scale=SC, accum=sm[:, 2:3])
            pm.free(i, t3)
            yield
            t4 = recip(sm[:, 3:4], sm[:, 2:3], t3)
            t5 = ts(p, p, sm[:, 3:4], None, ALU.mult, None, t4)
            smr.free(im, t5)
            yield
            if qt == 0:
                cur[h] = [pT1.get(), []]
            (it, pT, wT), done_ = cur[h]
            i, b, w = pt.get()
            for s in range(4):
                t0 = tr(b[:, s * 128:(s + 1) * 128], p[:, s * 128:(s + 1) * 128], con("ident"), t5, w, inc=s == 3)
            tmp.free(ip, t0)
            src = b.rearrange("p (s q) -> p s q", s=4)
            hi, lo = (x_[:, :, qt * 128:(qt + 1) * 128] for x_ in pT)
            c1 = act(hi, src, ACT.Copy, t0, wT)
            yield
            done_ += [c1, tt(lo, src, f32(hi), ALU.subtract, t0, c1, wT)]
            pt.free(i, done_)
            yield
            if qt == 1:
                o = (h % 2) * 64
                i, b, w = pm.get()
                for s in range(4):
                    vh, vl = V1h[:, s, h // 4, :], V1l[:, s, h // 4, :]
                    mm(b[:, 0:T], vh, pT[0][:, s, :], s == 0, False, done_, vtok[s], w)
                    mm(b[:, 0:T], vh, pT[1][:, s, :], False, False)
                    t0 = mm(b[:, 0:T], vl, pT[0][:, s, :], False, s == 3, inc=s == 3)
                pT1.free(it, t0)
                j = h // 2
                y = Y[:, j * T:(j + 1) * T]
                oat.setdefault(j, []).append(act(y[o:o + 64, :], b[o:o + 64, 0:T], ACT.Copy, t0, [xt[k] for k in range(8)]))
                pm.free(i, oat[j][-1])
                yield
                if h % 2:
                    hi, lo = Q1(j)
                    a = act(hi, y, ACT.Copy, oat[j], t0)
                    otok[j] = [a, tt(lo, y, f32(hi), ALU.subtract, a, t0, q=V if j == 7 else G)]

        def diff_scalar(l):
            at = (112, 208)[l]
            lv = SM[:, at:at + 4]
            dl = vec("diff_lambda_2", 4 * l, 4)
            t0 = tt(lv[:, 0:1], dl[:, 0:1], dl[:, 1:2], ALU.mult, in_tok)
            t1 = tt(lv[:, 1:2], dl[:, 2:3], dl[:, 3:4], ALU.mult, in_tok)
            yield
            i, b, w = pst.get()
            t2 = mm(b[:, 0:2], con("ones"), lv[:, 0:2], True, True, t0, t1, w, in_tok, inc=True)
            lam = SM[:, at + 4:at + 8]
            t3 = act(lam[:, 0:2], b[:, 0:2], ACT.Exp, t2)
            pst.free(i, t3)
            yield
            t4 = tt(lam[:, 2:3], lam[:, 0:1], lam[:, 1:2], ALU.subtract, t3)
            lam_t = ts(lam[:, 3:4], lam[:, 2:3], LAM_INIT[l], None, ALU.add, None, t4)
            subln = SM[:, at + 8:at + 9]
            sub_t = ts(subln, vec("diff_subln_2", l), 1.0 - LAM_INIT[l], None, ALU.mult, None, in_tok)
            lams[l] = lam, lam_t, subln, sub_t

        cur = {}
        lo_queue["f"] = lambda p: V if p % 3 == 2 else G
        for j in range(8):
            got = lin(8, lambda k: Hx(k, T)[0], lambda k: Hx(k, T)[1], T, lambda k: htoks[k])
            tq = got[2]
            pipe.run(headed(got, T, vec("attn_q_g"), q_finish(j)))
        pT1.rel = [[tq] for _ in range(2)]
        lo_queue["f"] = lambda p: G
        eager["f"] = False
        more = mod_steps(MOD_T)
        pipe.step()
        preload(ACT.Exp)
        for _ in range(3):
            next(more)
            pipe.step()
        lams = {}
        items = [a1_item(h, qt) for h in range(16) for qt in range(2)]
        for n in range(36):
            for m in (n - 1, n - 2, n, n - 2, n - 3, n - 4):
                if 0 <= m < 32:
                    next(items[m], None)
            pipe.step()
            if n in (6, 10):
                pipe.add(diff_scalar(n // 4 - 1))
            next(more, None)
            if n < 32:
                make_pieces(1)
        eager["f"] = True
        for _ in more:
            pass
        lo_queue["f"] = lambda p: V
        pipe.drain()
        otok = [otok[j] for j in range(8)]
        arena_free["t"] = [otok, (P.sem, P.n)]

        stat = Stat(T, adds=True)
        ytoks = []
        for m, (i, bk, t) in enumerate(lin_run(8, 4, 8, lambda k: Q1(k)[0], lambda k: Q1(k)[1], T, lambda k: otok[k])):
            a = act(Y[:, m * 512:m * 512 + T], bk, ACT.Copy, t, otok)
            pm.free(i, a)
            stat.square(Y[:, m * 512:m * 512 + T], a)
            ytoks.append(a)
        hfree["t"] = [t]
        sc = mod_scale(1, 1, 2, 1, 0.0)
        mpipe.drain()
        feed(MOD_G)
        xs_ = residual(1, 1, sc, stat, ytoks, 1)
        ffn_first(1, FFN1, 1, xs_, [])

        GT = [X[:, 1, k, :] for k in range(8)] + [Y[:, 2048 + k * T:2048 + (k + 1) * T] for k in range(8)]
        y2free = [xt[k] for k in range(8)]

        def layer_norm(toks, stat, gname, bname, l, hwait, then):
            s2, ct = center(stat, T, toks, T)
            ir, r, t1 = rstd(s2, "eps5", True)
            preload(then)
            ht, yr = [None] * 8, []

            def tile(k):
                i, t, w = tmp.get()
                g, b = vec(gname, l * 8 + k), vec(bname, l * 8 + k)
                a = stt(t[:, 0:T], Y[:, k * T:(k + 1) * T], g, r, ALU.mult, ALU.mult, t1, w, ct[k])
                yr.append(a)
                c1 = act(xh(k), t[:, 0:T], ACT.Identity, a, hwait, bias=b)
                yield
                c2 = stt(xl(k), t[:, 0:T], b, f32(xh(k)), ALU.add, ALU.subtract, a, c1, hwait)
                ht[k] = [c1, c2]
                c3 = tt(X[:, 0, k, :], t[:, 0:T], b.broadcast_to((128, T)), ALU.add, a, xt[k], q=G)
                xt[k] = [c3]
                tmp.free(i, c1, c2, c3)

            for k in range(8):
                pipe.run(tile(k))
                if k == 0:
                    pipe.step()
                if k > 1:
                    make_pieces(1, G)
            pipe.drain()
            a = yr[-1]
            pt.free(ir, a)
            return ht, [a, s2.tok]

        gate_free = {"t": []}
        dvar = SM[:, 242:250]
        dvar_free = {"t": []}
        yrest = {"t": []}
        for l in range(2):
            af = [arena_free["t"]]
            DQ, DK, DV, NQ, KD, VD, YCh, YCl = arena_open([
                (f"DQ{l}", [128, 4, T], F32), (f"DK{l}", [128, 4, T], F32), (f"DV{l}", [128, 2, 512], F32),
                (f"NQ{l}", [128, 4, T], F32), (f"KD{l}", [128, 2, 2, T], F32), (f"VD{l}", [128, 2, 2, 2, 128], F32),
                (f"YCh{l}", [128, 4, T], F32R), (f"YCl{l}", [128, 4, T], F32R)])

            lam, lam_t, subln, sub_t = lams[l]

            def xlin():
                return lin(8, xh, xl, T, lambda k: xtoks[k])

            def roped(dst, got, *after):
                i, bk, t = got
                it, r_, w = tmp.get()
                a = act(r_[:, 0:T], bk, ACT.Copy, t, w)
                pm.free(i, a)
                yield
                tk = rope(dst, r_[:, 0:T], a, "rot2", "cos2", "sin2", *after)
                tmp.free(it, tk)
                return tk

            dkt, dqt = [], []

            def d_tile(dst, got, toks):
                toks.append((yield from roped(dst, got, af)))

            tiles = lin_run(8, 4, 8, xh, xl, T, lambda k: xtoks[k])
            for m in range(4):
                pipe.run(d_tile(DK[:, m, :], next(tiles), dkt))
                pipe.run(d_tile(DQ[:, m, :], next(tiles), dqt))
            preload(ACT.Exp)
            got, t = lin_tok("w", 512, 512, xh, xl, 2, lambda k: xtoks[k])
            dvt = []
            for s, (i, bk) in enumerate(got):
                a = act(DV[:, s, :], bk, ACT.Copy, t, af)
                pm.free(i, a)
                dvt.append(a)

            kb, kdt, vdt, gat, nqt, hT, cmpt = {}, [], [], [], [], {}, {}
            gate = SM[:, 128:176].rearrange("p (s c) -> p s c", s=2)

            def compress_blocks(kv, src, tok):
                i, kbt, w = tmp.get()
                kbv = kbt[:, 0:480].rearrange("p (l g n) -> p l g n", l=16, g=2)
                tks = []
                for par in range(2):
                    for g in range(2):
                        for half in range(2):
                            sv = src[g * 64:(g + 1) * 64, half * 16:half * 16 + 240].rearrange("p (n l) -> p l n", l=16)
                            sv = sv[:, par:16:2, :]
                            dv = kbv[par * 64:(par + 1) * 64, half * 8:half * 8 + 8, g, :]
                            tks.append(vcopy(dv, sv, tok, w))
                pos = vec("nsa_cmp_pos_2", (l * 2 + kv) * 16, 16).rearrange("p (l o) -> p l o", o=1).broadcast_to((128, 16, 30))
                kb3 = kbt[:, 0:480].rearrange("p (l m) -> p l m", l=16)
                kb[kv] = (i, kb3, tt(kb3, kb3, pos, ALU.add, tks))
                return tks

            def z_kc():
                got = xlin()
                i, t, w = tmp.get()
                tok = yield from roped(t[:, 0:T], got, w)
                tmp.free(i, compress_blocks(0, t[:, 0:T], tok))

            def z_kdup(br):
                got = xlin()
                i, r_, w = tmp.get()
                a = yield from roped(r_[:, 0:T], got, w)
                yield
                for g in range(2):
                    ib, b, wb = pt.get()
                    t0 = mm(b[:, 0:T], con(f"dup{g}"), r_[:, 0:T], True, True, a, wb, inc=True)
                    kdt.append(act(KD[:, br, g, :], b[:, 0:T], ACT.Copy, t0, af))
                    pt.free(ib, kdt[-1])
                tmp.free(i, t0)

            def z_vc():
                i, bk, t = xlin()
                it, v, w = tmp.get()
                tok = act(v[:, 0:T], bk, ACT.Copy, t, w)
                pm.free(i, tok)
                tmp.free(it, compress_blocks(1, v[:, 0:T], tok))
                yield from ()

            def z_values():
                got, t = lin_tok("vvg", 512, 280, xh, xl, 2, lambda k: xtoks[k])
                for s, (i, bk) in enumerate(got):
                    b4 = bk[:, 0:256].rearrange("p (b g d) -> p b g d", b=2, g=2)
                    a = act(VD[:, s, :, :, 0:64], b4, ACT.Copy, t, af)
                    d_ = act(gate[:, s, :], bk[:, 256:280], ACT.Tanh, t, gate_free["t"], scale=0.5)
                    c_ = vcopy(VD[:, s, :, :, 64:128], b4, t, d_, af)
                    pm.free(i, a, c_)
                    vdt.append([a, c_])
                    gat.append(ts(gate[:, s, :], gate[:, s, :], 0.5, 0.5, ALU.mult, ALU.add, d_))
                yield from ()

            def z_nq(m):
                nqt.append((yield from roped(NQ[:, m, :], xlin(), af)))

            def z_hidden(kv):
                ib, b, w = pst.get()
                i, kb3, tk = kb[kv]
                for half in range(2):
                    w1, wt_, p = take_raw(8)
                    for k in range(8):
                        t0 = mm(b[0:30, 0:128], kb3[:, half * 8 + k, :], w1[:, k * 128:(k + 1) * 128], half == 0 and k == 0,
                                half == 1 and k == 7, tk, wt_, w, inc=k == 7)
                    raw_rel[p] = [t0]
                    dma_pieces()
                tmp.free(i, t0)
                ig_, gl, wg = tmp.get()
                a = act(gl[0:30, 0:128], b[0:30, 0:128], ACT.Gelu, t0, wg)
                pst.free(ib, a)
                yield
                ib, b, w = pst.get()
                t1 = tr(b[:, 256:286], gl[0:30, 0:128], con("ident", 0, 30, 0, 30), a, w, inc=True)
                a2 = act(gl[:, 128:158], b[:, 256:286], ACT.Copy, t1)
                pst.free(ib, a2)
                yield
                w2 = vec("nsa_phi_w2_2", (l * 2 + kv) * 128, 128)
                ib, b, w = pst.get()
                if kv == 0:
                    t0 = mm(b[:, 0:30], w2, gl[:, 128:158], True, True, a2, w, inc=True)
                    cmpt["k"] = SM[:, 176:206]
                    cmpt["kt"] = a = act(cmpt["k"], b[:, 0:30], ACT.Copy, t0, af)
                else:
                    for g in range(2):
                        t0 = mm(b[0:15, g * 128:g * 128 + 128], gl[:, 128 + g * 15:128 + (g + 1) * 15], w2, True, True, a2, w,
                                inc=True)
                    cmpt["v"] = [MOD[0:15].rearrange("p a b c -> p (a b c)")[:, 0:128], MA[0:15].rearrange("p a b c d -> p (a b c d)")[:, 0:128]]
                    cmpt["vt"] = [act(cmpt["v"][g], b[0:15, g * 128:g * 128 + 128], ACT.Copy, t0, af) for g in range(2)]
                    a = cmpt["vt"][-1]
                pst.free(ib, a)
                tmp.free(ig_, a)

            YA = lambda j: (Hh[:, 2048 + j * T:2048 + (j + 1) * T], Hl[:, 2048 + j * T:2048 + (j + 1) * T])
            yat = [None] * 12
            ga_t = [None] * 16

            def conv3(src, dst, w, bias, tok, wdst):
                if bias is None:
                    a = ts(dst, src[:, 0:T], w[0], None, ALU.mult, None, tok, wdst)
                else:
                    a = ts(dst, src[:, 0:T], w[0], bias, ALU.mult, ALU.add, tok, wdst)
                for i in (1, 2):
                    a = stt(dst, src[:, i:i + T], w[i], dst, ALU.mult, ALU.add, a)
                return a

            def fill_a(j):
                iv, bv, tv = xlin()
                ic, bc, tc = xlin()
                ix, bx, tx = xlin()
                i, t, w = tmp.get()
                a = act(t[:, 0:T], bv, ACT.Copy, tv, w)
                pm.free(iv, a)
                icb, cb, wc = cbr.get()
                b = tt(cb[:, 2:2 + T], bc, t[:, 0:T], ALU.mult, a, tc, wc, cb_zero)
                pm.free(ic, b)
                yield
                c_ = conv3(cb, t[:, 256:512], [vec("conv_a_w_2", l * 12 + q * 4 + j) for q in range(3)], None, b, w)
                cbr.free(icb, c_)
                d_ = tt(t[:, 0:T], bx, t[:, 256:512], ALU.mult, c_, tx)
                pm.free(ix, d_)
                yat[j] = split(*YA(j), t[:, 0:T], d_, y2read["t"])
                tmp.free(i, yat[j])

            def fill_g(m):
                i, bk, t = xlin()
                ga_t[m] = act(GT[m], bk, ACT.Tanh, t, y2free, scale=0.5)
                pm.free(i, ga_t[m])
                yield from ()

            if l == 0:
                y2read = {"t": [hfree["t"]]}
            early = [(z_kc,), (z_kdup, 0), (z_kdup, 1), (z_vc,), (z_values,), (z_nq, 0), (z_nq, 1), (z_nq, 2), (z_nq, 3),
                     (z_hidden, 0), (z_hidden, 1)]
            late = [(fill_a, j) for j in range(4)] + [(fill_g, m) for m in range(16)]

            def fill(what, n=1):
                for _ in range(n):
                    if what:
                        f, *a = what.pop(0)
                        pipe.run(f(*a))

            def masked(b, n, qt, p, mx, tok, wait):
                mask = con("causal", 128, 256) if qt == 0 else con("causal")
                t1 = V(lambda e: e.tensor_tensor_reduce(p, b, mask, 1.0, 0.0, ALU.add, ALU.max, mx[:, 0:1]), tok, wait, in_tok)
                t2 = ts(mx[:, 1:2], mx[:, 0:1], -SC, None, ALU.mult, None, t1)
                return t1, act(p, p, ACT.Exp, t2, bias=mx[:, 1:2], scale=SC, accum=mx[:, 2:3])

            PC = Y[0:15, 0:2048].rearrange("p (h q) -> p h q", h=8)
            pct = []
            def compressed(qt):
                pair = [pm.get() for _ in range(2)]
                for h in range(8):
                    o = (h % 2) * 64
                    g = h // 4
                    _, b, w = pair[h % 2]
                    t0 = mm(b[:, (h // 2) * 15:(h // 2) * 15 + 15], NQ[o:o + 64, h // 2, qt * 128:(qt + 1) * 128],
                            cmpt["k"][o:o + 64, g * 15:(g + 1) * 15], True, True, nqt, cmpt["kt"], w, inc=h == 7)
                ic, t, wc = tmp.get()
                im, sm, wm = smr.get()
                ir_, rr, wr_ = tmp.get()
                v3 = lambda ap: ap.rearrange("p (h n) -> p h n", h=8)
                s3 = v3(t[:, 0:120])
                bro = lambda ap: ap.rearrange("p (o n) -> p o n", o=1).broadcast_to((128, 8, 15))
                bro4 = lambda ap: ap.rearrange("p (o n) -> p o n", o=1).broadcast_to((128, 4, 15))
                col = lambda ap: ap.rearrange("p (h o) -> p h o", o=1).broadcast_to((128, 8, 15))
                for par, (i, b, _) in enumerate(pair):
                    a = tt(s3[:, par:8:2, :], b[:, 0:60].rearrange("p (h n) -> p h n", h=4),
                           bro4(con("cmpadd", qt * 15, qt * 15 + 15)), ALU.add, t0, wc, in_tok)
                    pm.free(i, a)
                a = V(lambda e, s3=s3, rr=rr: e.tensor_reduce(rr[:, 0:8], s3, AX, ALU.max), a, wr_)
                a = tt(s3, s3, col(rr[:, 0:8]), ALU.subtract, a)
                a = act(t[:, 0:120], t[:, 0:120], ACT.Exp, a, scale=SC)
                a = V(lambda e, s3=s3, rr=rr: e.tensor_reduce(rr[:, 8:16], s3, AX, ALU.add), a)
                a = recip(rr[:, 16:24], rr[:, 8:16], a)
                a = tt(rr[:, 24:32], rr[:, 16:24], gate[:, qt, 0:24:3], ALU.mult, a, gat[qt])
                b2 = tt(s3, s3, bro(con("cmpok", qt * 15, qt * 15 + 15)), ALU.mult, a)
                a = tt(s3, s3, col(rr[:, 24:32]), ALU.mult, a, b2)
                tmp.free(ir_, a)
                smr.free(im)
                yield
                cpt = []
                for hh in range(2):
                    i, b, w = pt.get()
                    for h in range(4):
                        t0 = tr(b[0:15, h * 128:(h + 1) * 128], s3[:, hh * 4 + h, :], con("ident"), a, w, inc=h == 3)
                    c_ = act(PC[:, hh * 4:hh * 4 + 4, qt * 128:(qt + 1) * 128],
                             b[0:15, :].rearrange("p (h q) -> p h q", h=4), ACT.Copy, t0, y2free, yrest["t"])
                    pt.free(i, c_)
                    pct.append(c_)
                tmp.free(ic, t0)

            def d_item(h, qt):
                n = 128 * (qt + 1)
                pair = [pm.get() for _ in range(2)]
                im, sm, wm = smr.get()
                ip, p, wp = tmp.get()
                sc_ = []
                for m, (i, b, w) in enumerate(pair):
                    o = m * 64
                    sc_.append(mm(b[:, 0:n], DQ[o:o + 64, h, qt * 128:(qt + 1) * 128], DK[o:o + 64, h, 0:n],
                                  True, True, dqt[h], dkt[h], w, inc=True))
                d_done.setdefault(h, []).extend(sc_)
                e = []
                for m, (i, b, w) in enumerate(pair):
                    t1, t2 = masked(b[:, 0:n], n, qt, p[:, m * 256:m * 256 + n], sm[:, 4 * m:4 * m + 4], sc_[m], [wp, wm])
                    e.append(t2)
                    pm.free(i, t1)
                yield
                a = recip(sm[:, 8:10], sm[:, 2:7:4], e)
                a2 = tt(sm[:, 10:11], sm[:, 9:10], lam[:, 3:4], ALU.mult, a, lam_t)
                a3 = ts(p[:, 256:256 + n], p[:, 256:256 + n], sm[:, 10:11], None, ALU.mult, None, a2)
                a4 = stt(p[:, 0:n], p[:, 0:n], sm[:, 8:9], p[:, 256:256 + n], ALU.mult, ALU.subtract, a3)
                smr.free(im, a4)
                yield
                yield
                if qt == 0:
                    cur[h] = [tmp.get(), []]
                (ia, aT, wa), at_ = cur[h]
                i, b, w = pt.get()
                for s in range(qt + 1):
                    t0 = tr(b[:, s * 128:(s + 1) * 128], p[:, s * 128:(s + 1) * 128], con("ident"), a4, w, inc=s == qt)
                tmp.free(ip, t0)
                a3 = aT.rearrange("p (s q) -> p s q", s=2)
                at_.append(act(a3[:, 0:qt + 1, qt * 128:(qt + 1) * 128],
                               b[:, 0:128 * (qt + 1)].rearrange("p (s q) -> p s q", q=128), ACT.Copy, t0, wa))
                pt.free(i, at_[-1])
                yield
                if qt == 1:
                    i, b, w = pm.get()
                    mm(b[:, 0:T], DV[:, 0, h * 128:(h + 1) * 128], a3[:, 0, :], True, False, at_, dvt, w)
                    t0 = mm(b[:, 128:T], DV[:, 1, h * 128:(h + 1) * 128], a3[:, 1, 128:T], False, True, inc=True)
                    tmp.free(ia, t0)
                    o_ = DQ[:, h, :]
                    a = act(o_, b[:, 0:T], ACT.Copy, t0, d_done[h])
                    pm.free(i, a)
                    i, t, w = tmp.get()
                    a2 = act(t[:, 0:T], o_, ACT.Square, a, w)
                    yield
                    s_ = Stat(T, "mean128", 1)
                    tmp.free(i, s_.add(t[:, 0:T], a2))
                    a3 = act(dvar[:, 2 * h:2 * h + 2], s_.bank, ACT.Copy, s_.tok, dvar_free["t"])
                    s_.free(a3)
                    d_out.append((h, a, a3))

            d_done, d_out = {}, []

            def d_roots():
                t0 = act(dvar, dvar, ACT.Sqrt, [a3 for _, _, a3 in d_out], in_tok, bias=con("eps5"))
                t1 = recip(dvar, dvar, t0)
                for h, a, _ in d_out:
                    d_root[h] = a, t1

            def d_norm(h):
                a, t0 = d_root[h]
                o_ = DQ[:, h, :]
                ir, r, t1 = spread(None, None, [dvar[:, 2 * h + c:2 * h + c + 1].broadcast_to((128, 128)) for c in range(2)], t0)
                dvar_free["t"].append(t1)
                c_ = stt(o_, o_, subln, r, ALU.mult, ALU.mult, t1, a, sub_t)
                pt.free(ir, c_)
                yat[4 + h] = split(*YA(4 + h), o_, c_, y2read["t"])

            d_root = {}

            yct = [[] for _ in range(4)]

            def n_item(h, qt):
                n = 128 * (qt + 1)
                o = (h % 2) * 64
                g = h // 4
                i, b, w = pm.get()
                im, sm, wm = smr.get()
                ip, p, wp = tmp.get()
                for br in range(2):
                    t0 = mm(b[:, br * 256:br * 256 + n], NQ[o:o + 64, h // 2, qt * 128:(qt + 1) * 128], KD[o:o + 64, br, g, 0:n],
                            True, True, nqt, kdt, w, inc=True)
                e, rd = [], []
                for br in range(2):
                    t1, t2 = masked(b[:, br * 256:br * 256 + n], n, qt, p[:, br * 256:br * 256 + n], sm[:, 4 * br:4 * br + 4], t0, [wp, wm])
                    e.append(t2)
                    rd.append(t1)
                pm.free(i, rd)
                a = recip(sm[:, 8:10], sm[:, 2:7:4], e)
                a = tt(sm[:, 10:12], sm[:, 8:10], gate[:, qt, 3 * h + 1:3 * h + 3], ALU.mult, a, gat[qt])
                for br in range(2):
                    c_ = ts(p[:, br * 256:br * 256 + n], p[:, br * 256:br * 256 + n], sm[:, 10 + br:11 + br], None, ALU.mult, None, a)
                smr.free(im, c_)
                yield
                yield
                if qt == 0:
                    cur[h] = [[tmp.get(), tmp.get()], []]
                nT, nt = cur[h]
                i, b, w = pt.get()
                for br in range(2):
                    for s in range(qt + 1):
                        t0 = tr(b[:, br * 256 + s * 128:br * 256 + (s + 1) * 128], p[:, br * 256 + s * 128:br * 256 + (s + 1) * 128],
                                con("ident"), c_, w, inc=br == 1 and s == qt)
                tmp.free(ip, t0)
                rd = []
                for br in range(2):
                    ia, aT, wa = nT[br]
                    a3 = aT.rearrange("p (s q) -> p s q", s=2)
                    rd.append(act(a3[:, 0:qt + 1, qt * 128:(qt + 1) * 128],
                                  b[:, br * 256:br * 256 + 128 * (qt + 1)].rearrange("p (s q) -> p s q", q=128), ACT.Copy, t0, wa))
                pt.free(i, rd)
                nt += rd
                yield
                if qt == 1:
                    i, b, w = pm.get()
                    mm(b[:, 0:T], cmpt["v"][g], PC[:, h, :], True, False, pct, cmpt["vt"], w)
                    for br in range(2):
                        a3 = nT[br][1].rearrange("p (s q) -> p s q", s=2)
                        mm(b[:, 0:T], VD[:, 0, br, g, :], a3[:, 0, :], False, False, nt, vdt)
                        t0 = mm(b[:, 128:T], VD[:, 1, br, g, :], a3[:, 1, 128:T], False, br == 1, inc=br == 1)
                    for br in range(2):
                        tmp.free(nT[br][0], t0)
                    hi, lo = YCh[o:o + 64, h // 2, :], YCl[o:o + 64, h // 2, :]
                    c1 = act(hi, b[o:o + 64, 0:T], ACT.Copy, t0, af)
                    c2 = tt(lo, b[o:o + 64, 0:T], f32(hi), ALU.subtract, t0, c1, af)
                    pm.free(i, c1, c2)
                    yct[h // 2] += [c1, c2]

            lo_queue["f"] = lambda p: G if p % 3 == 0 else V
            for h in range(4):
                for qt in range(2):
                    pipe.run(d_item(h, qt))
                    fill(early)
            fill(early, 100)
            pipe.drain()
            preload(ACT.Exp)
            for qt in range(2):
                pipe.run(compressed(qt))
                fill(late)
            pipe.drain()
            d_roots()
            preload(ACT.Exp)
            lo_queue["f"] = lambda p: G if p % 3 == 0 else V
            for h in range(8):
                for qt in range(2):
                    pipe.run(n_item(h, qt))
                    if len(late) > 2:
                        fill(late)
                if h in (5, 6):
                    d_norm(h - 5)
            norms = [2, 3]
            while pipe.tasks or late or norms:
                if late:
                    fill(late)
                else:
                    pipe.step()
                if norms:
                    d_norm(norms.pop(0))
            lo_queue["f"] = lambda p: V
            gate_free = {"t": [(V.sem, V.n)]}

            zdone = [(P.sem, P.n)]
            mgt = []
            for m in range(8):
                i2, b2_, t2 = xlin()
                i, t, w = tmp.get()
                g2 = act(t[:, 256:512], b2_, ACT.Tanh, t2, w, scale=0.5)
                pm.free(i2, g2)
                if m == 7:
                    ot = [split(xh(k), xl(k), Y[:, k * T:(k + 1) * T], mgt[k], t2) for k in range(7)]
                acc = None
                im_, mg, wm_ = tmp.get()
                for br in range(3):
                    if br < 2:
                        ib, bb, tb = lin(4, lambda k: YA(4 * br + k)[0], lambda k: YA(4 * br + k)[1], T, lambda k: yat[4 * br + k])
                        gt_, gtk = GT[8 * br + m], ga_t[8 * br + m]
                    else:
                        ib, bb, tb = lin(4, lambda k: YCh[:, k, :], lambda k: YCl[:, k, :], T, lambda k: yct[k])
                        gt_, gtk = t[:, 256:512], g2
                    if br == 0:
                        acc = stt(mg[:, 0:T], gt_, 1.0, bb, ALU.add, ALU.mult, tb, gtk, wm_)
                        pm.free(ib, acc)
                    else:
                        a = stt(t[:, 0:T], gt_, 1.0, bb, ALU.add, ALU.mult, tb, gtk, w, acc)
                        pm.free(ib, a)
                        acc = tt(mg[:, 0:T], mg[:, 0:T], t[:, 0:T], ALU.add, acc, a)
                tmp.free(i, acc)
                mgc = act(Y[:, m * T:(m + 1) * T], mg[:, 0:T], ACT.Copy, acc, zdone, scale=0.5)
                tmp.free(im_, mgc)
                mgt.append(mgc)
            xdone = [t2]
            y2read = {"t": [(P.sem, P.n)]}
            arena_free["t"] = [(P.sem, P.n), (V.sem, V.n)]
            ot.append(split(xh(7), xl(7), Y[:, 7 * T:8 * T], mgt[7], xdone))
            stat = Stat(T, adds=True, parts=0)
            toks = []
            for m, (i, bk, t) in enumerate(lin_run(8, 4, 8, xh, xl, T, lambda k: ot[k])):
                y = Y[:, m * T:(m + 1) * T]
                a = stt(y, X[:, 0, m, :], ALPHA, bk, ALU.mult, ALU.add, t, ot, xt[m])
                pm.free(i, a)
                stat.add(y, a)
                toks.append(a)
            ht, ydone = layer_norm(toks, stat, "ln1_g_2", "ln1_b_2", l, [t], ACT.Gelu)

            HIh, HIl = arena_open([(f"fh{l}", [128, 16, T], F32R), (f"fl{l}", [128, 16, T], F32R)])
            hidfree = list(arena_free["t"])
            lo_queue["f"] = lambda p: G if p % 3 == 2 else V
            j0 = 0
            toks = [None] * 8
            for pi, cnt in enumerate(FFN1):
                gt = [None] * cnt
                tiles = lin_run(2 * cnt, 4, 8, xh, xl, T, lambda k: ht[k])

                def hidden(j, jj):
                    res = []
                    for half in range(2):
                        c_ = jj + 22 * half
                        i, bk, t = next(tiles)
                        icb, cb, wc = cbr.get()
                        a = act(cb[:, 2:2 + T], bk, ACT.Copy, t, wc, cb_zero)
                        pm.free(i, a)
                        it, tb, wt_ = tmp.get()
                        a = conv3(cb, tb[:, 0:T], [vec("ffn_conv_w_2", l * 132 + q * 44 + c_) for q in range(3)],
                                  vec("ffn_conv_b_2", l * 44 + c_), a, wt_)
                        cbr.free(icb, a)
                        res.append((it, tb, a))
                    (ia, ta_, aa), (iu, tu, au) = res
                    yield
                    b = act(ta_[:, 0:T], ta_[:, 0:T], ACT.Gelu, aa)
                    c_ = tt(tu[:, 0:T], ta_[:, 0:T], tu[:, 0:T], ALU.mult, b, au)
                    tmp.free(ia, c_)
                    yield
                    gt[j] = split(HIh[:, j, :], HIl[:, j, :], tu[:, 0:T], c_, hidfree)
                    tmp.free(iu, gt[j])

                for j in range(cnt):
                    pipe.run(hidden(j, j0 + j))
                pipe.drain()
                if pi == 1:
                    stat = Stat(T, adds=True, parts=0)
                for m, (i, bk, t) in enumerate(lin_run(8, 4, cnt, lambda k: HIh[:, k, :], lambda k: HIl[:, k, :], T,
                                                       lambda k: gt[k])):
                    y = Y[:, m * T:(m + 1) * T]
                    if pi == 0:
                        toks[m] = stt(y, X[:, 0, m, :], ALPHA, bk, ALU.mult, ALU.add, t, ydone, xt[m])
                    else:
                        toks[m] = tt(y, bk, y, ALU.add, t, toks[m])
                        stat.add(y, toks[m])
                    pm.free(i, toks[m])
                hidfree = [t]
                j0 += cnt
            lo_queue["f"] = lambda p: V
            arena_free["t"] = [t]
            xtoks, yd = layer_norm(toks, stat, "ln2_g_2", "ln2_b_2", l, [t], ACT.Exp)
            yrest = {"t": yd}
            y2free = [yd]

        assert st["blk"] == len(plan)
        for k in range(8):
            S.items.append((flat(xt[k]), lambda e, k=k: e.dma_start(
                out[k * 128:(k + 1) * 128, :], X[:, 0, k, :]).then_inc(s_out, 16), False))
        for cm in reversed(arena):
            cm.__exit__(None, None, None)

        block = ctx.enter_context(nc.Block())

        @block.sync
        def _(eng):
            S.play(eng)
            eng.wait_ge(s_out, 16 * 8)

        @block.scalar
        def _(eng):
            A.play(eng)

        @block.vector
        def _(eng):
            V.play(eng)

        @block.gpsimd
        def _(eng):
            G.play(eng)

        @block.tensor
        def _(eng):
            P.play(eng)


def const_array():
    off, n = const_plan()
    c = np.zeros((128, n), np.float32)

    def put(name, a):
        c[:, off[name]:off[name] + a.shape[1]] = a

    i = np.arange(128)
    put("ident", np.eye(128))
    put("ones", np.ones((128, 128)))
    put("mean", np.full((128, 128), 1.0 / 1024))
    put("mean128", np.full((128, 128), 1.0 / 128))
    put("mean64", (i[:, None] // 64 == i[None, :] // 64) / 64.0)
    r1 = np.zeros((128, 128))
    for j in range(0, 128, 2):
        r1[j + 1, j] = -1
        r1[j, j + 1] = 1
    put("rot1", r1)
    r2 = np.zeros((128, 128))
    for b in (0, 64):
        for j in range(8):
            r2[b + 8 + j, b + j] = -1
            r2[b + j, b + 8 + j] = 1
    put("rot2", r2)
    for g in range(2):
        put(f"dup{g}", (i[:, None] == g * 64 + i[None, :] % 64).astype(np.float32))
    f = np.float32
    t = np.arange(T)
    freq = (f(10000.0) ** (-np.arange(16, dtype=f) / f(16))).astype(f)
    ang = np.concatenate([(t // 64).astype(f)[:, None] * freq, (t % 64).astype(f)[:, None] * freq], 1)
    put("cos1", np.cos(ang).T[(i % 64) // 2])
    put("sin1", np.sin(ang).T[(i % 64) // 2])
    inv = (f(500000.0) ** (-np.arange(0, 16, 2, dtype=f) / f(16))).astype(f)
    ang = t.astype(f)[:, None] * inv
    d = i % 64
    put("cos2", np.where(d[:, None] < 16, np.cos(ang).T[d % 8], 1.0))
    put("sin2", np.where(d[:, None] < 16, np.sin(ang).T[d % 8], 0.0))
    put("causal", np.concatenate([np.zeros((128, 128)), np.where(i[None, :] <= i[:, None], 0.0, -1e30)], 1))
    ok = np.concatenate([(np.arange(15) * 16 + 31)[None, :] <= (q * 128 + i)[:, None] for q in range(2)], 1)
    put("cmpok", ok.astype(np.float32))
    put("cmpadd", np.where(ok, 0.0, -1e30))
    put("eps6", np.full((128, 1), 1e-6))
    put("eps5", np.full((128, 1), 1e-5))
    return c


def vec_array(a):
    off, n = vec_plan()
    v = np.zeros((128, n), np.float32)

    def put(name, m):
        v[:m.shape[0], off[name]:off[name] + m.shape[1]] = m

    def cols(x):
        return np.asarray(x).reshape(-1, 128).T

    for name in ("c", "c_ctx", "b_mod", "norm_g", "conv_b_pw1", "conv_w_dw", "conv_b_dw", "conv_ln_g", "conv_ln_b",
                 "conv_b_pw2", "conv_a_w_2", "diff_subln_2", "ln1_g_2", "ln1_b_2", "ln2_g_2", "ln2_b_2",
                 "ffn_conv_w_2", "ffn_conv_b_2"):
        put(name, cols(a[name]))
    for name in ("attn_q_g", "attn_k_g"):
        g = np.asarray(a[name]).reshape(64, 1)
        put(name, np.concatenate([g, g], 0))
    put("diff_lambda_2", np.asarray(a["diff_lambda_2"]).reshape(8, 64).T)
    put("nsa_cmp_pos_2", cols(a["nsa_cmp_pos_2"]))
    w2 = np.asarray(a["nsa_phi_w2_2"]).reshape(4, 128, 64).transpose(1, 0, 2)
    put("nsa_phi_w2_2", np.concatenate([w2, w2], 2).reshape(128, 512))
    return v


def stream_array(a):
    plan, total = stream_plan()
    w = np.zeros((total // PIECE, 128, PIECE), np.float32)
    for at, (kind, name, idx, r0, c0, n, width) in plan:
        dst = w[at // PIECE, :, at % PIECE:at % PIECE + n]
        src = np.asarray(a[name])[idx]
        rows = src[r0:r0 + 128]
        if kind == "vvg":
            dst[:, 0:128] = rows[:, 3584 + 3 * 128:3584 + 4 * 128]
            dst[:, 128:256] = rows[:, 3584 + 5 * 128:3584 + 6 * 128]
            dst[:, 256:280] = rows[:, 4352:4376]
        else:
            dst[:] = rows[:, c0:c0 + n]
    return w


def kernel(**inputs):
    import concourse.bacc as bacc
    from concourse.bass_utils import run_bass_kernel_spmd

    a = {k: np.asarray(v) for k, v in inputs.items()}

    def feat(x):
        return np.ascontiguousarray(x[0].T.reshape(8, 128, T).transpose(1, 0, 2))

    arrays = {
        "wstream": stream_array(a),
        "vecs": vec_array(a),
        "consts": const_array(),
        "xin": np.stack([feat(a["x"]), feat(a["ctx"])]),
    }
    nc = bacc.Bacc("TRN2", target_bir_lowering=False, num_devices=1)
    aps = [nc.dram_tensor(n, v.shape, F32, kind="ExternalInput").ap() for n, v in arrays.items()]
    out = nc.dram_tensor("out", (D, T), F32, kind="ExternalOutput").ap()
    build(nc, *aps, out)
    r = run_bass_kernel_spmd(nc, [arrays], core_ids=[0])
    got = np.asarray(r.results[0]["out"])
    return np.ascontiguousarray(got.T)[None]
```
